# Optimizing a Trainium2 kernel written in Bass

```python
import jax, jax.numpy as jnp
from jax import lax
import numpy as np

D_MODEL = 1024
BATCH = 1
SEQ = 1024
DEPTH = 1

GRID_W = 64
HEAD_DIM = 64
RW_HEADS = 4
RW_WIDTH = RW_HEADS * HEAD_DIM
RW_DECAY_RANK = 32
RW_ICLR_RANK = 32
RW_GATE_RANK = 64
RW_GN_EPS = 64e-5
NA_HEADS = 4
NA_WIDTH = NA_HEADS * HEAD_DIM
NA_WIN_ROWS = 8
NA_WIN_COLS = 16
MLA_HEADS = 8
MLA_Q_RANK = 256
MLA_KV_RANK = 128
MLA_NOPE_DIM = 64
MLA_ROPE_DIM = 32
MLA_V_DIM = 64
MLA_WIDTH = MLA_HEADS * MLA_V_DIM
ROPE_THETA = 10000.0
Q_BLOCK = 128

MIX_WIDTH = RW_WIDTH + NA_WIDTH + MLA_WIDTH
RW_IN = 3 * RW_WIDTH + 2 * RW_DECAY_RANK + 2 * RW_ICLR_RANK + RW_GATE_RANK
NA_IN = 3 * NA_WIDTH
MLA_IN = MLA_Q_RANK + MLA_KV_RANK + MLA_ROPE_DIM
IN_WIDTH = RW_IN + NA_IN + MLA_IN
D_FF = -(-8 * D_MODEL // (3 * 256)) * 256
DN_ALPHA = (2 * DEPTH) ** 0.25
DN_BETA = (8 * DEPTH) ** -0.25
LN_EPS = 1e-5
RMS_EPS = 1e-6
NEG_INF = -1e30

kernel_name = "hybrid_rwkv7_natten2d_mla_encoder"

def layer_norm(x, g, b):
    xf = x.astype(jnp.float32)
    mu = xf.mean(-1, keepdims=True)
    var = jnp.square(xf - mu).mean(-1, keepdims=True)
    return ((xf - mu) * lax.rsqrt(var + LN_EPS) * g + b).astype(x.dtype)

def rms_norm(x, g):
    xf = x.astype(jnp.float32)
    return (xf * lax.rsqrt(jnp.square(xf).mean(-1, keepdims=True) + RMS_EPS) * g).astype(x.dtype)

def rope_tables(T):
    inv_freq = jnp.power(ROPE_THETA, -jnp.arange(0, MLA_ROPE_DIM, 2, dtype=jnp.float32) / MLA_ROPE_DIM)
    ang = jnp.arange(T, dtype=jnp.float32)[:, None] * inv_freq[None, :]
    return jnp.cos(ang), jnp.sin(ang)

def apply_rope(x, cos, sin):
    x1, x2 = jnp.split(x, 2, axis=-1)
    return jnp.concatenate([x1 * cos - x2 * sin, x2 * cos + x1 * sin], -1).astype(x.dtype)

def centred_token_shift(p, mu):
    zero = jnp.zeros_like(p[:, :1])
    prev = jnp.concatenate([zero, p[:, :-1]], 1)
    nxt = jnp.concatenate([p[:, 1:], zero], 1)
    return p + mu[0] * (prev - p) + mu[1] * (nxt - p)

def wkv7_scan(r, decay, k, v, a, b, inclusive):
    B, T, H, N = r.shape
    xs = tuple(jnp.moveaxis(t.astype(jnp.float32), 1, 0) for t in (r, decay, k, v, a, b))

    def step(S, inp):
        r_t, w_t, k_t, v_t, a_t, b_t = inp
        sa = jnp.einsum('bhvk,bhk->bhv', S, a_t)
        S_new = S * w_t[:, :, None, :] + sa[..., None] * b_t[:, :, None, :] + v_t[..., None] * k_t[:, :, None, :]
        y = jnp.einsum('bhvk,bhk->bhv', S_new if inclusive else S, r_t)
        return S_new, y

    S0 = jnp.zeros((B, H, N, N), jnp.float32)
    _, ys = lax.scan(step, S0, xs)
    return jnp.moveaxis(ys, 0, 1)

def rwkv7_mixer(p, mu, w0, w2, a0, a2, g2, k_k, k_a, r_k, gn_g, gn_b):
    B, T, _ = p.shape
    f32 = jnp.float32
    p = centred_token_shift(p, mu)
    W, Rd, Ra = RW_WIDTH, RW_DECAY_RANK, RW_ICLR_RANK
    r, k, v, wd, ad, gd = jnp.split(p, [W, 2 * W, 3 * W, 3 * W + 2 * Rd, 3 * W + 2 * Rd + 2 * Ra], -1)
    wd = wd.reshape(B, T, 2, Rd)
    ad = ad.reshape(B, T, 2, Ra)
    log_w = -jax.nn.softplus(-(w0 + jnp.einsum('btdr,drc->btdc', jnp.tanh(wd), w2))) - 0.5
    decay = jnp.exp(-jnp.exp(log_w.astype(f32)))
    iclr = jax.nn.sigmoid(a0 + jnp.einsum('btdr,drc->btdc', ad, a2))
    gate = jax.nn.sigmoid(gd) @ g2

    def heads(t):
        return t.reshape(*t.shape[:-1], RW_HEADS, HEAD_DIM)

    kk = heads(k * k_k).astype(f32)
    kk = kk / jnp.maximum(jnp.sqrt(jnp.sum(kk * kk, -1, keepdims=True)), 1e-12)
    k_dir = heads(k[:, :, None, :] * (1.0 + (iclr - 1.0) * k_a))
    a_h = heads(iclr).astype(f32)
    dec_h = heads(decay)
    rh, vh = heads(r), heads(v)

    y_fwd = wkv7_scan(rh, dec_h[:, :, 0], k_dir[:, :, 0], vh, -kk, kk * a_h[:, :, 0], True)

    def flip(t):
        return jnp.flip(t, 1)

    y_bwd = flip(wkv7_scan(flip(rh), flip(dec_h[:, :, 1]), flip(k_dir[:, :, 1]), flip(vh),
                           flip(-kk), flip(kk * a_h[:, :, 1]), False))
    y = y_fwd + y_bwd
    mu_y = y.mean(-1, keepdims=True)
    var_y = jnp.square(y - mu_y).mean(-1, keepdims=True)
    yn = ((y - mu_y) * lax.rsqrt(var_y + RW_GN_EPS)).reshape(B, T, W) * gn_g + gn_b
    bonus = jnp.sum(rh.astype(f32) * k_dir[:, :, 0].astype(f32) * r_k, -1, keepdims=True) * vh.astype(f32)
    out = (yn + bonus.reshape(B, T, W)) * gate
    return out.astype(p.dtype)

def neighbourhood_attention(p, rpb):
    B, T, _ = p.shape
    rows = T // GRID_W
    kr = min(NA_WIN_ROWS, rows)
    kc = NA_WIN_COLS
    q, k, v = jnp.split(p, 3, -1)
    grid = lambda t: t.reshape(B, rows, GRID_W, NA_HEADS, HEAD_DIM)
    q, k, v = grid(q), grid(k), grid(v)
    i = jnp.arange(rows)
    row_start = jnp.clip(i - kr // 2, 0, rows - kr)
    key_rows = row_start[:, None] + jnp.arange(kr)[None, :]
    j = jnp.arange(GRID_W)
    col_start = jnp.clip(j - kc // 2, 0, GRID_W - kc)
    col_mask = (j[None, :] >= col_start[:, None]) & (j[None, :] < col_start[:, None] + kc)
    kg = jnp.take(k, key_rows, axis=1)
    vg = jnp.take(v, key_rows, axis=1)
    s = jnp.einsum('biqhd,birkhd->bhiqrk', q, kg).astype(jnp.float32) * (HEAD_DIM ** -0.5)
    dr = key_rows - i[:, None] + (NA_WIN_ROWS - 1)
    dc = jnp.clip(j[None, :] - j[:, None] + (kc - 1), 0, 2 * kc - 2)
    bias = rpb[:, dr[:, None, :, None], dc[None, :, None, :]]
    s = jnp.where(col_mask[:, None, :], s + bias[None].astype(jnp.float32), NEG_INF)
    prob = jax.nn.softmax(s, axis=(-2, -1))
    o = jnp.einsum('bhiqrk,birkhd->biqhd', prob.astype(v.dtype), vg)
    return o.reshape(B, T, NA_WIDTH)

def mla_attention(p, q_norm_g, w_q_b, kv_norm_g, w_kv_b, cos, sin):
    B, T, _ = p.shape
    c_q, c_kv, k_pe = jnp.split(p, [MLA_Q_RANK, MLA_Q_RANK + MLA_KV_RANK], -1)
    q = (rms_norm(c_q, q_norm_g) @ w_q_b).reshape(B, T, MLA_HEADS, MLA_NOPE_DIM + MLA_ROPE_DIM)
    kv = (rms_norm(c_kv, kv_norm_g) @ w_kv_b).reshape(B, T, MLA_HEADS, MLA_NOPE_DIM + MLA_V_DIM)
    q_nope, q_pe = jnp.split(q, [MLA_NOPE_DIM], -1)
    k_nope, v = jnp.split(kv, [MLA_NOPE_DIM], -1)
    q_pe = apply_rope(q_pe, cos[:, None, :], sin[:, None, :])
    k_pe = apply_rope(k_pe, cos, sin)
    q = jnp.concatenate([q_nope, q_pe], -1)
    k = jnp.concatenate([k_nope, jnp.broadcast_to(k_pe[:, :, None, :], (B, T, MLA_HEADS, MLA_ROPE_DIM))], -1)
    scale = (MLA_NOPE_DIM + MLA_ROPE_DIM) ** -0.5
    nb = T // Q_BLOCK
    qb = jnp.moveaxis(q.reshape(B, nb, Q_BLOCK, MLA_HEADS, -1), 1, 0)

    def attend(q_blk):
        s = jnp.einsum('bqhd,bkhd->bhqk', q_blk, k).astype(jnp.float32) * scale
        prob = jax.nn.softmax(s, axis=-1)
        return jnp.einsum('bhqk,bkhd->bqhd', prob.astype(v.dtype), v)

    o = lax.map(attend, qb)
    return jnp.moveaxis(o, 0, 1).reshape(B, T, MLA_WIDTH)

def setup_inputs(seed: int = 0) -> dict:
    key = jax.random.key(seed)
    ks = list(jax.random.split(key, 40))
    f32 = jnp.float32
    L = DEPTH

    def nrm(idx, shape, scale):
        return jax.random.normal(ks[idx], shape, f32) * scale

    return {
        "x": nrm(0, (BATCH, SEQ, D_MODEL), 1.0),
        "ln_in_g": 1.0 + nrm(1, (D_MODEL,), 0.05),
        "ln_in_b": nrm(2, (D_MODEL,), 0.02),
        "w_in": nrm(3, (L, D_MODEL, IN_WIDTH), D_MODEL ** -0.5),
        "rw_mu": jax.random.uniform(ks[4], (L, 2, RW_IN), f32, 0.0, 0.5),
        "rw_w0": jax.random.uniform(ks[5], (L, 2, RW_WIDTH), f32, -6.0, -1.0),
        "rw_w2": nrm(6, (L, 2, RW_DECAY_RANK, RW_WIDTH), 0.1),
        "rw_a0": nrm(7, (L, 2, RW_WIDTH), 0.1),
        "rw_a2": nrm(8, (L, 2, RW_ICLR_RANK, RW_WIDTH), 0.1),
        "rw_g2": nrm(9, (L, RW_GATE_RANK, RW_WIDTH), RW_GATE_RANK ** -0.5),
        "rw_k_k": 0.85 + nrm(10, (L, RW_WIDTH), 0.05),
        "rw_k_a": 1.0 + nrm(11, (L, RW_WIDTH), 0.05),
        "rw_r_k": nrm(12, (L, RW_HEADS, HEAD_DIM), 0.1),
        "rw_gn_g": 1.0 + nrm(13, (L, RW_WIDTH), 0.05),
        "rw_gn_b": nrm(14, (L, RW_WIDTH), 0.02),
        "na_rpb": nrm(15, (L, NA_HEADS, 2 * NA_WIN_ROWS - 1, 2 * NA_WIN_COLS - 1), 0.1),
        "mla_q_norm_g": 1.0 + nrm(16, (L, MLA_Q_RANK), 0.05),
        "mla_w_q_b": nrm(17, (L, MLA_Q_RANK, MLA_HEADS * (MLA_NOPE_DIM + MLA_ROPE_DIM)), MLA_Q_RANK ** -0.5),
        "mla_kv_norm_g": 1.0 + nrm(18, (L, MLA_KV_RANK), 0.05),
        "mla_w_kv_b": nrm(19, (L, MLA_KV_RANK, MLA_HEADS * (MLA_NOPE_DIM + MLA_V_DIM)), MLA_KV_RANK ** -0.5),
        "w_out": nrm(20, (L, MIX_WIDTH, D_MODEL), DN_BETA * MIX_WIDTH ** -0.5),
        "ln1_g": 1.0 + nrm(21, (L, D_MODEL), 0.05),
        "ln1_b": nrm(22, (L, D_MODEL), 0.02),
        "w_ffn_gate": nrm(23, (L, D_MODEL, D_FF), D_MODEL ** -0.5),
        "w_ffn_up": nrm(24, (L, D_MODEL, D_FF), D_MODEL ** -0.5),
        "w_ffn_down": nrm(25, (L, D_FF, D_MODEL), DN_BETA * D_FF ** -0.5),
        "ln2_g": 1.0 + nrm(26, (L, D_MODEL), 0.05),
        "ln2_b": nrm(27, (L, D_MODEL), 0.02),
    }

def reference(x, ln_in_g, ln_in_b, w_in, rw_mu, rw_w0, rw_w2, rw_a0, rw_a2, rw_g2, rw_k_k, rw_k_a,
              rw_r_k, rw_gn_g, rw_gn_b, na_rpb, mla_q_norm_g, mla_w_q_b, mla_kv_norm_g, mla_w_kv_b,
              w_out, ln1_g, ln1_b, w_ffn_gate, w_ffn_up, w_ffn_down, ln2_g, ln2_b):
    B, T, _ = x.shape
    cos, sin = rope_tables(T)
    h = layer_norm(x, ln_in_g, ln_in_b)
    for l in range(DEPTH):
        p = h @ w_in[l]
        p_rw, p_na, p_mla = jnp.split(p, [RW_IN, RW_IN + NA_IN], -1)
        o_rw = rwkv7_mixer(p_rw, rw_mu[l], rw_w0[l], rw_w2[l], rw_a0[l], rw_a2[l], rw_g2[l],
                           rw_k_k[l], rw_k_a[l], rw_r_k[l], rw_gn_g[l], rw_gn_b[l])
        o_na = neighbourhood_attention(p_na, na_rpb[l])
        o_mla = mla_attention(p_mla, mla_q_norm_g[l], mla_w_q_b[l], mla_kv_norm_g[l], mla_w_kv_b[l], cos, sin)
        mix = jnp.concatenate([o_rw.astype(h.dtype), o_na.astype(h.dtype), o_mla.astype(h.dtype)], -1) @ w_out[l]
        h = layer_norm(DN_ALPHA * h + mix, ln1_g[l], ln1_b[l])
        ff = (jax.nn.silu(h @ w_ffn_gate[l]) * (h @ w_ffn_up[l])) @ w_ffn_down[l]
        h = layer_norm(DN_ALPHA * h + ff, ln2_g[l], ln2_b[l])
    return h


_drawn_inputs = setup_inputs


def setup_inputs(seed=0):
    import zlib

    import numpy as np

    out = dict(_drawn_inputs(seed))
    spreads = {}
    factors = {'rw_w2': 8.0,
     'rw_a0': 8.0,
     'rw_k_k': 45.276,
     'rw_k_a': 7.073,
     'rw_r_k': 3.642,
     'rw_gn_g': 21.827,
     'rw_gn_b': 64.0,
     'na_rpb': 43.491,
     'mla_q_norm_g': 8.0,
     'mla_kv_norm_g': 8.0,
     'ln1_b': 2.715,
     'ln2_b': 3.12}
    for name, (base, spread) in spreads.items():
        noise = np.random.default_rng([zlib.crc32(name.encode()), seed]).standard_normal(out[name].shape)
        drawn = base * np.exp(spread * noise) if base else spread * noise
        out[name] = __import__('jax').numpy.asarray(drawn.astype(out[name].dtype))
    for name, factor in factors.items():
        out[name] = (out[name] * factor).astype(out[name].dtype)
    return out
```

```python
from contextlib import ExitStack

import concourse.bass as bass
from concourse import mybir

F32 = mybir.dt.float32
F32R = mybir.dt.float32r
ALU = mybir.AluOpType
ACT = mybir.ActivationFunctionType
AX = mybir.AxisListType
ds = bass.ds

P = 128
T = 1024
D = 1024
NT = T // P
KT = D // P
HALF = 512
NH = T // HALF
D_FF = 2816
FT = D_FF // P
LN_EPS, RMS_EPS, GN_EPS = 1e-5, 1e-6, 64e-5
ALPHA = 2 ** 0.25
DECAY_SCALE = 0.6065306597126334

M_R, M_K, M_V, M_LORA, M_GATE, M_NQ, M_NK, M_CQ, M_CKV = 0, 2, 4, 6, 7, 8, 10, 12, 14
NM = 15
NSHIFT = 8
PW = T + 2

LEVELS = 7
C_ID, C_HEADS, C_ONES, C_REC_F, C_REC_B, C_BEFORE_F, C_BEFORE_B, C_LV = 0, 1, 2, 3, 4, 5, 6, 7
C_LVT = C_LV + LEVELS
C_COLS = C_LVT + LEVELS
NC = C_COLS + 1

PARAMS = {}


def _params():
    at = 0
    for name, n in (("ln_in_g", 8), ("ln_in_b", 8), ("mu0", 8), ("mu1", 8), ("w0", 4), ("a0", 4),
                    ("k_k", 2), ("k_a", 2), ("r_k", 2), ("gn_g", 2), ("gn_b", 2), ("qn_g", 2),
                    ("kvn_g", 1), ("ln1_g", 8), ("ln1_b", 8)):
        PARAMS[name] = (at, n)
        at += n
    return at


NPAR = _params()
EPILOGUE = (3, 6, 9, 12)
NDR, NDC = 15, 31


def chunk_jobs():
    jobs = []
    for d in range(2):
        jobs += [(f"A{d}", "act"), (f"N{d}", "dve"), (f"KA{d}", "dve"), (f"R{d}", "dve"), (f"KR{d}", "dve")]
        jobs += [(f"tok{d}{hp}", "act") for hp in range(2)] + [(f"V{d}", "act")]
    jobs += [(f"AV{d}", "act") for d in range(2)]
    for m in range(1, LEVELS):
        jobs += [(f"G{d}.{m}", "act") for d in range(2)]
        if m == LEVELS - 1:
            jobs += [(f"AZ{d}", "dve") for d in range(2)]
        for d in range(2):
            jobs += [(f"W{d}.{m}", "dve")] + [(f"T{d}.{m}", "dve")] * (m < LEVELS - 1)
    jobs += [(f"U{d}", "act") for d in range(2)]
    jobs += [(f"Y{d}", "dve") for d in range(2)]
    jobs += [(f"S{d}", "dve") for d in range(2)]
    return jobs


JOBS = chunk_jobs()
NJ = len(JOBS)
JOB = {name: j for j, (name, _) in enumerate(JOBS)}
NBANK = 8
NTH = {name: sum(e == eng for _, e in JOBS[:j + 1]) for j, (name, eng) in enumerate(JOBS)}
EACH = {e: sum(x == e for _, x in JOBS) for e in ("act", "dve")}
LAST_IN_BANK = {b: max(j for j in range(NJ) if j % NBANK == b) for b in range(NBANK)}


class Chain:

    def __init__(self, eng, sem):
        self.eng, self.sem, self.base, self.n = eng, sem, 0, 0

    def add(self, ins):
        ins.then_inc(self.sem, 1)
        self.n += 1

    def wait(self):
        self.eng.wait_ge(self.sem, self.base + self.n)

    def enter(self, i, each):
        self.start, self.each = self.base + self.n, each
        self.base, self.n = self.start + i * each, 0

    def leave(self, times):
        assert self.n == self.each, (self.n, self.each)
        self.base, self.n = self.start + times * self.each, 0


def hybrid_encoder(nc, a, out):
    with ExitStack() as ctx:
        def sb(name, cols, dt=F32):
            return ctx.enter_context(nc.sbuf_tensor(name, [P, cols], dt))

        def sem(name):
            return ctx.enter_context(nc.semaphore(name))

        resid_dram = nc.dram_tensor("resid_spill", (P, NT * D), F32, kind="Internal").ap()

        consts = sb("consts", NC * P)
        par = sb("par", NPAR)
        stats = sb("stats", 256)
        arena_at = (nc.sbuf_base + 31) // 32 * 32
        guard_at = (3 * 8192 + NM * PW + 2048 + 5120 + 7) // 8 * 8
        arena = sb("arena", guard_at + 2 * T)
        X0, MIX0, PR0 = 0, 8192, 16384
        HT0 = PR0 + NM * PW
        VN0 = HT0 + 8192
        WK0 = VN0 + 2048

        def reg(at, cols):
            return arena[:, at:at + cols]

        def rounded(name, at, cols):
            return nc.alloc_sbuf_tensor_at(name, [P, cols], F32R, offset=arena_at + 4 * at)[:, :]

        q_round = rounded("q_round", guard_at, T)
        k_round = rounded("k_round", guard_at + T, T)

        def cst(c, n=1):
            return consts[:, c * P:(c + n) * P]

        def pcol(name, i=0, rows=slice(0, P)):
            at, n = PARAMS[name]
            assert i < n
            return par[rows, at + i:at + i + 1]

        ident = cst(C_ID)
        resid = reg(X0, 8192).rearrange("p (t c) -> p t c", t=NT)
        mix = reg(MIX0, 8192).rearrange("p (m t) -> p m t", m=8)
        hT = reg(HT0, 8192).rearrange("p (k t) -> p k t", k=KT)
        proj = reg(PR0, NM * PW).rearrange("p (m t) -> p m t", m=NM)
        v_na = reg(VN0, 2048).rearrange("p (t c) -> p t c", t=NT)

        NSLOT = 3
        w_ring = [reg(WK0 + s * 1024, 1024).rearrange("p (k c) -> p k c", k=KT) for s in range(NSLOT)]
        g_row, b_row = reg(WK0 + 3072, 1024), reg(WK0 + 4096, 1024)
        wv_sb = reg(MIX0, 2048).rearrange("p (k c) -> p k c", k=KT)

        v_sh = reg(HT0, 1792).rearrange("p (t c) -> p t c", t=NT - 1)
        na_bias = reg(HT0 + 1792, 2 * NDR * 64).rearrange("p (h r c) -> p h r c", h=2, r=NDR)
        na_at = HT0 + 1792 + 2 * NDR * 64
        q_diag = reg(na_at, 2 * P).rearrange("p (b c) -> p b c", b=2)
        na_s = reg(na_at + 256, 2 * HALF).rearrange("p (b c) -> p b c", b=2)
        na_e = reg(na_at + 1280, 2 * HALF).rearrange("p (b c) -> p b c", b=2)
        na_et = reg(na_at + 2304, 2 * HALF).rearrange("p (b c) -> p b c", b=2)
        na_o = reg(na_at + 3328, 2 * 64).rearrange("p (b c) -> p b c", b=2)
        na_max, na_sum, na_inv = stats[:, 128:130], stats[:, 130:132], stats[:, 132:134]
        NU = 32

        def window(row):
            first = min(max(row - 4, 0), 8)
            return first, first - row + 7

        rope_sb = reg(HT0, T)
        qT = [reg(HT0 + 2048 + 1024 * b, T) for b in range(2)]
        kT = [reg(HT0 + 4096 + 1024 * b, T) for b in range(2)]
        vh = [reg(HT0 + 6144 + 1024 * b, 1024).rearrange("p (t c) -> p t c", t=NT) for b in range(2)]
        NE = 3
        e_ring = [reg(WK0 + 1024 * j, T) for j in range(NE)]
        w_q = [reg(WK0 + 3072 + 256 * b, 256).rearrange("p (k c) -> p k c", k=2) for b in range(2)]
        w_kv = [reg(WK0 + 3584 + P * b, P) for b in range(2)]
        rope_tmp = reg(WK0 + 3840, T)
        max_row = reg(HT0 + 1024, 2 * P).rearrange("p (b c) -> p b c", b=2)
        inv_sum = reg(VN0, T)
        g_max = stats[:, 136:152].rearrange("p (b c) -> p b c", b=2)
        HEADS = 8
        MLA_SCALE = 96 ** -0.5

        def tok(m):
            return proj[:, m, 1:1 + T]

        def halves(ap):
            return ap.rearrange("p (h c) -> p h c", h=NH)

        sh = reg(X0, 8192).rearrange("p (m t) -> p m t", m=NSHIFT)
        r_sh, k_sh, v_sh2, lora_sh, gate_sh = sh[:, 0:2], sh[:, 2:4], sh[:, 4:6], sh[:, 6], sh[:, 7]
        prod = reg(PR0, 16384).rearrange("p (s q t) -> p s q t", s=4, q=4)
        Rt, Kt, Bt, At = (prod[:, j] for j in range(4))
        gate_o = reg(PR0 + 16384, 2048).rearrange("p (h t) -> p h t", h=2)
        bonus = reg(PR0 + 18432, 2048).rearrange("p (h t) -> p h t", h=2)
        ST0 = PR0 + 20480
        kk = reg(MIX0, 2048).rearrange("p (h t) -> p h t", h=2)
        keep_sum = reg(ST0 + 2048, T)
        cum = reg(ST0 + 3072, T)
        y1 = [reg(ST0 + 4096 + 1024 * b, T) for b in range(2)]
        y0 = [reg(ST0 + 6144 + 1024 * b, T) for b in range(2)]
        ex = [reg(ST0 + 8192 + 1024 * b, T) for b in range(2)]
        lora_w = reg(MIX0 + 6144, 1024).rearrange("p (j c) -> p j c", j=8)
        key_norm = [reg(MIX0 + 4096 + 1024 * b, T) for b in range(2)]
        gate_w = reg(ST0 + 8192, 256).rearrange("p (j c) -> p j c", j=2)
        y_out = mix[:, 0:2]
        gfac = stats[:, 152:184].rearrange("p (q c) -> p q c", q=4)
        sfac = stats[:, 184:216].rearrange("p (q c) -> p q c", q=4)
        one_less_ka = stats[:, 216:218]

        at = [ST0, ST0 + 10240]
        free = [(X0, 4096), (X0 + 6144, 2048)]

        def small(cols):
            if at[0] + cols <= at[1]:
                at[0] += cols
                return reg(at[0] - cols, cols)
            at[0], n = free.pop(0)
            at[1] = at[0] + n
            return small(cols)

        Bm, Km, As, Vs, tokm, tokv, Xs, Zs, Us = [], [], [], [], [], [], [], [], []
        for q in range(4):
            Bm.append(small(256).rearrange("p (e t) -> p e t", e=2))
            Km.append(small(256).rearrange("p (e t) -> p e t", e=2))
            As.append(small(P))
            Vs.append(small(P))
            tokm.append(small(2 * P).rearrange("p (s c) -> p s c", s=2))
        for d in range(2):
            tokv.append(small(256).rearrange("p (h c) -> p h c", h=2))
            Xs.append(small(256).rearrange("p (h c) -> p h c", h=2))
            Us.append(small(256).rearrange("p (h c) -> p h c", h=2))
            Zs.append(small(256).rearrange("p (h c) -> p h c", h=2))
        Araw, Alev, Tm, Wm, Gm, KAm, Rm, KRm, AVs = [], [], [], [], [], [], [], [], []
        for d in range(2):
            four = [small(4 * P).rearrange("p (h t) -> p h t", h=4) for _ in range(9)]
            for lst, x in zip((Araw, Tm, Wm, Gm, KAm, Rm, KRm), four):
                lst.append(x)
            Alev.append(four[7:9])
            AVs.append(small(256).rearrange("p (h c) -> p h c", h=2))

        def chunk(tile, d, i):
            return tile[:, :, ds(i * P if d == 0 else i * (-P) + (NT - 1) * P, P)]

        def four_heads(m):
            return m.unsqueeze(1).to_broadcast([P, 4, P])

        def tiles(n, m):
            return n * 1024, m * 1024

        w_out = [reg(1024 * j, 1024) for j in (16, 17, 18, 19, 44, 45, 46, 47)]
        ln1_rows = [reg(1024 * j, 1024) for j in (20, 21)]
        raw_w = [reg(1024 * j, 1024) for j in (22, 23)]
        h1_hi = [rounded(f"h1_hi{k}", *tiles(24 + k, 1)) for k in range(KT)]
        h1_lo = [rounded(f"h1_lo{k}", *tiles(32 + k, 1)) for k in range(KT)]
        h1_tmp = [reg(1024 * 42 + HALF * j, HALF) for j in range(4)]
        w_hi = [[rounded(f"w_hi{b}{n}", *tiles(40 + 4 * b + 2 * n, 1)) for n in range(2)] for b in range(2)]
        w_lo = [[rounded(f"w_lo{b}{n}", *tiles(41 + 4 * b + 2 * n, 1)) for n in range(2)] for b in range(2)]
        EARLY = 14

        def act_tile(f):
            return reg(1024 * (f + 8 if f < EARLY else f - EARLY), 1024)

        wd_hi = [rounded(f"wd_hi{b}", *tiles(40 + 4 * b, 1)) for b in range(2)]
        wd_lo = [rounded(f"wd_lo{b}", *tiles(41 + 4 * b, 1)) for b in range(2)]
        act_hi = [rounded(f"act_hi{b}", 1024 * (42 + 4 * b), HALF) for b in range(2)]
        act_lo = [rounded(f"act_lo{b}", 1024 * (42 + 4 * b) + HALF, HALF) for b in range(2)]
        resid2 = reg(1024 * 24, 8192).rearrange("p (t c) -> p t c", t=NT)
        ln2_rows = [reg(1024 * j, 1024) for j in (32, 33)]

        psum = ctx.enter_context(nc.psum_tensor("psum", [P, 8, HALF], F32))

        def bank(b, cols=HALF, rows=slice(0, P)):
            return psum[rows, b, 0:cols]

        bn = stats[:, 0:NT * 12].rearrange("p (t s) -> p t s", t=NT)
        mv = stats[:, 96:96 + 2 * NT].rearrange("p (t s) -> p t s", t=NT)
        sd = stats[:, 112:120]
        rs = stats[:, 120:128]

        const_in, par_in, rows_in = sem("const_in"), sem("par_in"), sem("rows_in")
        x_in = [sem(f"x_in{t}") for t in range(NT)]
        dve, act_own, pool_own = sem("dve_own"), sem("act_own"), sem("pool_own")
        var_ready, sd_ready, norm_ready = sem("var_ready"), sem("sd_ready"), sem("norm_ready")
        ln_tr, ln_evac_a, ln_evac_v = sem("ln_tr"), sem("ln_evac_a"), sem("ln_evac_v")
        resid_ready, spilled = sem("resid_ready"), sem("spilled")
        w_in_ready = [sem(f"w_in_ready{s}") for s in range(NSLOT)]
        proj_done, evac_a, evac_v = sem("proj_done"), sem("evac_a"), sem("evac_v")
        wv_in, vproj_done, v_evac, pads, shifted = (sem("wv_in"), sem("vproj_done"), sem("v_evac"), sem("pads"),
                                                    sem("shifted"))
        bias_in, bias_ready, qd_zero, q_diag_ready = sem("bias_in"), sem("bias_ready"), sem("qd_zero"), sem("q_diag_ready")
        na_s_done, na_s_biased, na_max_ready, na_e_ready = (sem("na_s_done"), sem("na_s_biased"),
                                                            sem("na_max_ready"), sem("na_e_ready"))
        na_tr, na_et_ready, na_pv, na_o_ready, na_ot, na_mixed = (sem("na_tr"), sem("na_et_ready"), sem("na_pv"),
                                                                  sem("na_o_ready"), sem("na_ot"), sem("na_mixed"))
        rope_in, sq_ready, ms_done, ms_ready, ms_sd, lat_ready = (sem("rope_in"), sem("sq_ready"), sem("ms_done"),
                                                                  sem("ms_ready"), sem("ms_sd"), sem("lat_ready"))
        kpe_ready, v_ones, kpe_round = sem("kpe_ready"), sem("v_ones"), sem("kpe_round")
        w_head = [sem(f"w_head{b}") for b in range(2)]
        pr_q, pr_k, pr_v = sem("pr_q"), sem("pr_k"), sem("pr_v")
        q_nope, q_rope, q_rounded, k_nope, k_rounded, v_ready = (sem("q_nope"), sem("q_rope"), sem("q_rounded"),
                                                                 sem("k_nope"), sem("k_rounded"), sem("v_ready"))
        s_done, e_ready, g_done, g_max_ready, pv_done, o_inv, o_ready = (
            sem("s_done"), sem("e_ready"), sem("g_done"), sem("g_max_ready"), sem("pv_done"), sem("o_inv"),
            sem("o_ready"))
        mt_done, mt_copied, max_in = sem("mt_done"), sem("mt_copied"), [sem("max_in0"), sem("max_in1")]
        lora_in, gate_w_in, shift_done, lora_act, nrm_sq, nrm_done, nrm_sd, kk_ready, z_done, z_sig = (
            sem("lora_in"), sem("gate_w_in"), sem("shift_done"), sem("lora_act"), sem("nrm_sq"), sem("nrm_done"), sem("nrm_sd"),
            sem("kk_ready"), sem("z_done"), sem("z_sig"))
        y10_ready, ex_ready, prods_ready, rk_ready, bonus_done, bonus_ready, gate_done, gate_ready = (
            sem("y10_ready"), sem("ex_ready"), sem("prods_ready"), sem("rk_ready"), sem("bonus_done"),
            sem("bonus_ready"), sem("gate_done"), sem("gate_ready"))
        keep_ready, kb_ready, staged, cleared = sem("keep_ready"), sem("kb_ready"), sem("staged"), sem("cleared")
        job_done, out_a, out_v, lev_ready, t0_ready, z_ready = (sem("job_done"), sem("out_a"), sem("out_v"),
                                                                sem("lev_ready"), sem("t0_ready"), sem("z_ready"))
        OUT = {"act": out_a, "dve": out_v}

        def taken(eng, i, name, before=False):
            who = JOBS[JOB[name]][1]
            eng.wait_ge(OUT[who], i * EACH[who] + NTH[name] + (0 if before else EACH[who]))

        def computed(eng, i, name, before=False):
            eng.wait_ge(job_done, i * NJ + JOB[name] + 1 + (0 if before else NJ))

        gn_mean, gn_centred, gn_sq, gn_var, gn_ms, gn_sd, o_rw = (
            sem("gn_mean"), sem("gn_centred"), sem("gn_sq"), sem("gn_var"), sem("gn_ms"), sem("gn_sd"), sem("o_rw"))
        w_out_in, resid_in, rows1_in, rows2_in = sem("w_out_in"), sem("resid_in"), sem("rows1_in"), sem("rows2_in")
        mixed, sum1, var1, sd1, norm1, tr1, h1_hi_ready, h1_tmp_ready, h1_lo_ready, resid1, spilled1 = (
            sem("mixed"), sem("sum1"), sem("var1"), sem("sd1"), sem("norm1"), sem("tr1"), sem("h1_hi_ready"),
            [sem("h1_tmp_a"), sem("h1_tmp_v")], sem("h1_lo_ready"), sem("resid1"), sem("spilled1"))
        raw_in = [sem("gate_in"), sem("up_in")]
        w_hi_ready = [sem("gate_hi_ready"), sem("up_hi_ready")]
        w_lo_ready = [sem("gate_lo_ready"), sem("up_lo_ready")]
        wd_in = [sem(f"wd_in{b}") for b in range(2)]
        ff_done, silu_ready, ff_ready = sem("ff_done"), sem("silu_ready"), sem("ff_ready")
        wd_hi_ready, wd_lo_ready, act_hi_ready, act_lo_ready, resid2_in = (
            sem("wd_hi_ready"), sem("wd_lo_ready"), sem("act_hi_ready"), sem("act_lo_ready"), sem("resid2_in"))
        down_k, down_done, sum2, var2, sd2, y_ready = (sem("down_k"), sem("down_done"), sem("sum2"), sem("var2"),
                                                       sem("sd2"), sem("y_ready"))
        out_sem = sem("out_written")

        block = ctx.enter_context(nc.Block())

        @block.sync
        def _(sp):
            for t in range(NT):
                sp.dma_start(resid[:, t, :], a["x"][t]).then_inc(x_in[t], 16)
                if t == 3:
                    sp.dma_start(consts[:, :], a["consts"]).then_inc(const_in, 16)
            with sp.Fori(0, NM // NSLOT) as i:
                for s in range(NSLOT):
                    sp.wait_ge(proj_done, i * NSLOT + (s + 1))
                    sp.dma_start(w_ring[s], a["w_in"][i * NSLOT + s]).then_inc(w_in_ready[s], 16)
            sp.dma_start(wv_sb, a["w_nv"]).then_inc(wv_in, 16)
            sp.dma_start(lora_w, a["lora"][:, 0:8, :]).then_inc(lora_in, 16)
            sp.wait_ge(vproj_done, 4)
            sp.dma_start(na_bias, a["rpb"]).then_inc(bias_in, 16)
            for b in range(2):
                sp.dma_start(w_q[b], a["w_q"][b]).then_inc(w_head[b], 16)
                sp.dma_start(w_kv[b], a["w_kv"][b]).then_inc(w_head[b], 16)

            sp.wait_ge(na_pv, NU)
            sp.dma_start(rope_sb, a["rope"]).then_inc(rope_in, 16)

            def head_loads(i, b, weights):
                sp.wait_ge(mt_copied, 2 * i + (b + 1))
                sp.dma_start(qT[b][96:97, :], max_row[0:NT, b, :]).then_inc(max_in[b], 16)
                if weights:
                    sp.wait_ge(pr_v, 2 * i + (b + 1))
                    sp.dma_start(w_q[b], a["w_q"][2 * i + (b + 2)]).then_inc(w_head[b], 16)
                    sp.dma_start(w_kv[b], a["w_kv"][2 * i + (b + 2)]).then_inc(w_head[b], 16)

            with sp.Fori(0, HEADS // 2 - 1) as i:
                for b in range(2):
                    head_loads(i, b, True)
            for b in range(2):
                head_loads(HEADS // 2 - 1, b, False)
            sp.wait_ge(o_ready, HEADS + 1)
            sp.dma_start(gate_w, a["lora"][:, 8:10, :]).then_inc(gate_w_in, 16)
            sp.wait_ge(out_v, (NT + 1) * EACH["dve"])
            for k in range(8):
                sp.dma_start(w_out[k], a["w_out"][k]).then_inc(w_out_in, 16)
            sp.dma_start(reg(X0, 8192), resid_dram).then_inc(resid_in, 16)
            for n, w in enumerate(("w_gate", "w_up")):
                sp.dma_start(raw_w[n], a[w][0]).then_inc(raw_in[n], 16)
            for b in range(2):
                sp.dma_start(ln1_rows[b], a["rows"][2 + b:3 + b, :].partition_broadcast(P)).then_inc(rows1_in, 16)

            def gate_up_load(j, c):
                for n, w in enumerate(("w_gate", "w_up")):
                    sp.wait_ge(w_lo_ready[n], 2 * j + c)
                    sp.dma_start(raw_w[n], a[w][2 * j + c]).then_inc(raw_in[n], 16)

            gate_up_load(0, 1)
            gate_up_load(0, 2)
            sp.wait_ge(resid1, NT)
            sp.dma_start(resid_dram, reg(X0, 8192)).then_inc(spilled1, 16)
            with sp.Fori(0, (FT - 4) // 2) as j:
                for b in range(2):
                    gate_up_load(j, 3 + b)
            gate_up_load(0, FT - 1)

            for b in range(2):
                sp.wait_ge(w_lo_ready[b], FT)
                sp.dma_start(raw_w[b], a["w_down"][b]).then_inc(wd_in[b], 16)
            with sp.Fori(0, FT // 2 - 1) as j:
                for b in range(2):
                    sp.wait_ge(wd_lo_ready, 2 * j + (b + 1))
                    sp.dma_start(raw_w[b], a["w_down"][2 * j + (2 + b)]).then_inc(wd_in[b], 16)
            sp.wait_ge(ff_done, FT)
            sp.dma_start(reg(1024 * 24, 8192), resid_dram).then_inc(resid2_in, 16)
            for b in range(2):
                sp.dma_start(ln2_rows[b], a["rows"][4 + b:5 + b, :].partition_broadcast(P)).then_inc(rows2_in, 16)
            with sp.Fori(0, FT // 2) as j:
                for b in range(2):
                    sp.wait_ge(wd_lo_ready, 2 * j + (FT - 1 + b))
                    sp.dma_start(raw_w[b], a["w_down"][2 * j + b]).then_inc(wd_in[b], 16)
            for t in range(NT):
                sp.wait_ge(y_ready, t + 1)
                sp.dma_start(out[t], resid2[:, t, :]).then_inc(out_sem, 16)
            sp.wait_ge(out_sem, 16 * NT)

        @block.gpsimd
        def _(pool):
            own = Chain(pool, pool_own)
            pool.dma_start(par[:, :], a["params"]).then_inc(par_in, 16)
            pool.dma_start(g_row, a["rows"][0:1, :].partition_broadcast(P)).then_inc(rows_in, 16)
            pool.dma_start(b_row, a["rows"][1:2, :].partition_broadcast(P)).then_inc(rows_in, 16)
            pool.memset(proj[:, 0:NSHIFT, 0:1], 0.0).then_inc(pads, 1)
            pool.memset(proj[:, 0:NSHIFT, T + 1:T + 2], 0.0).then_inc(pads, 1)
            pool.wait_ge(rows_in, 32)
            for t in range(NT):
                pool.wait_ge(ln_tr, 8 * (t // 4 + 1))
                own.add(pool.tensor_tensor(resid[:, t, :], resid[:, t, :], g_row, ALU.mult))
                own.wait()
                pool.tensor_tensor(resid[:, t, :], resid[:, t, :], b_row, ALU.add).then_inc(resid_ready, 1)
            pool.wait_ge(resid_ready, NT)
            pool.dma_start(resid_dram, reg(X0, 8192)).then_inc(spilled, 16)
            pool.wait_ge(vproj_done, 4)
            pool.memset(q_diag[:, :, :], 0.0).then_inc(qd_zero, 1)
            pool.wait_ge(qd_zero, 1)
            pool.wait_ge(evac_a, NM + NSLOT)
            pool.wait_ge(evac_v, NM + NSLOT)
            for n in range(NU):
                row, hp = n // 2, n % 2
                if n >= 2:
                    pool.wait_ge(na_s_done, n - 1)
                for e in range(2):
                    rows = slice(64 * e, 64 * e + 64)
                    pool.tensor_copy(q_diag[rows, n % 2, 64 * e:64 * e + 64],
                                     proj[rows, M_NQ + hp, 1 + 64 * row:1 + 64 * row + 64]).then_inc(q_diag_ready, 1)
            pool.wait_ge(q_diag_ready, 2 * NU)
            pool.wait_ge(na_ot, NU)
            for b in range(2):
                pool.memset(vh[b][:, :, 64:128], 1.0).then_inc(v_ones, 1)
                pool.wait_ge(v_ones, 2 * b + 1)
                pool.memset(kT[b][96:97, :], 1.0).then_inc(v_ones, 1)
                pool.wait_ge(v_ones, 2 * b + 2)
            pool.wait_ge(z_sig, 8)
            pool.wait_ge(kk_ready, 8)
            for q in range(4):
                hp = q % 2
                own.add(pool.tensor_tensor(Bt[:, q], Kt[:, q], kk[:, hp], ALU.mult))
                own.wait()
                own.add(pool.tensor_scalar(Bt[:, q], Bt[:, q], -1.0, None, ALU.mult))
                own.add(pool.tensor_scalar(Kt[:, q], Kt[:, q], pcol("k_a", hp), one_less_ka[:, hp:hp + 1],
                                           ALU.mult, ALU.add))
                own.wait()
                pool.tensor_tensor(Kt[:, q], Kt[:, q], k_sh[:, hp], ALU.mult).then_inc(kb_ready, 1)
            pool.wait_ge(o_ready, HEADS + 1)
            pool.memset(keep_sum, 1.0).then_inc(keep_ready, 1)
            pool.wait_ge(keep_ready, 1)
            pool.memset(keep_sum.rearrange("p (c t) -> p c t", t=P)[:, :, 0:1], 0.0).then_inc(keep_ready, 1)
            pool.wait_ge(keep_ready, 2)
            pool.wait_ge(prods_ready, 16)
            pool.wait_ge(bonus_ready, 2)
            pool.wait_ge(gate_ready, 2)
            n = 0
            for ap in [x for q in range(4) for x in (Bm[q], Km[q])] + Zs + [y_out]:
                if n:
                    pool.wait_ge(cleared, n)
                pool.memset(ap, 0.0).then_inc(cleared, 1)
                n += 1
            pool.wait_ge(cleared, n)

            with pool.Fori(0, NT) as i:
                own.enter(i, 2)
                computed(pool, i, "V1", before=True)
                n = 0

                def stage(dst, src):
                    nonlocal n
                    pool.tensor_copy(dst, src).then_inc(staged, 1)
                    n += 1
                    pool.wait_ge(staged, i * 24 + n)

                for q in range(4):
                    d, hp = q // 2, q % 2
                    for e in range(2):
                        rows = slice(64 * e, 64 * e + 64)
                        stage(Bm[q][rows, e:e + 1, :], chunk(Bt[:, q:q + 1], d, i)[rows])
                        stage(Km[q][rows, e:e + 1, :], chunk(Kt[:, q:q + 1], d, i)[rows])
                    stage(Vs[q].unsqueeze(1), chunk(v_sh2[:, hp:hp + 1], d, i))
                computed(pool, i, "AZ1", before=True)
                for q in range(4):
                    stage(As[q].unsqueeze(1), chunk(At[:, q:q + 1], q // 2, i))
                for d in range(2):
                    taken(pool, i, f"A{d}")
                    own.add(pool.tensor_tensor(Tm[d], Araw[d], four_heads(cst(C_LV if d == 0 else C_LVT)), ALU.mult))
                    own.wait()
                    pool.tensor_tensor(Tm[d], Tm[d], four_heads(ident), ALU.add).then_inc(t0_ready, 1)
                for m in range(1, LEVELS):
                    for d in range(2):
                        if m >= 3:
                            computed(pool, i, f"G{d}.{m - 2}")
                        pool.tensor_tensor(Alev[d][m % 2], Araw[d], four_heads(cst((C_LV if d == 0 else C_LVT) + m)),
                                           ALU.mult).then_inc(lev_ready, 1)
                own.leave(NT)
            pool.wait_ge(rows1_in, 32)
            for t in range(NT):
                pool.wait_ge(tr1, 8 * (t // 4 + 1))
                own.add(pool.tensor_tensor(resid[:, t, :], resid[:, t, :], ln1_rows[0], ALU.mult))
                own.wait()
                pool.tensor_tensor(resid[:, t, :], resid[:, t, :], ln1_rows[1], ALU.add).then_inc(resid1, 1)

        @block.scalar
        def _(act):
            own = Chain(act, act_own)
            for hf in range(2):
                act.wait_ge(var_ready, hf + 1)
                act.activation(sd[:, 4 * hf:4 * hf + 4], mv[:, 4 * hf:4 * hf + 4, 1], ACT.Sqrt).then_inc(sd_ready, 1)
            act.wait_ge(par_in, 16)
            for hf in range(2):
                for k in range(0, KT, 2):
                    act.wait_ge(ln_tr, 8 * hf + k + 1)
                    act.activation(hT[:, k, hf * HALF:(hf + 1) * HALF], bank(k), ACT.Identity,
                                   bias=pcol("ln_in_b", k), scale=pcol("ln_in_g", k)).then_inc(ln_evac_a, 1)
            act.sem_inc(evac_a, NSLOT)
            with act.Fori(0, NM // NSLOT) as i:
                for s in range(NSLOT):
                    act.wait_ge(proj_done, i * NSLOT + (s + 1 + NSLOT))
                    act.activation(proj[:, ds(i * NSLOT + s, 1), 1:1 + HALF], bank(2 * s).unsqueeze(1),
                                   ACT.Copy).then_inc(evac_a, 1)
            for j in range(0, 4, 2):
                act.wait_ge(vproj_done, j + 1)
                act.activation(v_na[:, 2 * j:2 * j + 2, :], bank(j).rearrange("p (t c) -> p t c", t=2),
                               ACT.Copy).then_inc(v_evac, 1)
            act.wait_ge(shift_done, 2)
            act.activation(lora_sh[0:64], lora_sh[0:64], ACT.Tanh).then_inc(lora_act, 1)
            act.activation(gate_sh[0:64], gate_sh[0:64], ACT.Sigmoid).then_inc(lora_act, 1)
            act.wait_ge(shift_done, NSHIFT)
            for hp in range(2):
                act.activation(key_norm[hp], k_sh[:, hp], ACT.Square, scale=pcol("k_k", hp)).then_inc(nrm_sq, 1)
            act.wait_ge(evac_v, NM + NSLOT)
            for j, m in enumerate((M_CQ, M_CQ + 1, M_CKV)):
                act.activation(e_ring[j], tok(m), ACT.Square).then_inc(sq_ready, 1)
            for hp in range(2):
                act.wait_ge(nrm_done, hp + 1)
                act.activation(halves(key_norm[hp]), psum[:, 2 * hp:2 * hp + 2, :], ACT.Sqrt).then_inc(nrm_sd, 1)
            for j in range(8):
                act.wait_ge(z_done, j + 1)
                b = 2 * (j % 2) + 4
                act.activation(halves((Rt if j < 4 else Kt)[:, j % 4]), psum[:, b:b + 2, :], ACT.Sigmoid,
                               bias=pcol("w0" if j < 4 else "a0", j % 4)).then_inc(z_sig, 1)
            for j in range(2):
                act.wait_ge(ms_ready, j + 1)
                act.activation(e_ring[j], e_ring[j], ACT.Sqrt).then_inc(ms_sd, 1)
            for n in range(NU + 3):
                if n < NU:
                    b = n % 2
                    act.wait_ge(na_max_ready, n + 1)
                    if n >= 2:
                        act.wait_ge(na_tr, n - 1)
                        act.wait_ge(na_o_ready, 2 * (n - 1))
                    act.activation(na_e[:, b], na_s[:, b], ACT.Exp, bias=na_max[:, b:b + 1],
                                   accum_out=na_sum[:, b:b + 1]).then_inc(na_e_ready, 1)
                if 1 <= n <= NU:
                    b = (n - 1) % 2
                    act.wait_ge(na_tr, n)
                    if n >= 3:
                        act.wait_ge(na_pv, n - 2)
                    act.activation(na_et[:, b], bank(2 + b), ACT.Copy).then_inc(na_et_ready, 1)
                if n >= 3:
                    row, hp, b = (n - 3) // 2, (n - 3) % 2, (n - 3) % 2
                    act.wait_ge(na_ot, n - 2)
                    for e in range(2):
                        act.activation(mix[64 * e:64 * e + 64, 2 + hp, 64 * row:64 * row + 64],
                                       psum[0:64, 6 + b, 64 * e:64 * e + 64], ACT.Copy).then_inc(na_mixed, 1)
            act.wait_ge(kpe_ready, 4)
            act.activation(k_round[64:96, :], kT[0][64:96, :], ACT.Copy).then_inc(kpe_round, 1)

            def head_copies(i, b):
                act.wait_ge(pr_q, 2 * i + (b + 1))
                act.activation(halves(qT[b][0:64, :]), psum[0:64, 0:2, :], ACT.Copy).then_inc(q_nope, 1)
                act.wait_ge(pr_k, 2 * i + (b + 1))
                act.activation(halves(kT[b][0:64, :]), psum[0:64, 2:4, :], ACT.Copy).then_inc(k_nope, 1)
                act.activation(halves(k_round[0:64, :]), psum[0:64, 2:4, :], ACT.Copy).then_inc(k_rounded, 1)
                act.wait_ge(pr_v, 2 * i + (b + 1))
                act.activation(vh[b][:, :, 0:64], psum[:, 4:6, :].rearrange("p h (t c) -> p (h t) c", c=P)[:, :, 64:128],
                               ACT.Copy).then_inc(v_ready, 1)
                act.wait_ge(q_rope, 2 * i + (b + 1))
                act.wait_ge(q_nope, 2 * i + (b + 1))
                act.activation(q_round[0:96, :], qT[b][0:96, :], ACT.Copy).then_inc(q_rounded, 1)

            def copy_max(i, b):
                act.wait_ge(mt_done, 2 * i + (b + 1))
                act.activation(max_row[0:NT, b, :], psum[0:NT, 4, 0:P], ACT.Copy).then_inc(mt_copied, 1)

            def head_exps(i, b, ahead, ahead2):
                for kt in range(NT):
                    act.wait_ge(s_done, 16 * i + (8 * b + kt + 1))
                    if kt >= NE:
                        act.wait_ge(pv_done, 16 * i + (8 * b + kt - NE + 1))
                    act.activation(halves(e_ring[(kt) % NE]), psum[:, 2 * (kt % 2):2 * (kt % 2) + 2, :], ACT.Exp,
                                   scale=MLA_SCALE).then_inc(e_ready, 1)
                if ahead:
                    copy_max(i + (b + 1) // 2, (b + 1) % 2)
                if ahead2:
                    head_copies(i + 1, b)

            head_copies(0, 0)
            copy_max(0, 0)
            head_copies(0, 1)
            with act.Fori(0, HEADS // 2 - 1) as i:
                for b in range(2):
                    head_exps(i, b, True, True)
            for b in range(2):
                head_exps(HEADS // 2 - 1, b, b == 0, False)
            for hp in range(2):
                act.wait_ge(gate_done, hp + 1)
                act.activation(halves(gate_o[:, hp]), psum[:, 4 + 2 * hp:6 + 2 * hp, :], ACT.Copy).then_inc(gate_ready, 1)
            for q in range(4):
                b = q % 2
                act.wait_ge(y10_ready, 2 * q + 2)
                if q >= 2:
                    act.wait_ge(prods_ready, 4 * (q - 1))
                act.activation(gfac[:, q], y1[b].rearrange("p (c t) -> p c t", t=P)[:, :, P - 1], ACT.Exp,
                               scale=-DECAY_SCALE).then_inc(ex_ready, 1)
                if q < 2:
                    act.activation(At[:, q], y0[b], ACT.Exp, scale=-DECAY_SCALE).then_inc(ex_ready, 1)
                    act.activation(Rt[:, q], y1[b], ACT.Exp, scale=-DECAY_SCALE).then_inc(ex_ready, 1)
                    act.activation(ex[b], y1[b], ACT.Exp, scale=DECAY_SCALE).then_inc(ex_ready, 1)
                else:
                    act.activation(At[:, q], y1[b], ACT.Exp, scale=DECAY_SCALE).then_inc(ex_ready, 1)
                    act.activation(ex[b], y0[b], ACT.Exp, scale=-DECAY_SCALE).then_inc(ex_ready, 1)
            act.sem_inc(out_a, EACH["act"])
            with act.Fori(0, NT) as i:
                for name, who in JOBS:
                    if who != "act":
                        continue
                    bk = JOB[name] % NBANK
                    computed(act, i, name)
                    kind = name.rstrip("0123456789.")
                    if kind == "A":
                        d = int(name[1])
                        computed(act, i, f"G{d}.{LEVELS - 1}", before=True)
                        ins = act.activation(Araw[d].rearrange("p h t -> p (h t)"), bank(bk), ACT.Copy)
                    elif kind == "tok":
                        q = 2 * int(name[3]) + int(name[4])
                        for e in range(2):
                            ins = act.activation(tokm[q][:, :, 64 * e:64 * e + 64],
                                                 bank(bk).rearrange("p (s x) -> p s x", s=2)[:, :, 192 * e:192 * e + 64],
                                                 ACT.Copy)
                    elif kind == "V":
                        ins = act.activation(tokv[int(name[1])].rearrange("p h c -> p (h c)"), bank(bk, 256), ACT.Copy)
                    elif kind == "G":
                        d = int(name[1])
                        ins = act.activation(Gm[d].rearrange("p h t -> p (h t)"), bank(bk), ACT.Copy)
                    else:
                        d = int(name[-1])
                        dst = AVs[d] if kind == "AV" else Us[d]
                        if kind == "AV":
                            taken(act, i, f"AZ{d}", before=True)
                        for e in range(2):
                            ins = act.activation(dst[:, :, 64 * e:64 * e + 64],
                                                 bank(bk).rearrange("p (h x) -> p h x", h=2)[:, :, 192 * e:192 * e + 64],
                                                 ACT.Copy)
                    ins.then_inc(out_a, 1)
            for hp in range(2):
                act.wait_ge(gn_centred, hp + 1)
                act.activation(Bt[:, hp], At[:, hp], ACT.Square).then_inc(gn_sq, 1)
            for hp in range(2):
                act.wait_ge(gn_ms, hp + 1)
                act.activation(Bt[:, hp], Bt[:, hp], ACT.Sqrt).then_inc(gn_sd, 1)
            def weights_hi(n, b, j, c):
                act.wait_ge(raw_in[n], 32 * j + 16 * (c + 1))
                act.activation(w_hi[b][n], raw_w[n], ACT.Copy).then_inc(w_hi_ready[n], 1)

            for hf in range(2):
                act.wait_ge(var1, hf + 1)
                act.activation(sd[:, 4 * hf:4 * hf + 4], mv[:, 4 * hf:4 * hf + 4, 1], ACT.Sqrt).then_inc(sd1, 1)
                if hf == 0:
                    weights_hi(0, 0, 0, 0)
                for k in range(KT):
                    hi = h1_hi[k][:, hf * HALF:(hf + 1) * HALF]
                    if k % 2 == 0:
                        act.wait_ge(tr1, 8 * hf + k + 1)
                        if 8 * hf + k >= 4:
                            act.wait_ge(h1_lo_ready, 8 * hf + k - 3)
                        act.activation(h1_tmp[k % 4], bank(4 + k % 4), ACT.Identity,
                                       bias=pcol("ln1_b", k), scale=pcol("ln1_g", k)).then_inc(h1_tmp_ready[0], 1)
                        act.wait_ge(h1_tmp_ready[0], 4 * hf + k // 2 + 1)
                    else:
                        act.wait_ge(h1_tmp_ready[1], 4 * hf + k // 2 + 1)
                    act.activation(hi, h1_tmp[k % 4], ACT.Copy).then_inc(h1_hi_ready, 1)
            act.wait_ge(h1_lo_ready, 2 * KT)
            weights_hi(1, 0, 0, 0)
            act.wait_ge(mixed, NT)
            for n in range(2):
                weights_hi(n, 1, 0, 1)

            def silu(dst, b, j, c):
                act.wait_ge(ff_done, 2 * j + (c + 1))
                act.activation(halves(dst), psum[:, 4 * b:4 * b + 2, :], ACT.Silu).then_inc(silu_ready, 1)

            for first, at0, times in ((0, 8192, EARLY // 2), (EARLY, 0, (FT - EARLY) // 2 - 1)):
                if first:
                    act.wait_ge(spilled1, 16)
                with act.Fori(0, times) as j:
                    for b in range(2):
                        silu(arena[:, ds(j * 2048 + (at0 + 1024 * b), 1024)], b, j, first + b)
                        for n in range(2):
                            weights_hi(n, b, j, first + b + 2)

            def down_hi(quad, b, j, k, src):
                act.wait_ge(wd_in[b], 16 * j + 16 * (quad * (FT // 2) + k // 2 + 1))
                act.activation(wd_hi[b], raw_w[b], ACT.Copy).then_inc(wd_hi_ready, 1)
                act.activation(act_hi[b], src, ACT.Copy).then_inc(act_hi_ready, 1)

            def four_tiles(f, quad):
                return act_tile(f)[:, HALF * quad:HALF * quad + HALF]

            silu(act_tile(FT - 2), 0, 0, FT - 2)
            act.wait_ge(ff_ready, 1)
            down_hi(0, 0, 0, 0, four_tiles(0, 0))
            silu(act_tile(FT - 1), 1, 0, FT - 1)
            down_hi(0, 1, 0, 1, four_tiles(1, 0))
            for quad in range(2):
                for k in range(FT):
                    if not quad and k < 2:
                        continue
                    if k >= 2:
                        act.wait_ge(down_k, quad * (FT - 1) + k - 1)
                    elif k == 0:
                        act.wait_ge(down_k, FT - 1)
                    else:
                        act.wait_ge(down_done, 4)
                    act.wait_ge(ff_ready, k + 1)
                    down_hi(quad, k % 2, 0, k, four_tiles(k, quad))
                    if quad and k in EPILOGUE:
                        t = EPILOGUE.index(k)
                        act.wait_ge(var2, t + 1)
                        act.activation(sd[:, t:t + 1], mv[:, t, 1:2], ACT.Sqrt).then_inc(sd2, 1)
            for t in range(4, NT):
                act.wait_ge(var2, t + 1)
                act.activation(sd[:, t:t + 1], mv[:, t, 1:2], ACT.Sqrt).then_inc(sd2, 1)

        @block.vector
        def _(v):
            own = Chain(v, dve)
            for hf in range(2):
                for t in range(4 * hf, 4 * hf + 4):
                    v.wait_ge(x_in[t], 16)
                    for j in range(2):
                        own.add(v.bn_stats(bn[:, t, 6 * j:6 * j + 6], resid[:, t, j * HALF:(j + 1) * HALF]))
                    own.wait()
                    own.add(v.bn_aggr(mv[:, t, :], bn[:, t, :]))
                own.wait()
                v.tensor_scalar(mv[:, 4 * hf:4 * hf + 4, 1], mv[:, 4 * hf:4 * hf + 4, 1], LN_EPS, None,
                                ALU.add).then_inc(var_ready, 1)
            for hf in range(2):
                v.wait_ge(sd_ready, hf + 1)
                own.add(v.reciprocal(rs[:, 4 * hf:4 * hf + 4], sd[:, 4 * hf:4 * hf + 4]))
                own.wait()
                for t in range(4 * hf, 4 * hf + 4):
                    v.tensor_scalar(resid[:, t, :], resid[:, t, :], mv[:, t, 0:1], rs[:, t:t + 1],
                                    ALU.subtract, ALU.mult).then_inc(norm_ready, 1)
            v.wait_ge(par_in, 16)
            for hf in range(2):
                for k in range(1, KT, 2):
                    v.wait_ge(ln_tr, 8 * hf + k + 1)
                    v.tensor_scalar(hT[:, k, hf * HALF:(hf + 1) * HALF], bank(k), pcol("ln_in_g", k),
                                    pcol("ln_in_b", k), ALU.mult, ALU.add).then_inc(ln_evac_v, 1)
            v.sem_inc(evac_v, NSLOT)
            keep_c = stats[:, 224:224 + NSHIFT]
            own.add(v.tensor_tensor(keep_c, par[:, PARAMS["mu0"][0]:PARAMS["mu0"][0] + NSHIFT],
                                    par[:, PARAMS["mu1"][0]:PARAMS["mu1"][0] + NSHIFT], ALU.add))
            own.wait()
            own.add(v.tensor_scalar(keep_c, keep_c, -1.0, 1.0, ALU.mult, ALU.add))
            ka = PARAMS["k_a"][0]
            own.add(v.tensor_scalar(one_less_ka, par[:, ka:ka + 2], -1.0, 1.0, ALU.mult, ALU.add))
            own.wait()
            behind = NM - NSHIFT
            for j in range(NM):
                s = j % NSLOT
                v.wait_ge(proj_done, j + 1 + NSLOT)
                v.tensor_copy(proj[:, j, 1 + HALF:1 + T], bank(2 * s + 1)).then_inc(evac_v, 1)
                if j >= behind:
                    m = (M_LORA, M_GATE, 2, 3, 0, 1, 4, 5)[j - behind]
                    if j == behind:
                        v.wait_ge(pads, 2)
                        v.wait_ge(spilled, 16)
                    v.wait_ge(evac_a, m + 1 + NSLOT)
                    v.wait_ge(evac_v, m + 1 + NSLOT)
                    own.add(v.tensor_scalar(sh[:, m], tok(m), keep_c[:, m:m + 1], None, ALU.mult))
                    own.wait()
                    own.add(v.scalar_tensor_tensor(out=sh[:, m], in0=proj[:, m, 0:T], scalar=pcol("mu0", m),
                                                   in1=sh[:, m], op0=ALU.mult, op1=ALU.add))
                    own.wait()
                    v.scalar_tensor_tensor(out=sh[:, m], in0=proj[:, m, 2:T + 2], scalar=pcol("mu1", m),
                                           in1=sh[:, m], op0=ALU.mult, op1=ALU.add).then_inc(shift_done, 1)
            for j in range(1, 4, 2):
                v.wait_ge(vproj_done, j + 1)
                v.tensor_copy(v_na[:, 2 * j:2 * j + 2, :],
                              bank(j).rearrange("p (t c) -> p t c", t=2)).then_inc(v_evac, 1)
            v.wait_ge(vproj_done, 4)
            v.wait_ge(v_evac, 4)
            v.tensor_copy(v_sh[0:64], v_na[64:128, 0:NT - 1, :]).then_inc(shifted, 1)
            v.tensor_copy(v_sh[64:128], v_na[0:64, 1:NT, :]).then_inc(shifted, 1)
            v.wait_ge(bias_in, 16)
            v.wait_ge(const_in, 16)
            flat = na_bias.rearrange("p h r c -> p (h r) c")
            keep = cst(C_COLS)[:, 0:64].unsqueeze(1).to_broadcast([P, 2 * NDR, 64])
            fill = cst(C_COLS)[:, 64:128].unsqueeze(1).to_broadcast([P, 2 * NDR, 64])
            own.add(v.tensor_tensor(flat, flat, keep, ALU.mult))
            own.wait()
            v.tensor_tensor(flat, flat, fill, ALU.add).then_inc(bias_ready, 1)
            v.wait_ge(bias_ready, 1)
            for j, n in enumerate((2, 1)):
                v.wait_ge(ms_done, 2 * j + 2)
                v.tensor_scalar(halves(e_ring[j]), psum[:, 2 * j:2 * j + 2, :], 1.0 / (n * P), RMS_EPS,
                                ALU.mult, ALU.add).then_inc(ms_ready, 1)

            def unit_keys(hp, c):
                cols = slice(256 * c, 256 * c + 256)
                if c == 0:
                    v.wait_ge(nrm_sd, hp + 1)
                own.add(v.tensor_scalar(key_norm[hp][:, cols], key_norm[hp][:, cols], 1e-12, None, ALU.max))
                own.wait()
                own.add(v.reciprocal(key_norm[hp][:, cols], key_norm[hp][:, cols]))
                own.wait()
                v.scalar_tensor_tensor(out=kk[:, hp, cols], in0=k_sh[:, hp, cols], scalar=pcol("k_k", hp),
                                       in1=key_norm[hp][:, cols], op0=ALU.mult, op1=ALU.mult).then_inc(kk_ready, 1)

            def unit_latents(j, c):
                cols = slice(256 * c, 256 * c + 256)
                if c == 0:
                    v.wait_ge(ms_sd, j + 1)
                own.add(v.reciprocal(e_ring[j][:, cols], e_ring[j][:, cols]))
                own.wait()
                for k in range(2 - j):
                    lat = tok((M_CQ, M_CKV)[j] + k)[:, cols]
                    v.scalar_tensor_tensor(out=lat, in0=lat, scalar=pcol(("qn_g", "kvn_g")[j], k),
                                           in1=e_ring[j][:, cols], op0=ALU.mult, op1=ALU.mult).then_inc(lat_ready, 1)

            for n in range(NU + 2):
                if n < NU and n % 2:
                    (unit_keys if n < 16 else unit_latents)(n // 8 % 2, n // 2 % 4)
                if n < NU:
                    row, hp, b = n // 2, n % 2, n % 2
                    dr = window(row)[1]
                    v.wait_ge(na_s_done, n + 1)
                    if n >= 2:
                        v.wait_ge(na_e_ready, n - 1)
                    v.scalar_tensor_tensor(out=na_s[:, b], in0=bank(b), scalar=0.125,
                                           in1=na_bias[:, hp, dr:dr + 8, :].rearrange("p r c -> p (r c)"),
                                           op0=ALU.mult, op1=ALU.add).then_inc(na_s_biased, 1)
                    v.wait_ge(na_s_biased, n + 1)
                    v.tensor_reduce(na_max[:, b:b + 1], na_s[:, b], AX.X, ALU.max,
                                    negate=True).then_inc(na_max_ready, 1)
                if n >= 2:
                    b = (n - 2) % 2
                    v.wait_ge(na_e_ready, n - 1)
                    own.add(v.reciprocal(na_inv[:, b:b + 1], na_sum[:, b:b + 1]))
                    v.wait_ge(na_pv, n - 1)
                    if n >= 4:
                        v.wait_ge(na_ot, n - 3)
                    own.wait()
                    for e in range(2):
                        rows = slice(64 * e, 64 * e + 64)
                        v.tensor_scalar(na_o[rows, b], psum[rows, 4 + b, 64 * e:64 * e + 64],
                                        na_inv[rows, b:b + 1], None, ALU.mult).then_inc(na_o_ready, 1)
            v.wait_ge(rope_in, 16)
            v.tensor_tensor(kT[0][64:96, :], gate_sh[64:96], rope_sb[64:96, :], ALU.mult).then_inc(kpe_ready, 1)
            v.tensor_tensor(rope_tmp[64:96, :], gate_sh[96:128], rope_sb[96:128, :], ALU.mult).then_inc(kpe_ready, 1)
            v.wait_ge(kpe_ready, 2)
            v.tensor_tensor(kT[0][64:96, :], kT[0][64:96, :], rope_tmp[64:96, :], ALU.add).then_inc(kpe_ready, 1)
            v.wait_ge(kpe_ready, 3)
            v.tensor_copy(kT[1][64:96, :], kT[0][64:96, :]).then_inc(kpe_ready, 1)

            def head_rope(i, b):
                v.wait_ge(pr_q, 2 * i + (b + 1))
                own.add(v.tensor_tensor(halves(qT[b][64:96, :]), psum[64:96, 0:2, :], halves(rope_sb[64:96, :]),
                                        ALU.mult))
                own.add(v.tensor_tensor(halves(rope_tmp[64:96, :]), psum[96:128, 0:2, :], halves(rope_sb[96:128, :]),
                                        ALU.mult))
                own.wait()
                v.tensor_tensor(qT[b][64:96, :], qT[b][64:96, :], rope_tmp[64:96, :], ALU.add).then_inc(q_rope, 1)

            def head_max(i, b):
                for t in range(NT):
                    v.wait_ge(g_done, 16 * i + (8 * b + t + 1))
                    v.tensor_reduce(g_max[:, b, t:t + 1], psum[:, 4:6, :], AX.XY, ALU.max,
                                    negate=True).then_inc(g_max_ready, 1)

            def head_out(i, b):
                v.wait_ge(pv_done, 16 * i + (8 * b + 8))
                v.reciprocal(halves(inv_sum[0:64, :]), psum[64:128, 6:8, :]).then_inc(o_inv, 1)
                v.wait_ge(o_inv, 2 * i + (b + 1))
                v.tensor_tensor(mix[64 * b:64 * b + 64, ds(4 + i, 1), :].rearrange("p o (h c) -> p (o h) c", h=NH),
                                psum[0:64, 6:8, :], halves(inv_sum[0:64, :]), ALU.mult).then_inc(o_ready, 1)

            v.sem_inc(o_ready, 1)
            head_rope(0, 0)
            head_max(0, 0)
            head_rope(0, 1)
            with v.Fori(0, HEADS // 2 - 1) as i:
                own.enter(i, 4)
                for b in range(2):
                    head_max(i + (b + 1) // 2, (b + 1) % 2)
                    head_out(i, b)
                    head_rope(i + 1, b)
                own.leave(HEADS // 2 - 1)
            head_max(HEADS // 2 - 1, 1)
            for b in range(2):
                head_out(HEADS // 2 - 1, b)
            v.wait_ge(o_ready, HEADS + 1)
            v.wait_ge(kb_ready, 4)
            v.wait_ge(keep_ready, 2)

            def by_chunk(ap):
                return ap.rearrange("p (c t) -> p c t", t=P)

            def sums(q):
                b = q % 2
                own.add(v.tensor_tensor_scan(cum, keep_sum, Rt[:, q], 0.0, ALU.mult, ALU.add))
                own.wait()
                v.scalar_tensor_tensor(out=by_chunk(y1[b]), in0=by_chunk(cum)[:, :, P - 1:P].to_broadcast([P, NT, P]),
                                       scalar=-0.5, in1=by_chunk(cum), op0=ALU.mult, op1=ALU.add).then_inc(y10_ready, 1)
                v.wait_ge(y10_ready, 2 * q + 1)
                v.tensor_tensor(y0[b], y1[b], Rt[:, q], ALU.subtract).then_inc(y10_ready, 1)

            sums(0)
            for q in range(4):
                d, hp, b = q // 2, q % 2, q % 2
                if d == 0:
                    v.scalar_tensor_tensor(out=bonus[:, hp], in0=Kt[:, q], scalar=pcol("r_k", hp), in1=r_sh[:, hp],
                                           op0=ALU.mult, op1=ALU.mult).then_inc(rk_ready, 1)
                if q < 3:
                    if q >= 1:
                        v.wait_ge(ex_ready, (4, 8, 11)[q - 1])
                    sums(q + 1)
                v.wait_ge(ex_ready, (4, 8, 11, 14)[q])
                if d == 0:
                    v.tensor_tensor(Rt[:, q], Rt[:, q], r_sh[:, hp], ALU.mult).then_inc(prods_ready, 1)
                else:
                    v.tensor_tensor(Rt[:, q], At[:, q], r_sh[:, hp], ALU.mult).then_inc(prods_ready, 1)
                v.tensor_tensor(At[:, q], At[:, q], kk[:, hp], ALU.mult).then_inc(prods_ready, 1)
                v.tensor_tensor(Bt[:, q], Bt[:, q], ex[b], ALU.mult).then_inc(prods_ready, 1)
                v.tensor_tensor(Kt[:, q], Kt[:, q], ex[b], ALU.mult).then_inc(prods_ready, 1)
            for hp in range(2):
                v.wait_ge(bonus_done, hp + 1)
                v.tensor_tensor(halves(bonus[:, hp]), psum[:, 2 * hp:2 * hp + 2, :], halves(v_sh2[:, hp]),
                                ALU.mult).then_inc(bonus_ready, 1)
            own.add(v.memset(sfac, 1.0))
            own.wait()
            own.add(v.tensor_tensor(sfac[:, 0:2, 0:NT - 1], gfac[:, 0:2, 0:NT - 1], gfac[:, 0:2, 1:NT], ALU.mult))
            for j in range(NT - 1):
                own.add(v.tensor_tensor(sfac[:, 2:4, j:j + 1], gfac[:, 2:4, NT - 1 - j:NT - j],
                                        gfac[:, 2:4, NT - 2 - j:NT - 1 - j], ALU.mult))
            own.wait()
            v.wait_ge(cleared, 11)
            v.sem_inc(out_v, EACH["dve"])
            with v.Fori(0, NT) as i:
                own.enter(i, 8)
                for name, who in JOBS:
                    if who != "dve":
                        continue
                    bk = JOB[name] % NBANK
                    computed(v, i, name)
                    kind = name.split(".")[0][:-1]
                    d = int(name.split(".")[0][-1])
                    ps4 = bank(bk).rearrange("p (h t) -> p h t", h=4)
                    if kind == "N":
                        own.add(v.tensor_tensor(Wm[d], ps4, four_heads(cst(C_LVT if d == 0 else C_LV)), ALU.mult))
                        own.wait()
                        ins = v.tensor_tensor(Wm[d], Wm[d], four_heads(ident), ALU.add)
                    elif kind in ("KA", "R", "KR"):
                        dst = {"KA": KAm, "R": Rm, "KR": KRm}[kind][d]
                        mask = (C_BEFORE_F, C_BEFORE_B)[d] if kind == "KA" else (C_REC_F, C_REC_B)[d]
                        ins = v.tensor_tensor(dst, ps4, four_heads(cst(mask)), ALU.mult)
                    elif kind in ("W", "T"):
                        dst = (Wm if kind == "W" else Tm)[d]
                        ins = v.tensor_tensor(dst, ps4, dst, ALU.add)
                    elif kind == "AZ":
                        taken(v, i, f"AV{d}")
                        ins = v.tensor_tensor(Xs[d].rearrange("p h c -> p (h c)"), bank(bk, 256),
                                              AVs[d].rearrange("p h c -> p (h c)"), ALU.add)
                    elif kind == "S":
                        for e in range(2):
                            rows = slice(64 * e, 64 * e + 64)
                            own.add(v.tensor_tensor(Zs[d][rows, :, 64 * e:64 * e + 64],
                                                    bank(bk, 256, rows).rearrange("p (h c) -> p h c", h=2)[:, :, 64 * e:64 * e + 64],
                                                    Zs[d][rows, :, 64 * e:64 * e + 64], ALU.add))
                        own.wait()
                        for hp in range(2):
                            ins = v.tensor_scalar(Zs[d][:, hp, :], Zs[d][:, hp, :], sfac[:, 2 * d + hp, ds(i, 1)], None,
                                                  ALU.mult)
                            if hp == 0:
                                own.add(ins)
                    else:
                        ychunk = chunk(y_out, d, i)
                        ins = v.tensor_tensor(ychunk, bank(bk, 256).rearrange("p (h t) -> p h t", h=2), ychunk, ALU.add)
                    ins.then_inc(out_v, 1)
                own.leave(NT)
            for hp in range(2):
                v.wait_ge(gn_mean, hp + 1)
                v.scalar_tensor_tensor(out=halves(At[:, hp]), in0=psum[:, 2 * hp:2 * hp + 2, :], scalar=-1.0 / 64,
                                       in1=halves(y_out[:, hp]), op0=ALU.mult, op1=ALU.add).then_inc(gn_centred, 1)
            for hp in range(2):
                v.wait_ge(gn_var, hp + 1)
                v.tensor_scalar(halves(Bt[:, hp]), psum[:, 4 + 2 * hp:6 + 2 * hp, :], 1.0 / 64, GN_EPS,
                                ALU.mult, ALU.add).then_inc(gn_ms, 1)
            for hp in range(2):
                v.wait_ge(gn_sd, hp + 1)
                own.add(v.reciprocal(Bt[:, hp], Bt[:, hp]))
                own.wait()
                own.add(v.tensor_tensor(At[:, hp], At[:, hp], Bt[:, hp], ALU.mult))
                own.wait()
                own.add(v.tensor_scalar(At[:, hp], At[:, hp], pcol("gn_g", hp), pcol("gn_b", hp), ALU.mult, ALU.add))
                own.wait()
                own.add(v.tensor_tensor(At[:, hp], At[:, hp], bonus[:, hp], ALU.add))
                own.wait()
                v.tensor_tensor(y_out[:, hp], At[:, hp], gate_o[:, hp], ALU.mult).then_inc(o_rw, 1)

            def variances(t):
                for j in range(2):
                    own.add(v.bn_stats(bn[:, t, 6 * j:6 * j + 6], resid[:, t, j * HALF:(j + 1) * HALF]))
                own.wait()
                own.add(v.bn_aggr(mv[:, t, :], bn[:, t, :]))
                own.wait()

            def normalise1(hf):
                v.wait_ge(sd1, hf + 1)
                own.add(v.reciprocal(rs[:, 4 * hf:4 * hf + 4], sd[:, 4 * hf:4 * hf + 4]))
                own.wait()
                for t in range(4 * hf, 4 * hf + 4):
                    v.tensor_scalar(resid[:, t, :], resid[:, t, :], mv[:, t, 0:1], rs[:, t:t + 1],
                                    ALU.subtract, ALU.mult).then_inc(norm1, 1)

            def transposed1(hf):
                for k in range(KT):
                    if k % 2:
                        v.wait_ge(tr1, 8 * hf + k + 1)
                        v.tensor_scalar(h1_tmp[k % 4], bank(4 + k % 4), pcol("ln1_g", k), pcol("ln1_b", k),
                                        ALU.mult, ALU.add).then_inc(h1_tmp_ready[1], 1)
                    v.wait_ge(h1_hi_ready, 8 * hf + k + 1)
                    v.tensor_tensor(h1_lo[k][:, hf * HALF:(hf + 1) * HALF], h1_tmp[k % 4],
                                    h1_hi[k][:, hf * HALF:(hf + 1) * HALF], ALU.subtract).then_inc(h1_lo_ready, 1)

            def weights_lo(n, b, j, c):
                v.wait_ge(w_hi_ready[n], 2 * j + (c + 1))
                v.tensor_tensor(w_lo[b][n], raw_w[n], w_hi[b][n], ALU.subtract).then_inc(w_lo_ready[n], 1)

            v.wait_ge(resid_in, 16)
            for t in range(NT):
                b = 2 * (t % 2)
                if t == 6:
                    transposed1(0)
                v.wait_ge(mixed, t + 1)
                v.scalar_tensor_tensor(out=halves(resid[:, t]), in0=halves(resid[:, t]), scalar=ALPHA,
                                       in1=psum[:, b:b + 2, :], op0=ALU.mult, op1=ALU.add).then_inc(sum1, 1)
                v.wait_ge(sum1, t + 1)
                variances(t)
                if t % 4 == 3:
                    hf = t // 4
                    v.tensor_scalar(mv[:, 4 * hf:4 * hf + 4, 1], mv[:, 4 * hf:4 * hf + 4, 1], LN_EPS, None,
                                    ALU.add).then_inc(var1, 1)
                    normalise1(hf)
                    if hf == 0:
                        weights_lo(0, 0, 0, 0)
            transposed1(1)
            weights_lo(1, 0, 0, 0)
            for n in range(2):
                weights_lo(n, 1, 0, 1)

            def times_up(dst, b, j, c):
                v.wait_ge(silu_ready, 2 * j + (c + 1))
                v.tensor_tensor(halves(dst), psum[:, 4 * b + 2:4 * b + 4, :], halves(dst), ALU.mult).then_inc(ff_ready, 1)

            for first, at0, times in ((0, 8192, EARLY // 2), (EARLY, 0, (FT - EARLY) // 2 - 1)):
                with v.Fori(0, times) as j:
                    for b in range(2):
                        times_up(arena[:, ds(j * 2048 + (at0 + 1024 * b), 1024)], b, j, first + b)
                        for n in range(2):
                            weights_lo(n, b, j, first + b + 2)

            def down_lo(quad, k):
                b, n = k % 2, quad * FT + k
                v.wait_ge(wd_hi_ready, n + 1)
                v.tensor_tensor(wd_lo[b], raw_w[b], wd_hi[b], ALU.subtract).then_inc(wd_lo_ready, 1)
                v.wait_ge(act_hi_ready, n + 1)
                v.tensor_tensor(act_lo[b], act_tile(k)[:, HALF * quad:HALF * quad + HALF], act_hi[b],
                                ALU.subtract).then_inc(act_lo_ready, 1)

            def sum_down(t):
                b = 2 * (t % 4)
                v.wait_ge(down_done, t + 1)
                v.scalar_tensor_tensor(out=halves(resid2[:, t]), in0=halves(resid2[:, t]), scalar=ALPHA,
                                       in1=psum[:, b:b + 2, :], op0=ALU.mult, op1=ALU.add).then_inc(sum2, 1)

            def finish(t):
                v.wait_ge(sum2, t + 1)
                for j in range(2):
                    own.add(v.bn_stats(bn[:, t, 6 * j:6 * j + 6], resid2[:, t, j * HALF:(j + 1) * HALF]))
                own.wait()
                own.add(v.bn_aggr(mv[:, t, :], bn[:, t, :]))
                own.wait()
                v.tensor_scalar(mv[:, t, 1:2], mv[:, t, 1:2], LN_EPS, None, ALU.add).then_inc(var2, 1)
                own.add(v.scalar_tensor_tensor(out=resid2[:, t], in0=resid2[:, t], scalar=mv[:, t, 0:1],
                                               in1=ln2_rows[0], op0=ALU.subtract, op1=ALU.mult))
                v.wait_ge(sd2, t + 1)
                own.add(v.reciprocal(rs[:, t:t + 1], sd[:, t:t + 1]))
                own.wait()
                v.scalar_tensor_tensor(out=resid2[:, t], in0=resid2[:, t], scalar=rs[:, t:t + 1],
                                       in1=ln2_rows[1], op0=ALU.mult, op1=ALU.add).then_inc(y_ready, 1)

            times_up(act_tile(FT - 2), 0, 0, FT - 2)
            down_lo(0, 0)
            times_up(act_tile(FT - 1), 1, 0, FT - 1)
            for k in range(1, FT):
                down_lo(0, k)
            down_lo(1, 0)
            v.wait_ge(resid2_in, 16)
            for t in range(4):
                sum_down(t)
            v.wait_ge(rows2_in, 32)
            for k in range(1, FT):
                down_lo(1, k)
                if k in EPILOGUE:
                    finish(EPILOGUE.index(k))
            for t in range(4, NT):
                sum_down(t)
                finish(t)

        @block.tensor
        def _(pe):
            pe.wait_ge(const_in, 16)
            for hf in range(2):
                pe.wait_ge(norm_ready, 4 * hf + 4)
                for k in range(KT):
                    if hf:
                        pe.wait_ge((ln_evac_a, ln_evac_v)[k % 2], k // 2 + 1)
                    for t in range(4):
                        mm = pe.transpose(psum[:, k, t * P:(t + 1) * P],
                                          resid[:, 4 * hf + t, k * P:(k + 1) * P], ident)
                    mm.then_inc(ln_tr, 1)
            pe.wait_ge(ln_evac_a, 8)
            pe.wait_ge(ln_evac_v, 8)
            pe.sem_inc(proj_done, NSLOT)
            with pe.Fori(0, NM // NSLOT) as i:
                for s in range(NSLOT):
                    pe.wait_ge(w_in_ready[s], i * 16 + 16)
                    pe.wait_ge(evac_a, i * NSLOT + (s + 1))
                    pe.wait_ge(evac_v, i * NSLOT + (s + 1))
                    for hf in range(NH):
                        for k in range(KT):
                            mm = pe.matmul(bank(2 * s + hf), w_ring[s][:, k, :],
                                           hT[:, k, hf * HALF:(hf + 1) * HALF], start=(k == 0), stop=(k == KT - 1))
                    mm.then_inc(proj_done, 1)
            pe.wait_ge(wv_in, 16)
            pe.wait_ge(evac_a, NM + NSLOT)
            pe.wait_ge(evac_v, NM + NSLOT)
            for j in range(4):
                for t in range(2):
                    for k in range(KT):
                        mm = pe.matmul(psum[:, j, 256 * t:256 * t + 256], hT[:, k, (2 * j + t) * P:(2 * j + t + 1) * P],
                                       wv_sb[:, k, :], start=(k == 0), stop=(k == KT - 1))
                mm.then_inc(vproj_done, 1)
            def over_channels(b, weights, rhs):
                for hf in range(NH):
                    mm = pe.matmul(bank(b + hf), weights, rhs[:, hf * HALF:(hf + 1) * HALF], start=True, stop=True)
                return mm

            def low_rank(j):
                if j >= 2:
                    pe.wait_ge(z_sig, j - 1)
                over_channels(2 * (j % 2) + 4, lora_w[:, j, :], lora_sh).then_inc(z_done, 1)

            pe.wait_ge(v_evac, 4)
            pe.wait_ge(lora_in, 16)
            pe.wait_ge(lora_act, 2)
            for j in range(2):
                low_rank(j)
            for hp in range(2):
                pe.wait_ge(nrm_sq, hp + 1)
                over_channels(2 * hp, cst(C_HEADS), key_norm[hp]).then_inc(nrm_done, 1)
            pe.wait_ge(sq_ready, 3)
            for j, tiles_of in enumerate(((0, 1), (2,))):
                pe.wait_ge(nrm_sd, j + 1)
                for hf in range(NH):
                    for n, m in enumerate(tiles_of):
                        mm = pe.matmul(bank(2 * j + hf), cst(C_ONES), e_ring[m][:, hf * HALF:(hf + 1) * HALF],
                                       start=(n == 0), stop=(n == len(tiles_of) - 1))
                    mm.then_inc(ms_done, 1)
            for j in range(2, 8):
                low_rank(j)
            pe.wait_ge(shifted, 2)
            pe.wait_ge(ms_ready, 2)
            pe.wait_ge(z_sig, 8)
            for n in range(NU + 3):
                if n < NU:
                    row, hp, b = n // 2, n % 2, n % 2
                    first = window(row)[0]
                    pe.wait_ge(q_diag_ready, 2 * (n + 1))
                    if n >= 2:
                        pe.wait_ge(na_s_biased, n - 1)
                    pe.matmul(bank(b), q_diag[:, b, :], proj[:, M_NK + hp, 1 + 64 * first:1 + 64 * first + HALF],
                              start=True, stop=True).then_inc(na_s_done, 1)
                if 1 <= n <= NU:
                    b = (n - 1) % 2
                    pe.wait_ge(na_e_ready, n)
                    if n >= 3:
                        pe.wait_ge(na_et_ready, n - 2)
                    for j in range(4):
                        mm = pe.transpose(psum[:, 2 + b, j * P:(j + 1) * P], na_e[:, b, j * P:(j + 1) * P], ident)
                    mm.then_inc(na_tr, 1)
                if 2 <= n <= NU + 1:
                    row, hp, b = (n - 2) // 2, (n - 2) % 2, n % 2
                    first = window(row)[0]
                    vals = v_sh if first % 2 else v_na
                    pe.wait_ge(na_et_ready, n - 1)
                    if n >= 4:
                        pe.wait_ge(na_o_ready, 2 * (n - 3))
                    for j in range(4):
                        mm = pe.matmul(bank(4 + b, P), na_et[:, b, j * P:(j + 1) * P],
                                       vals[:, first // 2 + j, hp * P:(hp + 1) * P], start=(j == 0), stop=(j == 3))
                    mm.then_inc(na_pv, 1)
                if n >= 3:
                    b = (n - 3) % 2
                    pe.wait_ge(na_o_ready, 2 * (n - 2))
                    if n >= 5:
                        pe.wait_ge(na_mixed, 2 * (n - 4))
                    pe.transpose(psum[0:64, 6 + b, 0:P], na_o[:, b], ident).then_inc(na_ot, 1)
            pe.wait_ge(na_mixed, 2 * NU)
            pe.wait_ge(lat_ready, 12)

            def head_project(i, b):
                pe.wait_ge(w_head[b], 32 * i + 32)
                for hf in range(NH):
                    for k in range(2):
                        mm = pe.matmul(bank(hf), w_q[b][:, k, :], tok(M_CQ + k)[:, hf * HALF:(hf + 1) * HALF],
                                       start=(k == 0), stop=(k == 1))
                mm.then_inc(pr_q, 1)
                for hf in range(NH):
                    mm = pe.matmul(bank(2 + hf, rows=slice(0, 64)), w_kv[b][:, 0:64],
                                   tok(M_CKV)[:, hf * HALF:(hf + 1) * HALF], start=True, stop=True)
                mm.then_inc(pr_k, 1)

            def head_values(i, b):
                for t in range(NT):
                    mm = pe.matmul(psum[:, 4 + t // 4, t % 4 * P:t % 4 * P + P], tok(M_CKV)[:, t * P:(t + 1) * P],
                                   w_kv[b], start=True, stop=True)
                mm.then_inc(pr_v, 1)

            def guard(i, b, t):
                if t == 0:
                    pe.wait_ge(q_rounded, 2 * i + (b + 1))
                    pe.wait_ge(k_rounded, 2 * i + (b + 1))
                    pe.wait_ge(v_ready, 2 * i + (b + 1))
                else:
                    pe.wait_ge(g_max_ready, 16 * i + (8 * b + t))
                for hf in range(NH):
                    mm = pe.matmul(bank(4 + hf), q_round[0:96, t * P:(t + 1) * P],
                                   k_round[0:96, hf * HALF:(hf + 1) * HALF], start=True, stop=True)
                mm.then_inc(g_done, 1)

            def turn_max(i, b):
                pe.wait_ge(g_max_ready, 16 * i + (8 * b + 8))
                pe.transpose(psum[0:NT, 4, 0:P], g_max[:, b, :], ident).then_inc(mt_done, 1)

            def scores(i, b, kt, ahead):
                if kt == 0:
                    pe.wait_ge(max_in[b], 16 * i + 16)
                    for copied in (q_nope, q_rope, k_rounded):
                        pe.wait_ge(copied, 2 * i + (b + 1 + ahead))
                if kt >= 2:
                    pe.wait_ge(e_ready, 16 * i + (8 * b + kt - 1))
                for hf in range(NH):
                    mm = pe.matmul(bank(2 * (kt % 2) + hf), kT[b][0:97, kt * P:(kt + 1) * P],
                                   qT[b][0:97, hf * HALF:(hf + 1) * HALF], start=True, stop=True)
                mm.then_inc(s_done, 1)

            def values(i, b, kt):
                pe.wait_ge(e_ready, 16 * i + (8 * b + kt + 1))
                if kt == 0:
                    pe.wait_ge(o_ready, 2 * i + (b + 1))
                for hf in range(NH):
                    mm = pe.matmul(bank(6 + hf), vh[b][:, kt, :], e_ring[kt % NE][:, hf * HALF:(hf + 1) * HALF],
                                   start=(kt == 0), stop=(kt == NT - 1))
                mm.then_inc(pv_done, 1)

            def head(i, b, ahead, ahead2):
                nxt = (i + (b + 1) // 2, (b + 1) % 2)
                for kt in range(NT):
                    scores(i, b, kt, ahead)
                    if ahead:
                        guard(*nxt, kt)
                    if kt:
                        values(i, b, kt - 1)
                values(i, b, NT - 1)
                if ahead:
                    turn_max(*nxt)
                if ahead2:
                    head_project(i + 1, b)
                    pe.wait_ge(mt_copied, 2 * nxt[0] + (nxt[1] + 1))
                    head_values(i + 1, b)

            pe.wait_ge(kpe_round, 1)
            pe.wait_ge(v_ones, 4)
            head_project(0, 0)
            head_values(0, 0)
            for t in range(NT):
                guard(0, 0, t)
            turn_max(0, 0)
            pe.wait_ge(q_rounded, 1)
            head_project(0, 1)
            pe.wait_ge(mt_copied, 1)
            head_values(0, 1)
            with pe.Fori(0, HEADS // 2 - 1) as i:
                for b in range(2):
                    head(i, b, True, True)
            for b in range(2):
                head(HEADS // 2 - 1, b, b == 0, False)
            pe.wait_ge(o_ready, HEADS + 1)
            pe.wait_ge(gate_w_in, 16)
            for hp in range(2):
                over_channels(4 + 2 * hp, gate_w[:, hp, :], gate_sh).then_inc(gate_done, 1)
            for hp in range(2):
                pe.wait_ge(rk_ready, hp + 1)
                over_channels(2 * hp, cst(C_HEADS), bonus[:, hp]).then_inc(bonus_done, 1)
            pe.wait_ge(gate_ready, 2)
            pe.wait_ge(bonus_ready, 2)
            pe.sem_inc(job_done, NJ)
            with pe.Fori(0, NT) as i:
                for j, (name, who) in enumerate(JOBS):
                    bk = j % NBANK
                    last = JOBS[j - NBANK if j >= NBANK else LAST_IN_BANK[bk]][0]
                    taken(pe, i, last, before=j < NBANK)
                    kind = name.split(".")[0].rstrip("01")
                    d = int(name.split(".")[0][len(kind)])
                    m = int(name.split(".")[1]) if "." in name else 0
                    if kind in ("A", "N", "KA", "R", "KR") and name == "A0":
                        pe.wait_ge(staged, i * 24 + 24)
                    if kind == "A":
                        for hp in range(2):
                            mm = pe.matmul(psum[:, bk, 256 * hp:256 * hp + 256], As[2 * d + hp],
                                           Bm[2 * d + hp].rearrange("p e t -> p (e t)"), start=True, stop=True)
                    elif kind in ("N", "KA", "R", "KR"):
                        for h in range(4):
                            q, e = 2 * d + h // 2, h % 2
                            lhs = (Km if kind[0] == "K" else Bm)[q][:, e, :]
                            rhs = As[q] if kind in ("N", "KA") else chunk(Rt[:, q:q + 1], d, i)[:, 0]
                            mm = pe.matmul(psum[:, bk, P * h:P * h + P], lhs, rhs, start=True, stop=True)
                    elif kind == "tok":
                        q = 2 * d + int(name[-1])
                        for n, src in enumerate((Bm[q], Km[q])):
                            for e in range(2):
                                mm = pe.transpose(psum[:, bk, 256 * n + P * e:256 * n + P * e + P], src[:, e, :], ident)
                    elif kind == "V":
                        for hp in range(2):
                            mm = pe.transpose(psum[:, bk, P * hp:P * hp + P], Vs[2 * d + hp], ident)
                    elif kind == "AV":
                        taken(pe, i, f"KA{d}")
                        taken(pe, i, f"V{d}")
                        for h in range(4):
                            mm = pe.matmul(psum[:, bk, P * h:P * h + P], KAm[d][:, h, :],
                                           tokv[d][:, h // 2, :], start=True, stop=True)
                    elif kind == "G":
                        pe.wait_ge(lev_ready, i * 2 * (LEVELS - 1) + 2 * (m - 1) + d + 1)
                        taken(pe, i, f"N{d}" if m == 1 else f"W{d}.{m - 1}")
                        for h in range(4):
                            mm = pe.matmul(psum[:, bk, P * h:P * h + P], Alev[d][m % 2][:, h, :], Wm[d][:, h, :],
                                           start=True, stop=True)
                    elif kind == "W":
                        taken(pe, i, f"G{d}.{m}")
                        if m == 1:
                            pe.wait_ge(t0_ready, i * 2 + d + 1)
                        else:
                            taken(pe, i, f"T{d}.{m - 1}")
                        for h in range(4):
                            mm = pe.matmul(psum[:, bk, P * h:P * h + P], Tm[d][:, h, :], Gm[d][:, h, :],
                                           start=True, stop=True)
                    elif kind == "T":
                        for h in range(4):
                            mm = pe.matmul(psum[:, bk, P * h:P * h + P], Gm[d][:, h, :], Tm[d][:, h, :],
                                           start=True, stop=True)
                    elif kind == "AZ":
                        taken(pe, i, f"S{d}", before=True)
                        for hp in range(2):
                            mm = pe.matmul(psum[:, bk, P * hp:P * hp + P], As[2 * d + hp], Zs[d][:, hp, :],
                                           start=True, stop=True)
                    elif kind == "U":
                        taken(pe, i, f"W{d}.{LEVELS - 1}")
                        taken(pe, i, f"AZ{d}")
                        for h in range(4):
                            mm = pe.matmul(psum[:, bk, P * h:P * h + P], Wm[d][:, h, :], Xs[d][:, h // 2, :],
                                           start=True, stop=True)
                    elif kind == "Y":
                        taken(pe, i, f"U{d}")
                        taken(pe, i, f"KR{d}")
                        for hp in range(2):
                            q = 2 * d + hp
                            cols = slice(P * hp, P * hp + P)
                            pe.matmul(psum[:, bk, cols], Zs[d][:, hp, :], chunk(Rt[:, q:q + 1], d, i)[:, 0],
                                      start=True, stop=False, skip_group_check=True)
                            for e in range(2):
                                rows, own_half = slice(64 * e, 64 * e + 64), slice(64 * e, 64 * e + 64)
                                pe.matmul(psum[rows, bk, cols], Us[d][:, hp, own_half], Rm[d][:, 2 * hp + e, :],
                                          start=False, stop=False, skip_group_check=True)
                                mm = pe.matmul(psum[rows, bk, cols], tokv[d][:, hp, own_half], KRm[d][:, 2 * hp + e, :],
                                               start=False, stop=True, skip_group_check=True)
                    else:
                        for hp in range(2):
                            q = 2 * d + hp
                            cols = slice(P * hp, P * hp + P)
                            pe.matmul(psum[:, bk, cols], tokm[q][:, 0, :], Us[d][:, hp, :], start=True, stop=False)
                            mm = pe.matmul(psum[:, bk, cols], tokm[q][:, 1, :], tokv[d][:, hp, :], start=False, stop=True)
                    mm.then_inc(job_done, 1)
            taken(pe, NT - 1, "S1")
            for hp in range(2):
                over_channels(2 * hp, cst(C_HEADS), y_out[:, hp]).then_inc(gn_mean, 1)
            for hp in range(2):
                pe.wait_ge(gn_sq, hp + 1)
                over_channels(4 + 2 * hp, cst(C_HEADS), Bt[:, hp]).then_inc(gn_var, 1)

            def turn1(hf):
                pe.wait_ge(norm1, 4 * hf + 4)
                for k in range(KT):
                    n = 8 * hf + k
                    if n >= 4:
                        pe.wait_ge(h1_tmp_ready[k % 2], (n - 4) // 2 + 1)
                    for t in range(4):
                        mm = pe.transpose(psum[:, 4 + k % 4, t * P:(t + 1) * P],
                                          resid[:, 4 * hf + t, k * P:(k + 1) * P], ident)
                    mm.then_inc(tr1, 1)

            pe.wait_ge(o_rw, 2)
            pe.wait_ge(w_out_in, 16 * 8)
            for t in range(NT):
                if t >= 2:
                    pe.wait_ge(sum1, t - 1)
                if t == 6:
                    turn1(0)
                for hf in range(NH):
                    for k in range(8):
                        mm = pe.matmul(bank(2 * (t % 2) + hf), mix[:, k, t * P:(t + 1) * P],
                                       w_out[k][:, hf * HALF:(hf + 1) * HALF], start=(k == 0), stop=(k == 7))
                mm.then_inc(mixed, 1)
            turn1(1)
            pe.wait_ge(h1_lo_ready, 2 * KT)

            def gate_up(b, j, c):
                for n in range(2):
                    pe.wait_ge(w_lo_ready[n], 2 * j + (c + 1))
                    for hf in range(NH):
                        cols = slice(hf * HALF, (hf + 1) * HALF)
                        for k in range(KT):
                            for i, (w, x) in enumerate(((w_hi, h1_hi), (w_hi, h1_lo), (w_lo, h1_hi))):
                                mm = pe.matmul(bank(4 * b + 2 * n + hf), w[b][n][:, P * k:P * k + P], x[k][:, cols],
                                               start=(k == 0 and i == 0), stop=(k == KT - 1 and i == 2))
                mm.then_inc(ff_done, 1)

            gate_up(0, 0, 0)
            gate_up(1, 0, 1)
            with pe.Fori(0, FT // 2 - 1) as j:
                for b in range(2):
                    pe.wait_ge(ff_ready, 2 * j + (b + 1))
                    gate_up(b, j, b + 2)

            def down(b, j, n, ends=None, free=None):
                pe.wait_ge(wd_lo_ready, 2 * j + (n + 1))
                pe.wait_ge(act_lo_ready, 2 * j + (n + 1))
                for t in range(4):
                    if free:
                        pe.wait_ge(free, t + 1 if free is sum2 else FT - 1 + t // 2)
                    for hf in range(NH):
                        for i, (x, w) in enumerate(((act_hi, wd_hi), (act_hi, wd_lo), (act_lo, wd_hi))):
                            mm = pe.matmul(bank(2 * t + hf), x[b][:, t * P:(t + 1) * P],
                                           w[b][:, hf * HALF:(hf + 1) * HALF],
                                           start=(free is not None and i == 0), stop=(ends is not None and i == 2))
                    if ends:
                        mm.then_inc(down_done, 1)
                if not ends:
                    mm.then_inc(down_k, 1)

            for quad in range(2):
                down(0, 0, quad * FT, free=sum2 if quad else ff_ready)
                down(1, 0, quad * FT + 1)
                with pe.Fori(0, FT // 2 - 2) as j:
                    for b in range(2):
                        down(b, j, quad * FT + 2 + b)
                down(0, 0, quad * FT + FT - 2)
                down(1, 0, quad * FT + FT - 1, ends=down_done)


def tables():
    import numpy as np
    r = np.arange(P)
    row, col = r[:, None], r[None, :]
    c = np.zeros((P, NC, P), np.float32)
    c[:, C_ID] = np.eye(P)
    c[:, C_HEADS] = row // 64 == col // 64
    c[:, C_ONES] = 1
    c[:, C_BEFORE_F] = row < col
    c[:, C_BEFORE_B] = row > col
    c[:, C_REC_F] = row <= col
    c[:, C_REC_B] = row > col
    for m in range(LEVELS):
        b = 1 << m
        lv = (row // (2 * b) == col // (2 * b)) & (row // b % 2 == 1) & (col // b % 2 == 0)
        c[:, C_LV + m] = lv
        c[:, C_LVT + m] = lv.T
    j, kc = np.arange(P) % 64, np.arange(64)
    start = np.clip(j - 8, 0, 48)[:, None]
    ok = (kc >= start) & (kc < start + 16)
    c[:, C_COLS, 0:64] = ok
    c[:, C_COLS, 64:128] = np.where(ok, 0, -1e30)
    return c.reshape(P, NC * P)


def rope():
    import numpy as np
    inv = np.power(np.float32(10000.0), -np.arange(0, 32, 2, dtype=np.float32) / np.float32(32)).astype(np.float32)
    ang = (np.arange(T, dtype=np.float32)[:, None] * inv[None, :]).astype(np.float32)
    cos, sin = np.cos(ang).T, np.sin(ang).T
    one = np.concatenate([np.concatenate([cos, cos]), np.concatenate([-sin, sin])], 0)
    return np.ascontiguousarray(np.concatenate([one, one], 0), np.float32)


def layout(x, ln_in_g, ln_in_b, w_in, rw_mu, rw_w0, rw_w2, rw_a0, rw_a2, rw_g2, rw_k_k, rw_k_a,
           rw_r_k, rw_gn_g, rw_gn_b, na_rpb, mla_q_norm_g, mla_w_q_b, mla_kv_norm_g, mla_w_kv_b,
           w_out, ln1_g, ln1_b, w_ffn_gate, w_ffn_up, w_ffn_down, ln2_g, ln2_b):
    import numpy as np
    f = np.float32
    z = {}
    z["x"] = np.asarray(x).reshape(NT, P, D)
    w = np.asarray(w_in)[0]
    pe0 = 960 + 768 + 384
    cols = list(range(0, 960)) + list(range(pe0, pe0 + 32)) + list(range(pe0 + 16, pe0 + 32)) + \
        list(range(pe0, pe0 + 16)) + list(range(960, 960 + 512)) + list(range(1728, 1728 + 384))
    assert len(cols) == NM * P
    z["w_in"] = w[:, cols].reshape(KT, P, NM, P).transpose(2, 1, 0, 3)
    z["w_nv"] = w[:, 960 + 512:1728].reshape(KT, P, 256).transpose(1, 0, 2)
    par = np.zeros((P, NPAR), f)

    def put(name, v):
        at, n = PARAMS[name]
        par[:, at:at + n] = np.asarray(v).reshape(n, P).T

    put("ln_in_g", ln_in_g)
    put("ln_in_b", ln_in_b)
    mu = np.zeros((2, NSHIFT * P), f)
    mu[:, :960] = np.asarray(rw_mu)[0]
    put("mu0", mu[0])
    put("mu1", mu[1])
    for name, v in (("w0", rw_w0), ("a0", rw_a0), ("k_k", rw_k_k), ("k_a", rw_k_a), ("r_k", rw_r_k),
                    ("gn_g", rw_gn_g), ("gn_b", rw_gn_b), ("qn_g", mla_q_norm_g), ("kvn_g", mla_kv_norm_g),
                    ("ln1_g", ln1_g), ("ln1_b", ln1_b)):
        put(name, v)
    z["params"] = par
    z["rows"] = np.stack([np.asarray(v).reshape(-1) for v in (ln_in_g, ln_in_b, ln1_g, ln1_b, ln2_g, ln2_b)])
    z["consts"] = tables()
    z["rope"] = rope()
    lora = np.zeros((10, P, P), f)
    for d in range(2):
        for hp in range(2):
            lora[2 * d + hp, 32 * d:32 * d + 32] = np.asarray(rw_w2)[0, d][:, hp * P:(hp + 1) * P]
            lora[4 + 2 * d + hp, 64 + 32 * d:96 + 32 * d] = np.asarray(rw_a2)[0, d][:, hp * P:(hp + 1) * P]
    for hp in range(2):
        lora[8 + hp, 0:64] = np.asarray(rw_g2)[0][:, hp * P:(hp + 1) * P]
    z["lora"] = lora.transpose(1, 0, 2)
    dc = np.clip(np.arange(64)[None, :] - np.arange(64)[:, None] + 15, 0, NDC - 1)
    z["rpb"] = np.asarray(na_rpb)[0][:, :, dc].reshape(2, 2, NDR, 64, 64).transpose(1, 3, 0, 2, 4).reshape(P, 2, NDR, 64)
    wq = np.asarray(mla_w_q_b)[0].reshape(2, P, 8, 96)
    sw = list(range(96)) + list(range(80, 96)) + list(range(64, 80))
    z["w_q"] = wq[:, :, :, sw].transpose(2, 1, 0, 3)
    z["w_kv"] = np.asarray(mla_w_kv_b)[0].reshape(P, 8, P).transpose(1, 0, 2)
    z["w_out"] = np.asarray(w_out)[0].reshape(8, P, 1024)
    z["w_gate"] = np.asarray(w_ffn_gate)[0].reshape(KT, P, FT, P).transpose(2, 1, 0, 3)
    z["w_up"] = np.asarray(w_ffn_up)[0].reshape(KT, P, FT, P).transpose(2, 1, 0, 3)
    z["w_down"] = np.asarray(w_ffn_down)[0].reshape(FT, P, 1024)
    return {k: np.ascontiguousarray(v) for k, v in z.items()}


def kernel(**inputs):
    import concourse.bacc as bacc
    from concourse.bass_utils import run_bass_kernel_spmd

    nc = bacc.Bacc("TRN2", target_bir_lowering=False, num_devices=1)
    arrays = layout(**inputs)
    aps = {n: nc.dram_tensor(f"in_{n}", v.shape, mybir.dt.from_np(v.dtype), kind="ExternalInput").ap()
           for n, v in arrays.items()}
    y = nc.dram_tensor("out_y", (NT, P, D), F32, kind="ExternalOutput").ap()
    hybrid_encoder(nc, aps, y)
    r = run_bass_kernel_spmd(nc, [{f"in_{n}": v for n, v in arrays.items()}], core_ids=[0])
    return r.results[0]["out_y"].reshape(1, T, D)
```

```python
from contextlib import ExitStack

import concourse.bass as bass
from concourse import mybir

F32 = mybir.dt.float32
F32R = mybir.dt.float32r
ALU = mybir.AluOpType
ACT = mybir.ActivationFunctionType
AX = mybir.AxisListType
ds = bass.ds

P = 128
T = 1024
D = 1024
NT = T // P
KT = D // P
HALF = 512
NH = T // HALF
D_FF = 2816
FT = D_FF // P
LN_EPS, RMS_EPS, GN_EPS = 1e-5, 1e-6, 64e-5
ALPHA = 2 ** 0.25
DECAY_SCALE = 0.6065306597126334

M_R, M_K, M_V, M_LORA, M_GATE, M_NQ, M_NK, M_CQ, M_CKV = 0, 2, 4, 6, 7, 8, 10, 12, 14
NM = 15
NSHIFT = 8
PW = T + 2

LEVELS = 7
C_ID, C_HEADS, C_ONES, C_REC_F, C_REC_B, C_BEFORE_F, C_BEFORE_B, C_LV = 0, 1, 2, 3, 4, 5, 6, 7
C_LVT = C_LV + LEVELS
C_COLS = C_LVT + LEVELS
NC = C_COLS + 1

PARAMS = {}


def _params():
    at = 0
    for name, n in (("ln_in_g", 8), ("ln_in_b", 8), ("mu0", 8), ("mu1", 8), ("w0", 4), ("a0", 4),
                    ("k_k", 2), ("k_a", 2), ("r_k", 2), ("gn_g", 2), ("gn_b", 2), ("qn_g", 2),
                    ("kvn_g", 1), ("ln1_g", 8), ("ln1_b", 8)):
        PARAMS[name] = (at, n)
        at += n
    return at


NPAR = _params()
EPILOGUE = (3, 6, 9, 12)
NDR, NDC = 15, 31


def chunk_jobs():
    jobs = []
    for d in range(2):
        jobs += [(f"A{d}", "act"), (f"KA{d}", "dve"), (f"N{d}", "dve"), (f"R{d}", "dve"), (f"KR{d}", "dve")]
        jobs += [(f"tok{d}{hp}", "act") for hp in range(2)] + [(f"V{d}", "act")]
    jobs += [(f"AV{d}", "act") for d in range(2)]
    for m in range(1, LEVELS):
        jobs += [(f"G{d}.{m}", "act") for d in range(2)]
        if m == LEVELS - 1:
            jobs += [(f"AZ{d}", "dve") for d in range(2)]
        jobs += [(f"W{d}.{m}", "dve") for d in range(2)]
        if m < LEVELS - 1:
            jobs += [(f"T{d}.{m}", "act") for d in range(2)]
    jobs += [(f"U{d}", "act") for d in range(2)]
    jobs += [(f"Y{d}", "dve") for d in range(2)]
    jobs += [(f"S{d}", "dve") for d in range(2)]
    return jobs


JOBS = chunk_jobs()
NJ = len(JOBS)
JOB = {name: j for j, (name, _) in enumerate(JOBS)}
NBANK = 8
NTH = {name: sum(e == eng for _, e in JOBS[:j + 1]) for j, (name, eng) in enumerate(JOBS)}
EACH = {e: sum(x == e for _, x in JOBS) for e in ("act", "dve")}
LAST_IN_BANK = {b: max(j for j in range(NJ) if j % NBANK == b) for b in range(NBANK)}


class Chain:

    def __init__(self, eng, sem):
        self.eng, self.sem, self.base, self.n = eng, sem, 0, 0

    def add(self, ins):
        ins.then_inc(self.sem, 1)
        self.n += 1

    def wait(self):
        self.eng.wait_ge(self.sem, self.base + self.n)

    def enter(self, i, each):
        self.start, self.each = self.base + self.n, each
        self.base, self.n = self.start + i * each, 0

    def leave(self, times):
        assert self.n == self.each, (self.n, self.each)
        self.base, self.n = self.start + times * self.each, 0


def hybrid_encoder(nc, a, out):
    with ExitStack() as ctx:
        def sb(name, cols, dt=F32):
            return ctx.enter_context(nc.sbuf_tensor(name, [P, cols], dt))

        def sem(name):
            return ctx.enter_context(nc.semaphore(name))

        resid_dram = nc.dram_tensor("resid_spill", (P, NT * D), F32, kind="Internal").ap()

        consts = sb("consts", NC * P)
        par = sb("par", NPAR)
        stats = sb("stats", 320)
        arena_at = (nc.sbuf_base + 31) // 32 * 32
        guard_at = 3 * 8192 + (NM * PW + 7) // 8 * 8 + 2048 + 5120
        arena = sb("arena", guard_at + 2 * T)
        X0, MIX0, PR0 = 0, 8192, 16384
        HT0 = (PR0 + NM * PW + 7) // 8 * 8
        VN0 = HT0 + 8192
        WK0 = VN0 + 2048

        def reg(at, cols):
            return arena[:, at:at + cols]

        def rounded(name, at, cols):
            return nc.alloc_sbuf_tensor_at(name, [P, cols], F32R, offset=arena_at + 4 * at)[:, :]

        q_round = rounded("q_round", guard_at, T)
        k_round = rounded("k_round", guard_at + T, T)

        def cst(c, n=1):
            return consts[:, c * P:(c + n) * P]

        def pcol(name, i=0, rows=slice(0, P)):
            at, n = PARAMS[name]
            assert i < n
            return par[rows, at + i:at + i + 1]

        ident = cst(C_ID)
        resid = reg(X0, 8192).rearrange("p (t c) -> p t c", t=NT)
        mix = reg(MIX0, 8192).rearrange("p (m t) -> p m t", m=8)
        proj = reg(PR0, NM * PW).rearrange("p (m t) -> p m t", m=NM)
        v_na = reg(VN0, 2048).rearrange("p (t c) -> p t c", t=NT)

        NSLOT = 2
        w_raw = [reg(WK0 + s * 1024, 1024) for s in range(NSLOT)]
        w_parts = [[rounded(f"w_in_{part}{b}", (WK0 + 3072, VN0)[b] + 1024 * n, 1024) for n, part in
                    enumerate(("hi", "lo"))] for b in range(2)]
        h_hi = [rounded(f"h_hi{k}", HT0 + 1024 * k, 1024) for k in range(KT)]
        h_lo = [rounded(f"h_lo{k}", MIX0 + 1024 * k, 1024) for k in range(KT)]
        h_tmp = [reg(PR0 + 10 * PW + HALF * j, HALF) for j in range(4)]
        g_row, b_row = reg(PR0 + 12 * PW, 1024), reg(PR0 + 13 * PW, 1024)
        wv_raw = reg(guard_at, 2048).rearrange("p (k c) -> p k c", k=KT)
        wv_parts = [rounded(f"wv_parts{n}", at, 1024) for n, at in
                    enumerate((WK0 + 1024, WK0 + 2048, guard_at, WK0))]

        def wv_part(n, part):
            return wv_parts[n].rearrange("p (k s c) -> p k s c", k=2, s=2)[:, :, part, :]

        v_sh = reg(HT0, 1792).rearrange("p (t c) -> p t c", t=NT - 1)
        na_bias = reg(HT0 + 1792, 2 * NDR * 64).rearrange("p (h r c) -> p h r c", h=2, r=NDR)
        na_at = HT0 + 1792 + 2 * NDR * 64
        q_diag = reg(na_at, 2 * P).rearrange("p (b c) -> p b c", b=2)
        na_s = reg(na_at + 256, 2 * HALF).rearrange("p (b c) -> p b c", b=2)
        na_e = reg(na_at + 1280, 2 * HALF).rearrange("p (b c) -> p b c", b=2)
        na_et = reg(na_at + 2304, 2 * HALF).rearrange("p (b c) -> p b c", b=2)
        na_o = reg(na_at + 3328, 2 * 64).rearrange("p (b c) -> p b c", b=2)
        na_max, na_sum, na_inv = stats[:, 128:130], stats[:, 232:240], stats[:, 240:248]
        NU = 32

        def window(row):
            first = min(max(row - 4, 0), 8)
            return first, first - row + 7

        rope_sb = reg(HT0, T)
        qT = [reg(HT0 + 2048 + 1024 * b, T) for b in range(2)]
        kT = [reg(HT0 + 4096 + 1024 * b, T) for b in range(2)]
        vh = [reg(HT0 + 6144 + 1024 * b, 1024).rearrange("p (t c) -> p t c", t=NT) for b in range(2)]
        NE = 3
        e_ring = [reg(WK0 + 1024 * j, T) for j in range(NE)]
        w_q = [reg(WK0 + 3072 + 256 * b, 256).rearrange("p (k c) -> p k c", k=2) for b in range(2)]
        w_kv = [reg(WK0 + 3584 + P * b, P) for b in range(2)]
        rope_tmp = reg(WK0 + 3840, T)
        max_row = reg(HT0 + 1024, 2 * P).rearrange("p (b c) -> p b c", b=2)
        inv_sum = reg(VN0 + 1024, T)
        last_sums = reg(guard_at, T)
        g_max = stats[:, 136:152].rearrange("p (b c) -> p b c", b=2)
        HEADS = 8
        MLA_SCALE = 96 ** -0.5

        def tok(m):
            return proj[:, m, 1:1 + T]

        def halves(ap):
            return ap.rearrange("p (h c) -> p h c", h=NH)

        sh = reg(X0, 8192).rearrange("p (m t) -> p m t", m=NSHIFT)
        r_sh, k_sh, v_sh2, lora_sh, gate_sh = sh[:, 0:2], sh[:, 2:4], sh[:, 4:6], sh[:, 6], sh[:, 7]
        prod = reg(PR0, 16384).rearrange("p (s q t) -> p s q t", s=4, q=4)
        Rt, Kt, Bt, At = (prod[:, j] for j in range(4))
        gate_o = reg(PR0 + 16384, 2048).rearrange("p (h t) -> p h t", h=2)
        bonus = reg(PR0 + 18432, 2048).rearrange("p (h t) -> p h t", h=2)
        ST0 = PR0 + 20480
        kk = reg(MIX0, 2048).rearrange("p (h t) -> p h t", h=2)
        half = lora_sh
        lora_w = reg(guard_at + 1024, 1024).rearrange("p (j c) -> p j c", j=8)
        key_norm = [reg(MIX0 + 4096 + 1024 * b, T) for b in range(2)]
        gate_w = reg(guard_at + 1024, 256).rearrange("p (j c) -> p j c", j=2)
        y_out = mix[:, 0:2]
        gfac = stats[:, 152:184].rearrange("p (q c) -> p q c", q=4)
        sfac = stats[:, 184:216].rearrange("p (q c) -> p q c", q=4)
        one_less_ka = stats[:, 216:218]
        middle = stats[:, 256:288].rearrange("p (q c) -> p q c", q=4)
        lead = stats[:, 288:304].rearrange("p (q c) -> p q c", q=2)
        PRODS = (3, 6, 8, 10)

        def by_chunk(ap):
            return ap.rearrange("p (c t) -> p c t", t=P)


        at = [ST0, ST0 + 10240]
        free = [(X0, 4096), (X0 + 6144, 2048)]

        def small(cols):
            if at[0] + cols <= at[1]:
                at[0] += cols
                return reg(at[0] - cols, cols)
            at[0], n = free.pop(0)
            at[1] = at[0] + n
            return small(cols)

        Bm, Km, As, Vs, tokm, tokv, Xs, Zs, Us = [], [], [], [], [], [], [], [], []
        for q in range(4):
            Bm.append(small(256).rearrange("p (e t) -> p e t", e=2))
            Km.append(small(256).rearrange("p (e t) -> p e t", e=2))
            As.append(small(P))
            Vs.append(small(P))
            tokm.append(small(2 * P).rearrange("p (s c) -> p s c", s=2))
        for d in range(2):
            Zs.append(small(256).rearrange("p (h c) -> p h c", h=2))
        for d in range(2):
            tokv.append(small(256).rearrange("p (h c) -> p h c", h=2))
            Xs.append(small(256).rearrange("p (h c) -> p h c", h=2))
            Us.append(small(256).rearrange("p (h c) -> p h c", h=2))
        Araw, Alev, Tm, Wm, Gm, KAm, Rm, KRm, AVs = [], [], [], [], [], [], [], [], []
        for d in range(2):
            four = [small(4 * P).rearrange("p (h t) -> p h t", h=4) for _ in range(9)]
            for lst, x in zip((Araw, Tm, Wm, Gm, KAm, Rm, KRm), four):
                lst.append(x)
            Alev.append(four[7:9])
            AVs.append(small(256).rearrange("p (h c) -> p h c", h=2))

        def chunk(tile, d, i):
            return tile[:, :, ds(i * P if d == 0 else i * (-P) + (NT - 1) * P, P)]

        def four_heads(m):
            return m.unsqueeze(1).to_broadcast([P, 4, P])

        def tiles(n, m):
            return n * 1024, m * 1024

        w_out = [reg(at, 1024) for at in (18 * 1024, 19 * 1024, guard_at + 1024, 46 * 1024, 16 * 1024, 17 * 1024,
                                          44 * 1024, 45 * 1024)]
        ln1_rows = [reg(1024 * j, 1024) for j in (20, 21)]
        raw_w = [reg(1024 * j, 1024) for j in (22, 23)]
        h1_hi = [rounded(f"h1_hi{k}", *tiles(24 + k, 1)) for k in range(KT)]
        h1_lo = [rounded(f"h1_lo{k}", *tiles(32 + k, 1)) for k in range(KT)]
        h1_tmp = [[reg(at + HALF * j, HALF) for j in range(4)] for at in (1024 * 42, MIX0)]
        def mixed_bank(t):
            return 0 if t == 2 else 4 + 2 * (t % 2)

        w_hi = [[rounded(f"w_hi{b}{n}", *tiles(40 + 4 * b + 2 * n, 1)) for n in range(2)] for b in range(2)]
        w_lo = [[rounded(f"w_lo{b}{n}", *tiles(41 + 4 * b + 2 * n, 1)) for n in range(2)] for b in range(2)]
        EARLY = 14

        def act_tile(f):
            return reg(1024 * (f + 8 if f < EARLY else f - EARLY), 1024)

        wd_hi = [rounded(f"wd_hi{b}", *tiles(40 + 4 * b, 1)) for b in range(2)]
        wd_lo = [rounded(f"wd_lo{b}", *tiles(41 + 4 * b, 1)) for b in range(2)]
        act_hi = [rounded(f"act_hi{b}", 1024 * (42 + 4 * b), HALF) for b in range(2)]
        act_lo = [rounded(f"act_lo{b}", 1024 * (42 + 4 * b) + HALF, HALF) for b in range(2)]
        resid2 = reg(1024 * 24, 8192).rearrange("p (t c) -> p t c", t=NT)
        ln2_rows = [reg(1024 * j, 1024) for j in (32, 33)]

        psum = ctx.enter_context(nc.psum_tensor("psum", [P, 8, HALF], F32))

        def bank(b, cols=HALF, rows=slice(0, P)):
            return psum[rows, b, 0:cols]

        bn = stats[:, 0:NT * 12].rearrange("p (t s) -> p t s", t=NT)
        mv = stats[:, 96:96 + 2 * NT].rearrange("p (t s) -> p t s", t=NT)
        sd = stats[:, 112:120]
        rs = stats[:, 120:128]

        ident_in, const_in, par_in, rows_in = sem("ident_in"), sem("const_in"), sem("par_in"), sem("rows_in")
        x_in = [sem(f"x_in{t}") for t in range(NT // 2)]
        dve, pool_own = sem("dve_own"), sem("pool_own")
        var_ready, sd_ready, norm_ready = sem("var_ready"), sem("sd_ready"), sem("norm_ready")
        ln_tr, h_tmp_ready, h_hi_ready, h_lo_ready = sem("ln_tr"), [sem("h_tmp_a"), sem("h_tmp_v")], sem("h_hi_ready"), sem("h_lo_ready")
        resid_ready, spilled = sem("resid_ready"), sem("spilled")
        w_in_ready = [sem(f"w_in_ready{s}") for s in range(NSLOT)]
        p_hi_ready, p_lo_ready, wv_hi_ready, wv_lo_ready = (sem("p_hi_ready"), sem("p_lo_ready"), sem("wv_hi_ready"),
                                                            sem("wv_lo_ready"))
        proj_done, evac_a, evac_v = sem("proj_done"), sem("evac_a"), sem("evac_v")
        wv_in, vproj_done, v_evac, v_half, pads, shifted = (sem("wv_in"), sem("vproj_done"), sem("v_evac"), sem("v_half"), sem("pads"),
                                                    sem("shifted"))
        bias_in, bias_ready, qd_zero, q_diag_ready = sem("bias_in"), sem("bias_ready"), sem("qd_zero"), sem("q_diag_ready")
        na_s_done, na_s_biased, na_max_ready, na_e_ready = (sem("na_s_done"), sem("na_s_biased"),
                                                            sem("na_max_ready"), sem("na_e_ready"))
        na_inv_ready, na_tr, na_et_ready, na_pv, na_o_ready, na_ot, na_mixed = (sem("na_inv_ready"), sem("na_tr"), sem("na_et_ready"), sem("na_pv"),
                                                                  sem("na_o_ready"), sem("na_ot"), sem("na_mixed"))
        rope_in, sq_ready, ms_done, ms_ready, ms_sd, lat_ready = (sem("rope_in"), sem("sq_ready"), sem("ms_done"),
                                                                  sem("ms_ready"), sem("ms_sd"), sem("lat_ready"))
        kpe_ready, v_ones, kpe_round = sem("kpe_ready"), sem("v_ones"), sem("kpe_round")
        w_head = [sem(f"w_head{b}") for b in range(2)]
        pr_q, pr_k, pr_v = sem("pr_q"), sem("pr_k"), sem("pr_v")
        q_nope, q_rope, q_rounded, k_nope, k_rounded, v_ready = (sem("q_nope"), sem("q_rope"), sem("q_rounded"),
                                                                 sem("k_nope"), sem("k_rounded"), sem("v_ready"))
        s_done, e_ready, g_done, g_max_ready, pv_done, sums_copied, o_ready, normed = (
            sem("s_done"), sem("e_ready"), sem("g_done"), sem("g_max_ready"), sem("pv_done"),
            sem("sums_copied"), sem("o_ready"), sem("normed"))
        mt_done, mt_copied, max_in = sem("mt_done"), sem("mt_copied"), [sem("max_in0"), sem("max_in1")]
        lora_in, shift_done, lora_act, nrm_sq, nrm_done, nrm_sd, kk_ready, z_done, z_sig = (
            sem("lora_in"), sem("shift_done"), sem("lora_act"), sem("nrm_sq"), sem("nrm_done"), sem("nrm_sd"),
            sem("kk_ready"), sem("z_done"), sem("z_sig"))
        sums_ready, ex_ready, prods_ready, rk_ready, bonus_done, bonus_ready, gate_done, gate_ready = (
            sem("sums_ready"), sem("ex_ready"), sem("prods_ready"), sem("rk_ready"), sem("bonus_done"),
            sem("bonus_ready"), sem("gate_done"), sem("gate_ready"))
        kb_ready, staged, cleared, y_cleared = (sem("kb_ready"), sem("staged"),
                                                                 sem("cleared"), sem("y_cleared"))
        job_done, out_a, out_v, lev_ready, t0_ready = (sem("job_done"), sem("out_a"), sem("out_v"),
                                                                sem("lev_ready"), sem("t0_ready"))
        OUT = {"act": out_a, "dve": out_v}

        def taken(eng, i, name, before=False):
            who = JOBS[JOB[name]][1]
            eng.wait_ge(OUT[who], i * EACH[who] + NTH[name] + (0 if before else EACH[who]))

        def computed(eng, i, name, before=False):
            eng.wait_ge(job_done, i * NJ + JOB[name] + 1 + (0 if before else NJ))

        gn_mean, gn_centred, gn_sq, gn_var, gn_ms, gn_sd, o_rw = (
            sem("gn_mean"), sem("gn_centred"), sem("gn_sq"), sem("gn_var"), sem("gn_ms"), sem("gn_sd"), sem("o_rw"))
        w_out_in, resid_in, rows1_in = [sem(f"w_out_in{k}") for k in range(4)], sem("resid_in"), sem("rows1_in")
        mixed, sum1, var1, sd1, norm1, tr1, h1_hi_ready, h1_tmp_ready, h1_lo_ready, resid1, spilled1 = (
            sem("mixed"), sem("sum1"), sem("var1"), sem("sd1"), sem("norm1"), sem("tr1"), sem("h1_hi_ready"),
            [sem("h1_tmp_a"), sem("h1_tmp_v")], sem("h1_lo_ready"), sem("resid1"), sem("spilled1"))
        raw_in = [sem("gate_in"), sem("up_in")]
        w_hi_ready = [sem("gate_hi_ready"), sem("up_hi_ready")]
        w_lo_ready = [sem("gate_lo_ready"), sem("up_lo_ready")]
        wd_in = [sem(f"wd_in{b}") for b in range(2)]
        ff_done, silu_ready, ff_ready = sem("ff_done"), sem("silu_ready"), sem("ff_ready")
        wd_hi_ready, wd_lo_ready, act_hi_ready, act_lo_ready, resid2_in = (
            sem("wd_hi_ready"), sem("wd_lo_ready"), sem("act_hi_ready"), sem("act_lo_ready"), sem("resid2_in"))
        down_k, down_done, sum2, var2, sd2, y_ready = (sem("down_k"), sem("down_done"), sem("sum2"), sem("var2"),
                                                       sem("sd2"), sem("y_ready"))
        out_sem = sem("out_written")

        block = ctx.enter_context(nc.Block())

        @block.sync
        def _(sp):
            for t in range(NT):
                sp.dma_start(resid[:, t, :], a["x"][t]).then_inc(x_in[t // 2], 16)
                if t == 0:
                    sp.dma_start(ident, a["consts"][:, 0:P]).then_inc(ident_in, 16)
            sp.dma_start(w_raw[0], a["w_in"][0]).then_inc(w_in_ready[0], 16)
            sp.dma_start(consts[:, P:], a["consts"][:, P:]).then_inc(const_in, 16)
            sp.dma_start(w_raw[1], a["w_in"][1]).then_inc(w_in_ready[1], 16)
            sp.dma_start(wv_raw, a["w_nv"]).then_inc(wv_in, 16)
            with sp.Fori(0, NM // 2 - 1) as i:
                for s in range(NSLOT):
                    sp.wait_ge(p_lo_ready, i * 2 + (s + 1))
                    sp.dma_start(w_raw[s], a["w_in"][i * 2 + (s + 2)]).then_inc(w_in_ready[s], 16)
            sp.wait_ge(p_lo_ready, NM - 2)
            sp.dma_start(w_raw[0], a["w_in"][NM - 1]).then_inc(w_in_ready[0], 16)
            sp.wait_ge(wv_lo_ready, 4)
            sp.dma_start(lora_w, a["lora"][:, 0:8, :]).then_inc(lora_in, 16)
            sp.wait_ge(vproj_done, NT)
            sp.dma_start(na_bias, a["rpb"]).then_inc(bias_in, 16)
            for b in range(2):
                sp.dma_start(w_q[b], a["w_q"][b]).then_inc(w_head[b], 16)
                sp.dma_start(w_kv[b], a["w_kv"][b]).then_inc(w_head[b], 16)

            sp.wait_ge(na_pv, NU)
            sp.dma_start(rope_sb, a["rope"]).then_inc(rope_in, 16)

            def head_loads(i, b, weights):
                sp.wait_ge(mt_copied, 2 * i + (b + 1))
                sp.dma_start(qT[b][96:97, :], max_row[0:NT, b, :]).then_inc(max_in[b], 16)
                if weights:
                    sp.wait_ge(pr_v, 2 * i + (b + 1))
                    sp.dma_start(w_q[b], a["w_q"][2 * i + (b + 2)]).then_inc(w_head[b], 16)
                    sp.dma_start(w_kv[b], a["w_kv"][2 * i + (b + 2)]).then_inc(w_head[b], 16)

            with sp.Fori(0, HEADS // 2 - 1) as i:
                for b in range(2):
                    head_loads(i, b, True)
            for b in range(2):
                head_loads(HEADS // 2 - 1, b, False)
            sp.wait_ge(o_ready, HEADS + 1)
            sp.wait_ge(sums_copied, HEADS + 1)
            sp.dma_start(gate_w, a["lora"][:, 8:10, :]).then_inc(lora_in, 16)
            sp.wait_ge(gate_done, 2)
            sp.dma_start(w_out[2], a["w_out"][2]).then_inc(w_out_in[1], 16)
            sp.wait_ge(out_v, (NT + 1) * EACH["dve"])
            for k in (3, 4, 5, 6, 7, 0, 1):
                sp.dma_start(w_out[k], a["w_out"][k]).then_inc(w_out_in[k // 2], 16)
            sp.dma_start(reg(X0, 8192), resid_dram).then_inc(resid_in, 16)
            for n, w in enumerate(("w_gate", "w_up")):
                sp.dma_start(raw_w[n], a[w][0]).then_inc(raw_in[n], 16)
            for b in range(2):
                sp.dma_start(ln1_rows[b], a["rows"][2 + b:3 + b, :].partition_broadcast(P)).then_inc(rows1_in, 16)

            def gate_up_load(j, c):
                for n, w in enumerate(("w_gate", "w_up")):
                    sp.wait_ge(w_lo_ready[n], 2 * j + c)
                    sp.dma_start(raw_w[n], a[w][2 * j + c]).then_inc(raw_in[n], 16)

            gate_up_load(0, 1)
            gate_up_load(0, 2)
            sp.wait_ge(resid1, NT)
            sp.dma_start(resid_dram, reg(X0, 8192)).then_inc(spilled1, 16)
            with sp.Fori(0, (FT - 4) // 2) as j:
                for b in range(2):
                    gate_up_load(j, 3 + b)
            gate_up_load(0, FT - 1)

            for b in range(2):
                sp.wait_ge(w_lo_ready[b], FT)
                sp.dma_start(raw_w[b], a["w_down"][b]).then_inc(wd_in[b], 16)
            def down_load(j, k):
                b = k % 2
                sp.wait_ge(wd_lo_ready, 2 * j + (k - 1))
                sp.dma_start(raw_w[b], a["w_down"][2 * j + k]).then_inc(wd_in[b], 16)

            sp.wait_ge(ff_done, FT)
            with sp.Fori(0, NT) as j:
                for k in (2, 3):
                    down_load(j, k)
                sp.dma_start(arena[:, ds(j * 1024 + 24 * 1024, 1024)],
                             resid_dram[:, ds(j * 1024, 1024)]).then_inc(resid2_in, 16)
            for k in range(2 * NT + 2, FT):
                down_load(0, k)
            for b in range(2):
                sp.dma_start(ln2_rows[b], a["rows"][4 + b:5 + b, :].partition_broadcast(P)).then_inc(resid2_in, 16)
            with sp.Fori(0, FT // 2) as j:
                for b in range(2):
                    sp.wait_ge(wd_lo_ready, 2 * j + (FT - 1 + b))
                    sp.dma_start(raw_w[b], a["w_down"][2 * j + b]).then_inc(wd_in[b], 16)
            for t in range(NT):
                sp.wait_ge(y_ready, t + 1)
                sp.dma_start(out[t], resid2[:, t, :]).then_inc(out_sem, 16)
            sp.wait_ge(out_sem, 16 * NT)

        @block.gpsimd
        def _(pool):
            own = Chain(pool, pool_own)
            pool.dma_start(par[:, :], a["params"]).then_inc(par_in, 16)
            pool.dma_start(g_row, a["rows"][0:1, :].partition_broadcast(P)).then_inc(rows_in, 16)
            pool.dma_start(b_row, a["rows"][1:2, :].partition_broadcast(P)).then_inc(rows_in, 16)
            pool.memset(proj[:, 0:NSHIFT, 0:1], 0.0).then_inc(pads, 1)
            pool.memset(proj[:, 0:NSHIFT, T + 1:T + 2], 0.0).then_inc(pads, 1)
            pool.wait_ge(rows_in, 32)
            pool.wait_ge(h_lo_ready, 2 * KT)
            for t in range(NT):
                pool.wait_ge(ln_tr, 8 * (t // 4 + 1))
                own.add(pool.tensor_tensor(resid[:, t, :], resid[:, t, :], g_row, ALU.mult))
                own.wait()
                pool.tensor_tensor(resid[:, t, :], resid[:, t, :], b_row, ALU.add).then_inc(resid_ready, 1)
            pool.wait_ge(resid_ready, NT)
            pool.dma_start(resid_dram, reg(X0, 8192)).then_inc(spilled, 16)
            pool.wait_ge(vproj_done, NT)
            pool.memset(q_diag[:, :, :], 0.0).then_inc(qd_zero, 1)
            pool.wait_ge(qd_zero, 1)
            pool.wait_ge(evac_a, NM + NSLOT)
            pool.wait_ge(evac_v, NM + NSLOT)
            for n in range(NU):
                row, hp = n // 2, n % 2
                if n >= 2:
                    pool.wait_ge(na_s_done, n - 1)
                for e in range(2):
                    rows = slice(64 * e, 64 * e + 64)
                    pool.tensor_copy(q_diag[rows, n % 2, 64 * e:64 * e + 64],
                                     proj[rows, M_NQ + hp, 1 + 64 * row:1 + 64 * row + 64]).then_inc(q_diag_ready, 1)
            pool.wait_ge(q_diag_ready, 2 * NU)
            pool.wait_ge(na_ot, NU)
            for b in range(2):
                pool.memset(vh[b][:, :, 64:128], 1.0).then_inc(v_ones, 1)
                pool.wait_ge(v_ones, 2 * b + 1)
                pool.memset(kT[b][96:97, :], 1.0).then_inc(v_ones, 1)
                pool.wait_ge(v_ones, 2 * b + 2)
            pool.wait_ge(z_sig, 8)
            pool.wait_ge(kk_ready, 8)
            pool.wait_ge(s_done, 1)
            for q in range(4):
                hp = q % 2
                own.add(pool.tensor_tensor(Bt[:, q], Kt[:, q], kk[:, hp], ALU.mult))
                own.wait()
                own.add(pool.tensor_scalar(Bt[:, q], Bt[:, q], -1.0, None, ALU.mult))
                own.add(pool.tensor_scalar(Kt[:, q], Kt[:, q], pcol("k_a", hp), one_less_ka[:, hp:hp + 1],
                                           ALU.mult, ALU.add))
                own.wait()
                own.add(pool.tensor_tensor(Kt[:, q], Kt[:, q], k_sh[:, hp], ALU.mult))
                own.wait()
                pool.wait_ge(ex_ready, 4 * (q + 1))
                own.add(pool.tensor_tensor(Bt[:, q], Bt[:, q], half, ALU.mult))
                own.wait()
                pool.tensor_tensor(Kt[:, q], Kt[:, q], half, ALU.mult).then_inc(kb_ready, 1)
            pool.wait_ge(o_ready, HEADS + 1)
            pool.wait_ge(sums_copied, HEADS + 1)
            n = 0
            for ap in [x for q in range(4) for x in (Bm[q], Km[q])]:
                if n:
                    pool.wait_ge(cleared, n)
                pool.memset(ap, 0.0).then_inc(cleared, 1)
                n += 1
            pool.wait_ge(cleared, n)

            with pool.Fori(0, NT) as i:
                own.enter(i, 2)
                computed(pool, i, "V1", before=True)
                n = 0

                def stage(dst, src):
                    nonlocal n
                    pool.tensor_copy(dst, src).then_inc(staged, 1)
                    n += 1
                    pool.wait_ge(staged, i * 24 + n)

                for q in range(4):
                    d, hp = q // 2, q % 2
                    for e in range(2):
                        rows = slice(64 * e, 64 * e + 64)
                        stage(Bm[q][rows, e:e + 1, :], chunk(Bt[:, q:q + 1], d, i)[rows])
                        stage(Km[q][rows, e:e + 1, :], chunk(Kt[:, q:q + 1], d, i)[rows])
                    stage(Vs[q].unsqueeze(1), chunk(v_sh2[:, hp:hp + 1], d, i))
                computed(pool, i, "AZ1", before=True)
                for q in range(4):
                    pool.wait_ge(prods_ready, PRODS[q])
                    stage(As[q].unsqueeze(1), chunk(At[:, q:q + 1], q // 2, i))
                for d in range(2):
                    taken(pool, i, f"A{d}")
                    own.add(pool.tensor_tensor(Tm[d], Araw[d], four_heads(cst(C_LV if d == 0 else C_LVT)), ALU.mult))
                    own.wait()
                    pool.tensor_tensor(Tm[d], Tm[d], four_heads(ident), ALU.add).then_inc(t0_ready, 1)
                for m in range(1, LEVELS):
                    for d in range(2):
                        if m >= 3:
                            computed(pool, i, f"G{d}.{m - 2}")
                        pool.tensor_tensor(Alev[d][m % 2], Araw[d], four_heads(cst((C_LV if d == 0 else C_LVT) + m)),
                                           ALU.mult).then_inc(lev_ready, 1)
                own.leave(NT)
            pool.wait_ge(rows1_in, 32)
            for t in range(NT):
                pool.wait_ge(tr1, 8 * (t // 4 + 1))
                own.add(pool.tensor_tensor(resid[:, t, :], resid[:, t, :], ln1_rows[0], ALU.mult))
                own.wait()
                pool.tensor_tensor(resid[:, t, :], resid[:, t, :], ln1_rows[1], ALU.add).then_inc(resid1, 1)

        @block.scalar
        def _(act):
            for hf in range(2):
                act.wait_ge(var_ready, hf + 1)
                act.activation(sd[:, 4 * hf:4 * hf + 4], mv[:, 4 * hf:4 * hf + 4, 1], ACT.Sqrt).then_inc(sd_ready, 1)
            act.wait_ge(par_in, 16)

            def p_hi(j):
                act.wait_ge(w_in_ready[j % 2], 16 * (j // 2) + 16)
                act.activation(w_parts[j % 2][0], w_raw[j % 2], ACT.Copy).then_inc(p_hi_ready, 1)

            def wv_hi(n):
                act.activation(wv_part(n, 0), wv_raw[:, 2 * n:2 * n + 2, :], ACT.Copy).then_inc(wv_hi_ready, 1)

            for hf in range(2):
                def copy_even(k):
                    act.wait_ge(ln_tr, 8 * hf + k + 1)
                    if 8 * hf + k >= 4:
                        act.wait_ge(h_lo_ready, 8 * hf + k - 3)
                    act.activation(h_tmp[k % 4], bank(k), ACT.Identity,
                                   bias=pcol("ln_in_b", k), scale=pcol("ln_in_g", k)).then_inc(h_tmp_ready[0], 1)

                copy_even(0)
                for k in range(KT):
                    act.wait_ge(h_tmp_ready[k % 2], 4 * hf + k // 2 + 1)
                    act.activation(h_hi[k][:, hf * HALF:(hf + 1) * HALF], h_tmp[k % 4], ACT.Copy).then_inc(h_hi_ready, 1)
                    if k % 2 == 0 and k + 2 < KT:
                        copy_even(k + 2)
                p_hi(hf)
            act.sem_inc(evac_a, NSLOT)
            for j in range(NM):
                act.wait_ge(proj_done, j + 1 + NSLOT)
                act.activation(proj[:, j, 1:1 + HALF], bank(2 * (j % 2)), ACT.Copy).then_inc(evac_a, 1)
                if j + 2 < NM:
                    p_hi(j + 2)
                if j == NM - 2:
                    act.wait_ge(wv_in, 16)
                    act.wait_ge(p_lo_ready, NM)
                    for n in range(4):
                        if n == 2:
                            act.wait_ge(wv_lo_ready, 2)
                        wv_hi(n)
            for t in range(NT):
                act.wait_ge(vproj_done, t + 1)
                act.activation(v_na[:, t, :], bank(t, 256), ACT.Copy).then_inc(v_half, 1)
            act.wait_ge(shift_done, 2)
            act.activation(lora_sh[0:64], lora_sh[0:64], ACT.Tanh).then_inc(lora_act, 1)
            act.activation(gate_sh[0:64], gate_sh[0:64], ACT.Sigmoid).then_inc(lora_act, 1)
            act.wait_ge(shift_done, NSHIFT)
            for hp in range(2):
                act.activation(key_norm[hp], k_sh[:, hp], ACT.Square, scale=pcol("k_k", hp)).then_inc(nrm_sq, 1)
            act.wait_ge(evac_v, NM + NSLOT)
            for j, m in enumerate((M_CQ, M_CQ + 1, M_CKV)):
                act.activation(e_ring[j], tok(m), ACT.Square).then_inc(sq_ready, 1)
            for hp in range(2):
                act.wait_ge(nrm_done, hp + 1)
                act.activation(halves(key_norm[hp]), psum[:, 2 * hp:2 * hp + 2, :], ACT.Sqrt).then_inc(nrm_sd, 1)
            for j in range(8):
                act.wait_ge(z_done, j + 1)
                b = 2 * (j % 2) + 4
                act.activation(halves((Rt if j < 4 else Kt)[:, j % 4]), psum[:, b:b + 2, :], ACT.Sigmoid,
                               bias=pcol("w0" if j < 4 else "a0", j % 4)).then_inc(z_sig, 1)
            for j in range(2):
                act.wait_ge(ms_ready, j + 1)
                act.activation(e_ring[j], e_ring[j], ACT.Sqrt).then_inc(ms_sd, 1)
            for n in range(NU + 5):
                if n < NU:
                    b = n % 2
                    act.wait_ge(na_max_ready, n + 1)
                    if n >= 2:
                        act.wait_ge(na_tr, n - 1)
                    if n >= 8:
                        act.wait_ge(na_inv_ready, n - 7)
                    act.activation(na_e[:, b], na_s[:, b], ACT.Exp, bias=na_max[:, b:b + 1],
                                   accum_out=na_sum[:, n % 8:n % 8 + 1]).then_inc(na_e_ready, 1)
                if 2 <= n <= NU + 1:
                    u = n - 2
                    act.wait_ge(na_tr, u + 1)
                    if u >= 2:
                        act.wait_ge(na_pv, u - 1)
                    act.activation(na_et[:, u % 2], bank(2 + u % 2), ACT.Copy).then_inc(na_et_ready, 1)
                if 4 <= n <= NU + 3:
                    u = n - 4
                    b = u % 2
                    act.wait_ge(na_inv_ready, u + 1)
                    act.wait_ge(na_pv, u + 1)
                    if u >= 2:
                        act.wait_ge(na_ot, u - 1)
                    for e in range(2):
                        rows = slice(64 * e, 64 * e + 64)
                        act.activation(na_o[rows, b], psum[rows, 4 + b, 64 * e:64 * e + 64], ACT.Copy,
                                       scale=na_inv[rows, u % 8:u % 8 + 1]).then_inc(na_o_ready, 1)
                if n >= 5:
                    u = n - 5
                    row, hp, b = u // 2, u % 2, u % 2
                    act.wait_ge(na_ot, u + 1)
                    for e in range(2):
                        act.activation(mix[64 * e:64 * e + 64, 2 + hp, 64 * row:64 * row + 64],
                                       psum[0:64, 6 + b, 64 * e:64 * e + 64], ACT.Copy).then_inc(na_mixed, 1)
            act.wait_ge(kpe_ready, 4)
            act.activation(k_round[64:96, :], kT[0][64:96, :], ACT.Copy).then_inc(kpe_round, 1)

            def head_copies(i, b):
                act.wait_ge(pr_q, 2 * i + (b + 1))
                act.activation(halves(qT[b][0:64, :]), psum[0:64, 0:2, :], ACT.Copy).then_inc(q_nope, 1)
                act.wait_ge(pr_k, 2 * i + (b + 1))
                act.activation(halves(kT[b][0:64, :]), psum[0:64, 2:4, :], ACT.Copy).then_inc(k_nope, 1)
                act.activation(halves(k_round[0:64, :]), psum[0:64, 2:4, :], ACT.Copy).then_inc(k_rounded, 1)
                act.wait_ge(pr_v, 2 * i + (b + 1))
                act.activation(vh[b][:, :, 0:64], psum[:, 4:6, :].rearrange("p h (t c) -> p (h t) c", c=P)[:, :, 64:128],
                               ACT.Copy).then_inc(v_ready, 1)
                act.wait_ge(q_rope, 2 * i + (b + 1))
                act.wait_ge(q_nope, 2 * i + (b + 1))
                act.activation(q_round[0:96, :], qT[b][0:96, :], ACT.Copy).then_inc(q_rounded, 1)

            def copy_max(i, b):
                act.wait_ge(mt_done, 2 * i + (b + 1))
                act.activation(max_row[0:NT, b, :], psum[0:NT, 4, 0:P], ACT.Copy).then_inc(mt_copied, 1)

            def decays(q):
                act.wait_ge(sums_ready, q + 1)
                if q:
                    act.wait_ge(kb_ready, q)
                sums = by_chunk(Rt[:, q])

                def exp(dst, src, sign):
                    act.activation(dst, src, ACT.Exp, scale=sign * DECAY_SCALE).then_inc(ex_ready, 1)

                exp(gfac[:, q], sums[:, :, P - 1], -1)
                if q < 2:
                    exp(lead[:, q], middle[:, q], -1)
                    exp(half, Rt[:, q], 1)
                else:
                    exp(by_chunk(half)[:, :, 0], middle[:, q], -1)
                    exp(by_chunk(half)[:, :, 1:P], sums[:, :, 0:P - 1], -1)
                act.wait_ge(ex_ready, 4 * q + 3)
                exp(Rt[:, q], Rt[:, q], -1 if q < 2 else 1)

            def head_exps(i, b, ahead, ahead2, with_decays=False, last=False):
                for kt in range(NT):
                    if with_decays and kt in (2, 6):
                        decays(2 * b + kt // 4)
                    act.wait_ge(s_done, 16 * i + (8 * b + kt + 1))
                    if kt >= NE:
                        act.wait_ge(pv_done, 16 * i + (8 * b + kt - NE + 1))
                    act.activation(halves(e_ring[(kt) % NE]), psum[:, 2 * (kt % 2):2 * (kt % 2) + 2, :], ACT.Exp,
                                   scale=MLA_SCALE).then_inc(e_ready, 1)
                if last and ahead:
                    copy_max(i, 1)
                act.wait_ge(pv_done, 16 * i + (8 * b + 8))
                if not last:
                    act.wait_ge(normed, 4 * i + 4)
                act.activation(halves((last_sums if last else inv_sum)[64 * b:64 * b + 64, :]), psum[64:128, 6:8, :],
                               ACT.Copy).then_inc(sums_copied, 1)
                if ahead and not last:
                    copy_max(i + (b + 1) // 2, (b + 1) % 2)
                if ahead2:
                    head_copies(i + 1, b)

            act.sem_inc(sums_copied, 1)
            head_copies(0, 0)
            copy_max(0, 0)
            head_copies(0, 1)
            for b in range(2):
                head_exps(0, b, True, True, with_decays=True)
            with act.Fori(0, HEADS // 2 - 2) as j:
                for b in range(2):
                    head_exps(j + 1, b, True, True)
            for b in range(2):
                head_exps(HEADS // 2 - 1, b, b == 0, False, last=True)
            for hp in range(2):
                act.wait_ge(gate_done, hp + 1)
                act.activation(halves(gate_o[:, hp]), psum[:, 4 + 2 * hp:6 + 2 * hp, :], ACT.Copy).then_inc(gate_ready, 1)
            act.sem_inc(out_a, EACH["act"])
            with act.Fori(0, NT) as i:
                for name, who in JOBS:
                    if who != "act":
                        continue
                    bk = JOB[name] % NBANK
                    computed(act, i, name)
                    kind = name.rstrip("0123456789.")
                    if kind == "A":
                        d = int(name[1])
                        computed(act, i, f"G{d}.{LEVELS - 1}", before=True)
                        ins = act.activation(Araw[d].rearrange("p h t -> p (h t)"), bank(bk), ACT.Copy)
                    elif kind == "tok":
                        q = 2 * int(name[3]) + int(name[4])
                        for e in range(2):
                            ins = act.activation(tokm[q][:, :, 64 * e:64 * e + 64],
                                                 bank(bk).rearrange("p (s x) -> p s x", s=2)[:, :, 192 * e:192 * e + 64],
                                                 ACT.Copy)
                    elif kind == "V":
                        ins = act.activation(tokv[int(name[1])].rearrange("p h c -> p (h c)"), bank(bk, 256), ACT.Copy)
                    elif kind in ("G", "T"):
                        d = int(name[1])
                        ins = act.activation((Gm if kind == "G" else Tm)[d].rearrange("p h t -> p (h t)"), bank(bk),
                                             ACT.Copy)
                    else:
                        d = int(name[-1])
                        dst = AVs[d] if kind == "AV" else Us[d]
                        if kind == "AV":
                            taken(act, i, f"AZ{d}", before=True)
                        for e in range(2):
                            ins = act.activation(dst[:, :, 64 * e:64 * e + 64],
                                                 bank(bk).rearrange("p (h x) -> p h x", h=2)[:, :, 192 * e:192 * e + 64],
                                                 ACT.Copy)
                    ins.then_inc(out_a, 1)
            for hp in range(2):
                act.wait_ge(gn_centred, hp + 1)
                act.activation(Bt[:, hp], At[:, hp], ACT.Square).then_inc(gn_sq, 1)
            for hp in range(2):
                act.wait_ge(gn_ms, hp + 1)
                act.activation(Bt[:, hp], Bt[:, hp], ACT.Sqrt).then_inc(gn_sd, 1)
            def weights_hi(n, b, j, c):
                act.wait_ge(raw_in[n], 32 * j + 16 * (c + 1))
                act.activation(w_hi[b][n], raw_w[n], ACT.Copy).then_inc(w_hi_ready[n], 1)

            for hf in range(2):
                act.wait_ge(var1, hf + 1)
                act.activation(sd[:, 4 * hf:4 * hf + 4], mv[:, 4 * hf:4 * hf + 4, 1], ACT.Sqrt).then_inc(sd1, 1)
                if hf == 0:
                    weights_hi(0, 0, 0, 0)
                else:
                    act.wait_ge(mixed, NT)
                def copy_even(k):
                    act.wait_ge(tr1, 8 * hf + k + 1)
                    if 8 * hf + k >= 4:
                        act.wait_ge(h1_lo_ready, 8 * hf + k - 3)
                    act.activation(h1_tmp[hf][k % 4], bank(4 * hf + k % 4), ACT.Identity,
                                   bias=pcol("ln1_b", k), scale=pcol("ln1_g", k)).then_inc(h1_tmp_ready[0], 1)

                copy_even(0)
                for k in range(KT):
                    act.wait_ge(h1_tmp_ready[k % 2], 4 * hf + k // 2 + 1)
                    act.activation(h1_hi[k][:, hf * HALF:(hf + 1) * HALF], h1_tmp[hf][k % 4], ACT.Copy).then_inc(h1_hi_ready, 1)
                    if k % 2 == 0 and k + 2 < KT:
                        copy_even(k + 2)
                if hf == 0:
                    act.wait_ge(h1_lo_ready, KT)
                    weights_hi(1, 0, 0, 0)
            act.wait_ge(mixed, NT)
            for n in range(2):
                weights_hi(n, 1, 0, 1)

            def silu(dst, b, j, c):
                act.wait_ge(ff_done, 2 * j + (c + 1))
                act.activation(halves(dst), psum[:, 4 * b:4 * b + 2, :], ACT.Silu).then_inc(silu_ready, 1)

            for first, at0, times in ((0, 8192, EARLY // 2), (EARLY, 0, (FT - EARLY) // 2 - 1)):
                if first:
                    act.wait_ge(spilled1, 16)
                with act.Fori(0, times) as j:
                    for b in range(2):
                        silu(arena[:, ds(j * 2048 + (at0 + 1024 * b), 1024)], b, j, first + b)
                        for n in range(2):
                            weights_hi(n, b, j, first + b + 2)

            def down_hi(quad, b, j, k, src):
                act.wait_ge(wd_in[b], 16 * j + 16 * (quad * (FT // 2) + k // 2 + 1))
                act.activation(wd_hi[b], raw_w[b], ACT.Copy).then_inc(wd_hi_ready, 1)
                act.activation(act_hi[b], src, ACT.Copy).then_inc(act_hi_ready, 1)

            def four_tiles(f, quad):
                return act_tile(f)[:, HALF * quad:HALF * quad + HALF]

            silu(act_tile(FT - 2), 0, 0, FT - 2)
            act.wait_ge(ff_ready, 1)
            down_hi(0, 0, 0, 0, four_tiles(0, 0))
            silu(act_tile(FT - 1), 1, 0, FT - 1)
            down_hi(0, 1, 0, 1, four_tiles(1, 0))
            for quad in range(2):
                for k in range(FT):
                    if not quad and k < 2:
                        continue
                    if k >= 2:
                        act.wait_ge(down_k, quad * (FT - 1) + k - 1)
                    elif k == 0:
                        act.wait_ge(down_k, FT - 1)
                    else:
                        act.wait_ge(down_done, 4)
                    act.wait_ge(ff_ready, k + 1)
                    down_hi(quad, k % 2, 0, k, four_tiles(k, quad))
                    if quad and k in EPILOGUE:
                        t = EPILOGUE.index(k)
                        act.wait_ge(var2, t + 1)
                        act.activation(sd[:, t:t + 1], mv[:, t, 1:2], ACT.Sqrt).then_inc(sd2, 1)
            for t in range(4, NT):
                act.wait_ge(var2, t + 1)
                act.activation(sd[:, t:t + 1], mv[:, t, 1:2], ACT.Sqrt).then_inc(sd2, 1)

        @block.vector
        def _(v):
            own = Chain(v, dve)
            for hf in range(2):
                for t in range(4 * hf, 4 * hf + 4):
                    v.wait_ge(x_in[t // 2], 32)
                    for j in range(2):
                        own.add(v.bn_stats(bn[:, t, 6 * j:6 * j + 6], resid[:, t, j * HALF:(j + 1) * HALF]))
                    own.wait()
                    own.add(v.bn_aggr(mv[:, t, :], bn[:, t, :]))
                own.wait()
                v.tensor_scalar(mv[:, 4 * hf:4 * hf + 4, 1], mv[:, 4 * hf:4 * hf + 4, 1], LN_EPS, None,
                                ALU.add).then_inc(var_ready, 1)
            for hf in range(2):
                v.wait_ge(sd_ready, hf + 1)
                own.add(v.reciprocal(rs[:, 4 * hf:4 * hf + 4], sd[:, 4 * hf:4 * hf + 4]))
                own.wait()
                for t in range(4 * hf, 4 * hf + 4):
                    v.tensor_scalar(resid[:, t, :], resid[:, t, :], mv[:, t, 0:1], rs[:, t:t + 1],
                                    ALU.subtract, ALU.mult).then_inc(norm_ready, 1)
            v.wait_ge(par_in, 16)

            def p_lo(j):
                v.wait_ge(p_hi_ready, j + 1)
                v.tensor_tensor(w_parts[j % 2][1], w_raw[j % 2], w_parts[j % 2][0], ALU.subtract).then_inc(p_lo_ready, 1)

            for hf in range(2):
                for k in range(0, KT, 2):
                    v.wait_ge(ln_tr, 8 * hf + k + 2)
                    v.tensor_scalar(h_tmp[k % 4 + 1], bank(k + 1), pcol("ln_in_g", k + 1), pcol("ln_in_b", k + 1),
                                    ALU.mult, ALU.add).then_inc(h_tmp_ready[1], 1)
                    for j in range(k, k + 2):
                        v.wait_ge(h_hi_ready, 8 * hf + j + 1)
                        v.tensor_tensor(h_lo[j][:, hf * HALF:(hf + 1) * HALF], h_tmp[j % 4],
                                        h_hi[j][:, hf * HALF:(hf + 1) * HALF], ALU.subtract).then_inc(h_lo_ready, 1)
                p_lo(hf)
            v.sem_inc(evac_v, NSLOT)
            keep_c = stats[:, 224:224 + NSHIFT]
            own.add(v.tensor_tensor(keep_c, par[:, PARAMS["mu0"][0]:PARAMS["mu0"][0] + NSHIFT],
                                    par[:, PARAMS["mu1"][0]:PARAMS["mu1"][0] + NSHIFT], ALU.add))
            own.wait()
            own.add(v.tensor_scalar(keep_c, keep_c, -1.0, 1.0, ALU.mult, ALU.add))
            ka = PARAMS["k_a"][0]
            own.add(v.tensor_scalar(one_less_ka, par[:, ka:ka + 2], -1.0, 1.0, ALU.mult, ALU.add))
            own.wait()
            behind = NM - NSHIFT
            for j in range(NM):
                v.wait_ge(proj_done, j + 1 + NSLOT)
                v.tensor_copy(proj[:, j, 1 + HALF:1 + T], bank(2 * (j % 2) + 1)).then_inc(evac_v, 1)
                if j + 2 < NM:
                    p_lo(j + 2)
                if j >= behind:
                    m = (M_LORA, M_GATE, 2, 3, 0, 1, 4, 5)[j - behind]
                    if j == behind:
                        v.wait_ge(pads, 2)
                        v.wait_ge(spilled, 16)
                    v.wait_ge(evac_a, m + 1 + NSLOT)
                    v.wait_ge(evac_v, m + 1 + NSLOT)
                    own.add(v.tensor_scalar(sh[:, m], tok(m), keep_c[:, m:m + 1], None, ALU.mult))
                    own.wait()
                    own.add(v.scalar_tensor_tensor(out=sh[:, m], in0=proj[:, m, 0:T], scalar=pcol("mu0", m),
                                                   in1=sh[:, m], op0=ALU.mult, op1=ALU.add))
                    own.wait()
                    v.scalar_tensor_tensor(out=sh[:, m], in0=proj[:, m, 2:T + 2], scalar=pcol("mu1", m),
                                           in1=sh[:, m], op0=ALU.mult, op1=ALU.add).then_inc(shift_done, 1)
                if j == NM - 2:
                    for n in range(4):
                        v.wait_ge(wv_hi_ready, n + 1)
                        v.tensor_tensor(wv_part(n, 1), wv_raw[:, 2 * n:2 * n + 2, :], wv_part(n, 0),
                                        ALU.subtract).then_inc(wv_lo_ready, 1)
            for t in range(NT):
                v.wait_ge(v_half, t + 1)
                v.tensor_tensor(v_na[:, t, :], psum[:, t, 256:512], v_na[:, t, :], ALU.add).then_inc(v_evac, 1)
            v.wait_ge(vproj_done, NT)
            v.wait_ge(v_evac, NT)
            v.tensor_copy(v_sh[0:64], v_na[64:128, 0:NT - 1, :]).then_inc(shifted, 1)
            v.tensor_copy(v_sh[64:128], v_na[0:64, 1:NT, :]).then_inc(shifted, 1)
            v.wait_ge(bias_in, 16)
            v.wait_ge(const_in, 16)
            flat = na_bias.rearrange("p h r c -> p (h r) c")
            keep = cst(C_COLS)[:, 0:64].unsqueeze(1).to_broadcast([P, 2 * NDR, 64])
            fill = cst(C_COLS)[:, 64:128].unsqueeze(1).to_broadcast([P, 2 * NDR, 64])
            own.add(v.tensor_tensor(flat, flat, keep, ALU.mult))
            own.wait()
            v.tensor_tensor(flat, flat, fill, ALU.add).then_inc(bias_ready, 1)
            v.wait_ge(bias_ready, 1)
            for j, n in enumerate((2, 1)):
                v.wait_ge(ms_done, 2 * j + 2)
                v.tensor_scalar(halves(e_ring[j]), psum[:, 2 * j:2 * j + 2, :], 1.0 / (n * P), RMS_EPS,
                                ALU.mult, ALU.add).then_inc(ms_ready, 1)

            def unit_keys(hp, c):
                cols = slice(256 * c, 256 * c + 256)
                if c == 0:
                    v.wait_ge(nrm_sd, hp + 1)
                own.add(v.tensor_scalar(key_norm[hp][:, cols], key_norm[hp][:, cols], 1e-12, None, ALU.max))
                own.wait()
                own.add(v.reciprocal(key_norm[hp][:, cols], key_norm[hp][:, cols]))
                own.wait()
                v.scalar_tensor_tensor(out=kk[:, hp, cols], in0=k_sh[:, hp, cols], scalar=pcol("k_k", hp),
                                       in1=key_norm[hp][:, cols], op0=ALU.mult, op1=ALU.mult).then_inc(kk_ready, 1)

            def unit_latents(j, c):
                cols = slice(256 * c, 256 * c + 256)
                if c == 0:
                    v.wait_ge(ms_sd, j + 1)
                own.add(v.reciprocal(e_ring[j][:, cols], e_ring[j][:, cols]))
                own.wait()
                for k in range(2 - j):
                    lat = tok((M_CQ, M_CKV)[j] + k)[:, cols]
                    v.scalar_tensor_tensor(out=lat, in0=lat, scalar=pcol(("qn_g", "kvn_g")[j], k),
                                           in1=e_ring[j][:, cols], op0=ALU.mult, op1=ALU.mult).then_inc(lat_ready, 1)

            for n in range(NU + 3):
                if n < NU and n % 2:
                    (unit_keys if n < 16 else unit_latents)(n // 8 % 2, n // 2 % 4)
                if n < NU:
                    row, hp, b = n // 2, n % 2, n % 2
                    dr = window(row)[1]
                    v.wait_ge(na_s_done, n + 1)
                    if n >= 2:
                        v.wait_ge(na_e_ready, n - 1)
                    v.scalar_tensor_tensor(out=na_s[:, b], in0=bank(b), scalar=0.125,
                                           in1=na_bias[:, hp, dr:dr + 8, :].rearrange("p r c -> p (r c)"),
                                           op0=ALU.mult, op1=ALU.add).then_inc(na_s_biased, 1)
                    v.wait_ge(na_s_biased, n + 1)
                    v.tensor_reduce(na_max[:, b:b + 1], na_s[:, b], AX.X, ALU.max,
                                    negate=True).then_inc(na_max_ready, 1)
                if n >= 3:
                    u = n - 3
                    v.wait_ge(na_e_ready, u + 1)
                    v.reciprocal(na_inv[:, u % 8:u % 8 + 1], na_sum[:, u % 8:u % 8 + 1]).then_inc(na_inv_ready, 1)
            v.wait_ge(rope_in, 16)
            v.tensor_tensor(kT[0][64:96, :], gate_sh[64:96], rope_sb[64:96, :], ALU.mult).then_inc(kpe_ready, 1)
            v.tensor_tensor(rope_tmp[64:96, :], gate_sh[96:128], rope_sb[96:128, :], ALU.mult).then_inc(kpe_ready, 1)
            v.wait_ge(kpe_ready, 2)
            v.tensor_tensor(kT[0][64:96, :], kT[0][64:96, :], rope_tmp[64:96, :], ALU.add).then_inc(kpe_ready, 1)
            v.wait_ge(kpe_ready, 3)
            v.tensor_copy(kT[1][64:96, :], kT[0][64:96, :]).then_inc(kpe_ready, 1)

            def head_rope(i, b):
                v.wait_ge(pr_q, 2 * i + (b + 1))
                own.add(v.tensor_tensor(halves(qT[b][64:96, :]), psum[64:96, 0:2, :], halves(rope_sb[64:96, :]),
                                        ALU.mult))
                own.add(v.tensor_tensor(halves(rope_tmp[64:96, :]), psum[96:128, 0:2, :], halves(rope_sb[96:128, :]),
                                        ALU.mult))
                own.wait()
                v.tensor_tensor(qT[b][64:96, :], qT[b][64:96, :], rope_tmp[64:96, :], ALU.add).then_inc(q_rope, 1)

            def sums(q):
                x = by_chunk(Rt[:, q])
                for c in range(NT):
                    own.add(v.tensor_tensor_scan(x[:, c], cst(C_ONES), x[:, c], 0.0, ALU.mult, ALU.add))
                own.wait()
                own.add(v.tensor_scalar(middle[:, q], x[:, :, P - 1], -0.5, None, ALU.mult))
                own.wait()
                v.tensor_tensor(x, x, middle[:, q].unsqueeze(2).to_broadcast([P, NT, P]), ALU.add).then_inc(sums_ready, 1)

            def head_max(i, b, before=None, pairs=1):
                for t in range(NT):
                    if before is not None and not isinstance(before, tuple) and t % 2:
                        divide(before, t // 2)
                    if isinstance(before, tuple) and t % 4 == 0:
                        sums(before[t // 4])
                    v.wait_ge(g_done, 16 * i + (8 * b + t + 1))
                    g_banks = slice(4 + 2 * (t % pairs), 6 + 2 * (t % pairs))
                    v.tensor_reduce(g_max[:, b, t:t + 1], psum[:, g_banks, :], AX.XY, ALU.max,
                                    negate=True).then_inc(g_max_ready, 1)

            def head_out(i, b):
                v.wait_ge(pv_done, 16 * i + (8 * b + 8))
                v.tensor_copy(mix[64 * b:64 * b + 64, ds(4 + i, 1), :].rearrange("p o (h c) -> p (o h) c", h=NH),
                              psum[0:64, 6:8, :]).then_inc(o_ready, 1)

            def divide(i, c):
                cols = slice(256 * c, 256 * c + 256)
                if c == 0:
                    v.wait_ge(sums_copied, 2 * i + 3)
                    v.wait_ge(o_ready, 2 * i + 3)
                own.add(v.reciprocal(inv_sum[:, cols], inv_sum[:, cols]))
                own.wait()
                out = mix[:, ds(4 + i, 1), cols].rearrange("p o c -> p (o c)")
                v.tensor_tensor(out, out, inv_sum[:, cols], ALU.mult).then_inc(normed, 1)

            def pair(i, before):
                for b in range(2):
                    head_max(i + (b + 1) // 2, (b + 1) % 2,
                             (2 * b, 2 * b + 1) if before is None else None if b else before)
                    head_out(i, b)
                    head_rope(i + 1, b)

            v.sem_inc(o_ready, 1)
            v.sem_inc(normed, 4)
            head_rope(0, 0)
            head_max(0, 0, pairs=2)
            head_rope(0, 1)
            pair(0, None)
            with v.Fori(0, HEADS // 2 - 2) as j:
                own.enter(j, 8)
                pair(j + 1, j)
                own.leave(HEADS // 2 - 2)
            head_max(HEADS // 2 - 1, 1, HEADS // 2 - 2)
            for b in range(2):
                head_out(HEADS // 2 - 1, b)
            v.wait_ge(sums_copied, HEADS + 1)
            v.wait_ge(kb_ready, 4)
            v.wait_ge(ex_ready, 16)
            for q in range(4):
                hp = q % 2
                if q < 2:
                    v.tensor_tensor(by_chunk(At[:, q])[:, :, 0], by_chunk(kk[:, hp])[:, :, 0], lead[:, q],
                                    ALU.mult).then_inc(prods_ready, 1)
                    v.tensor_tensor(by_chunk(At[:, q])[:, :, 1:P], by_chunk(Rt[:, q])[:, :, 0:P - 1],
                                    by_chunk(kk[:, hp])[:, :, 1:P], ALU.mult).then_inc(prods_ready, 1)
                else:
                    v.tensor_tensor(At[:, q], Rt[:, q], kk[:, hp], ALU.mult).then_inc(prods_ready, 1)
                v.wait_ge(prods_ready, PRODS[q] - 1)
                v.tensor_tensor(Rt[:, q], Rt[:, q], r_sh[:, hp], ALU.mult).then_inc(prods_ready, 1)
                if q < 2:
                    v.wait_ge(prods_ready, PRODS[q])
                    v.scalar_tensor_tensor(out=bonus[:, hp], in0=Kt[:, q], scalar=pcol("r_k", hp), in1=Rt[:, q],
                                           op0=ALU.mult, op1=ALU.mult).then_inc(rk_ready, 1)
            v.sem_inc(out_v, EACH["dve"])
            for hp in range(2):
                v.wait_ge(bonus_done, hp + 1)
                v.tensor_tensor(halves(bonus[:, hp]), psum[:, 4 + 2 * hp:6 + 2 * hp, :], halves(v_sh2[:, hp]),
                                ALU.mult).then_inc(bonus_ready, 1)
            own.add(v.memset(sfac, 1.0))
            own.wait()
            own.add(v.tensor_tensor(sfac[:, 0:2, 0:NT - 1], gfac[:, 0:2, 0:NT - 1], gfac[:, 0:2, 1:NT], ALU.mult))
            for j in range(NT - 1):
                own.add(v.tensor_tensor(sfac[:, 2:4, j:j + 1], gfac[:, 2:4, NT - 1 - j:NT - j],
                                        gfac[:, 2:4, NT - 2 - j:NT - 1 - j], ALU.mult))
            own.wait()
            for ap in (y_out, *Zs):
                v.memset(ap, 0.0).then_inc(y_cleared, 1)
            v.wait_ge(y_cleared, 3)
            with v.Fori(0, NT) as i:
                own.enter(i, 9)
                own.add(v.reciprocal(last_sums[:, ds(i * P, P)], last_sums[:, ds(i * P, P)]))
                own.wait()
                last_out = mix[:, 7, ds(i * P, P)]
                v.tensor_tensor(last_out, last_out, last_sums[:, ds(i * P, P)], ALU.mult).then_inc(normed, 1)
                for name, who in JOBS:
                    if who != "dve":
                        continue
                    bk = JOB[name] % NBANK
                    computed(v, i, name)
                    kind = name.split(".")[0][:-1]
                    d = int(name.split(".")[0][-1])
                    ps4 = bank(bk).rearrange("p (h t) -> p h t", h=4)
                    if kind == "N":
                        own.add(v.tensor_tensor(Wm[d], ps4, four_heads(cst(C_LVT if d == 0 else C_LV)), ALU.mult))
                        own.wait()
                        ins = v.tensor_tensor(Wm[d], Wm[d], four_heads(ident), ALU.add)
                    elif kind in ("KA", "R", "KR"):
                        dst = {"KA": KAm, "R": Rm, "KR": KRm}[kind][d]
                        mask = (C_BEFORE_F, C_BEFORE_B)[d] if kind == "KA" else (C_REC_F, C_REC_B)[d]
                        ins = v.tensor_tensor(dst, ps4, four_heads(cst(mask)), ALU.mult)
                    elif kind == "W":
                        ins = v.tensor_tensor(Wm[d], ps4, Wm[d], ALU.add)
                    elif kind == "AZ":
                        taken(v, i, f"AV{d}")
                        ins = v.tensor_tensor(Xs[d].rearrange("p h c -> p (h c)"), bank(bk, 256),
                                              AVs[d].rearrange("p h c -> p (h c)"), ALU.add)
                    elif kind == "S":
                        for e in range(2):
                            rows = slice(64 * e, 64 * e + 64)
                            own.add(v.tensor_tensor(Zs[d][rows, :, 64 * e:64 * e + 64],
                                                    bank(bk, 256, rows).rearrange("p (h c) -> p h c", h=2)[:, :, 64 * e:64 * e + 64],
                                                    Zs[d][rows, :, 64 * e:64 * e + 64], ALU.add))
                        own.wait()
                        for hp in range(2):
                            ins = v.tensor_scalar(Zs[d][:, hp, :], Zs[d][:, hp, :], sfac[:, 2 * d + hp, ds(i, 1)], None,
                                                  ALU.mult)
                            if hp == 0:
                                own.add(ins)
                    else:
                        ychunk = chunk(y_out, d, i)
                        ins = v.tensor_tensor(ychunk, bank(bk, 256).rearrange("p (h t) -> p h t", h=2), ychunk, ALU.add)
                    ins.then_inc(out_v, 1)
                own.leave(NT)
            for hp in range(2):
                v.wait_ge(gn_mean, hp + 1)
                v.scalar_tensor_tensor(out=halves(At[:, hp]), in0=psum[:, 2 * hp:2 * hp + 2, :], scalar=-1.0 / 64,
                                       in1=halves(y_out[:, hp]), op0=ALU.mult, op1=ALU.add).then_inc(gn_centred, 1)
            for hp in range(2):
                v.wait_ge(gn_var, hp + 1)
                v.tensor_scalar(halves(Bt[:, hp]), psum[:, 2 * hp:2 * hp + 2, :], 1.0 / 64, GN_EPS,
                                ALU.mult, ALU.add).then_inc(gn_ms, 1)
            for hp in range(2):
                v.wait_ge(gn_sd, hp + 1)
                own.add(v.reciprocal(Bt[:, hp], Bt[:, hp]))
                own.wait()
                own.add(v.tensor_tensor(At[:, hp], At[:, hp], Bt[:, hp], ALU.mult))
                own.wait()
                own.add(v.tensor_scalar(At[:, hp], At[:, hp], pcol("gn_g", hp), pcol("gn_b", hp), ALU.mult, ALU.add))
                own.wait()
                own.add(v.tensor_tensor(At[:, hp], At[:, hp], bonus[:, hp], ALU.add))
                own.wait()
                v.tensor_tensor(y_out[:, hp], At[:, hp], gate_o[:, hp], ALU.mult).then_inc(o_rw, 1)

            def variances(t):
                for j in range(2):
                    own.add(v.bn_stats(bn[:, t, 6 * j:6 * j + 6], resid[:, t, j * HALF:(j + 1) * HALF]))
                own.wait()
                own.add(v.bn_aggr(mv[:, t, :], bn[:, t, :]))
                own.wait()

            def normalise1(hf):
                v.wait_ge(sd1, hf + 1)
                own.add(v.reciprocal(rs[:, 4 * hf:4 * hf + 4], sd[:, 4 * hf:4 * hf + 4]))
                own.wait()
                for t in range(4 * hf, 4 * hf + 4):
                    v.tensor_scalar(resid[:, t, :], resid[:, t, :], mv[:, t, 0:1], rs[:, t:t + 1],
                                    ALU.subtract, ALU.mult).then_inc(norm1, 1)

            def transposed1(hf):
                for k in range(0, KT, 2):
                    v.wait_ge(tr1, 8 * hf + k + 2)
                    v.tensor_scalar(h1_tmp[hf][k % 4 + 1], bank(4 * hf + k % 4 + 1), pcol("ln1_g", k + 1), pcol("ln1_b", k + 1),
                                    ALU.mult, ALU.add).then_inc(h1_tmp_ready[1], 1)
                    for j in range(k, k + 2):
                        v.wait_ge(h1_hi_ready, 8 * hf + j + 1)
                        v.tensor_tensor(h1_lo[j][:, hf * HALF:(hf + 1) * HALF], h1_tmp[hf][j % 4],
                                        h1_hi[j][:, hf * HALF:(hf + 1) * HALF], ALU.subtract).then_inc(h1_lo_ready, 1)

            def weights_lo(n, b, j, c):
                v.wait_ge(w_hi_ready[n], 2 * j + (c + 1))
                v.tensor_tensor(w_lo[b][n], raw_w[n], w_hi[b][n], ALU.subtract).then_inc(w_lo_ready[n], 1)

            v.wait_ge(resid_in, 16)
            for t in range(NT):
                b = mixed_bank(t)
                if t == 6:
                    transposed1(0)
                    weights_lo(1, 0, 0, 0)
                v.wait_ge(mixed, t + 1)
                v.scalar_tensor_tensor(out=halves(resid[:, t]), in0=halves(resid[:, t]), scalar=ALPHA,
                                       in1=psum[:, b:b + 2, :], op0=ALU.mult, op1=ALU.add).then_inc(sum1, 1)
                v.wait_ge(sum1, t + 1)
                variances(t)
                if t % 4 == 3:
                    hf = t // 4
                    v.tensor_scalar(mv[:, 4 * hf:4 * hf + 4, 1], mv[:, 4 * hf:4 * hf + 4, 1], LN_EPS, None,
                                    ALU.add).then_inc(var1, 1)
                    normalise1(hf)
                    if hf == 0:
                        weights_lo(0, 0, 0, 0)
            transposed1(1)
            for n in range(2):
                weights_lo(n, 1, 0, 1)

            def times_up(dst, b, j, c):
                v.wait_ge(silu_ready, 2 * j + (c + 1))
                v.tensor_tensor(halves(dst), psum[:, 4 * b + 2:4 * b + 4, :], halves(dst), ALU.mult).then_inc(ff_ready, 1)

            for first, at0, times in ((0, 8192, EARLY // 2), (EARLY, 0, (FT - EARLY) // 2 - 1)):
                with v.Fori(0, times) as j:
                    for b in range(2):
                        times_up(arena[:, ds(j * 2048 + (at0 + 1024 * b), 1024)], b, j, first + b)
                        for n in range(2):
                            weights_lo(n, b, j, first + b + 2)

            def down_lo(quad, k):
                b, n = k % 2, quad * FT + k
                v.wait_ge(wd_hi_ready, n + 1)
                v.tensor_tensor(wd_lo[b], raw_w[b], wd_hi[b], ALU.subtract).then_inc(wd_lo_ready, 1)
                v.wait_ge(act_hi_ready, n + 1)
                v.tensor_tensor(act_lo[b], act_tile(k)[:, HALF * quad:HALF * quad + HALF], act_hi[b],
                                ALU.subtract).then_inc(act_lo_ready, 1)

            def sum_down(t):
                b = 2 * (t % 4)
                v.wait_ge(down_done, t + 1)
                v.scalar_tensor_tensor(out=halves(resid2[:, t]), in0=halves(resid2[:, t]), scalar=ALPHA,
                                       in1=psum[:, b:b + 2, :], op0=ALU.mult, op1=ALU.add).then_inc(sum2, 1)

            def finish(t):
                v.wait_ge(sum2, t + 1)
                for j in range(2):
                    own.add(v.bn_stats(bn[:, t, 6 * j:6 * j + 6], resid2[:, t, j * HALF:(j + 1) * HALF]))
                own.wait()
                own.add(v.bn_aggr(mv[:, t, :], bn[:, t, :]))
                own.wait()
                v.tensor_scalar(mv[:, t, 1:2], mv[:, t, 1:2], LN_EPS, None, ALU.add).then_inc(var2, 1)
                own.add(v.scalar_tensor_tensor(out=resid2[:, t], in0=resid2[:, t], scalar=mv[:, t, 0:1],
                                               in1=ln2_rows[0], op0=ALU.subtract, op1=ALU.mult))
                v.wait_ge(sd2, t + 1)
                own.add(v.reciprocal(rs[:, t:t + 1], sd[:, t:t + 1]))
                own.wait()
                v.scalar_tensor_tensor(out=resid2[:, t], in0=resid2[:, t], scalar=rs[:, t:t + 1],
                                       in1=ln2_rows[1], op0=ALU.mult, op1=ALU.add).then_inc(y_ready, 1)

            times_up(act_tile(FT - 2), 0, 0, FT - 2)
            down_lo(0, 0)
            times_up(act_tile(FT - 1), 1, 0, FT - 1)
            for k in range(1, FT):
                down_lo(0, k)
            down_lo(1, 0)
            v.wait_ge(resid2_in, 16 * (NT + 2))
            for t in range(4):
                sum_down(t)
            for k in range(1, FT):
                down_lo(1, k)
                if k in EPILOGUE:
                    finish(EPILOGUE.index(k))
            for t in range(4, NT):
                sum_down(t)
                finish(t)

        @block.tensor
        def _(pe):
            pe.wait_ge(ident_in, 16)
            for hf in range(2):
                pe.wait_ge(norm_ready, 4 * hf + 4)
                for k in range(KT):
                    if hf:
                        pe.wait_ge(h_tmp_ready[k % 2], k // 2 + 1)
                    for t in range(4):
                        mm = pe.transpose(psum[:, k, t * P:(t + 1) * P],
                                          resid[:, 4 * hf + t, k * P:(k + 1) * P], ident)
                    mm.then_inc(ln_tr, 1)
            pe.sem_inc(proj_done, NSLOT)

            def project(b, i, j, ahead=False):
                pe.wait_ge(p_lo_ready, 2 * i + (j + 1))
                pe.wait_ge(evac_a, 2 * i + (j + 1))
                pe.wait_ge(evac_v, 2 * i + (j + 1))
                w_hi_b, w_lo_b = w_parts[b]
                for hf in range(NH):
                    cols = slice(hf * HALF, (hf + 1) * HALF)
                    if ahead:
                        pe.wait_ge(h_lo_ready, 8 * hf + 8)
                    for k in range(KT):
                        for n, (w, x) in enumerate(((w_hi_b, h_hi), (w_hi_b, h_lo), (w_lo_b, h_hi))):
                            mm = pe.matmul(bank(2 * b + hf), w[:, P * k:P * k + P], x[k][:, cols],
                                           start=(k == 0 and n == 0), stop=(k == KT - 1 and n == 2))
                mm.then_inc(proj_done, 1)

            project(0, 0, 0, ahead=True)
            project(1, 0, 1)
            with pe.Fori(0, NM // 2 - 1) as i:
                for b in range(2):
                    project(b, i, b + 2)
            project(0, 0, NM - 1)
            pe.wait_ge(wv_lo_ready, 4)
            pe.wait_ge(evac_a, NM + NSLOT)
            pe.wait_ge(evac_v, NM + NSLOT)
            for t in range(NT):
                for k in range(KT):
                    for n, x in enumerate((h_hi, h_lo)):
                        mm = pe.matmul(bank(t), x[k][:, t * P:(t + 1) * P],
                                       wv_parts[k // 2][:, HALF * (k % 2):HALF * (k % 2) + HALF],
                                       start=(k == 0 and n == 0), stop=(k == KT - 1 and n == 1))
                mm.then_inc(vproj_done, 1)
            def over_channels(b, weights, rhs):
                for hf in range(NH):
                    mm = pe.matmul(bank(b + hf), weights, rhs[:, hf * HALF:(hf + 1) * HALF], start=True, stop=True)
                return mm

            def low_rank(j):
                if j >= 2:
                    pe.wait_ge(z_sig, j - 1)
                over_channels(2 * (j % 2) + 4, lora_w[:, j, :], lora_sh).then_inc(z_done, 1)

            pe.wait_ge(v_evac, NT)
            pe.wait_ge(const_in, 16)
            pe.wait_ge(lora_in, 16)
            pe.wait_ge(lora_act, 2)
            for j in range(2):
                low_rank(j)
            for hp in range(2):
                pe.wait_ge(nrm_sq, hp + 1)
                over_channels(2 * hp, cst(C_HEADS), key_norm[hp]).then_inc(nrm_done, 1)
            pe.wait_ge(sq_ready, 3)
            for j, tiles_of in enumerate(((0, 1), (2,))):
                pe.wait_ge(nrm_sd, j + 1)
                for hf in range(NH):
                    for n, m in enumerate(tiles_of):
                        mm = pe.matmul(bank(2 * j + hf), cst(C_ONES), e_ring[m][:, hf * HALF:(hf + 1) * HALF],
                                       start=(n == 0), stop=(n == len(tiles_of) - 1))
                    mm.then_inc(ms_done, 1)
            for j in range(2, 8):
                low_rank(j)
            pe.wait_ge(shifted, 2)
            pe.wait_ge(ms_ready, 2)
            pe.wait_ge(z_sig, 8)
            for n in range(NU + 5):
                if n < NU:
                    row, hp, b = n // 2, n % 2, n % 2
                    first = window(row)[0]
                    pe.wait_ge(q_diag_ready, 2 * (n + 1))
                    if n >= 2:
                        pe.wait_ge(na_s_biased, n - 1)
                    pe.matmul(bank(b), q_diag[:, b, :], proj[:, M_NK + hp, 1 + 64 * first:1 + 64 * first + HALF],
                              start=True, stop=True).then_inc(na_s_done, 1)
                if 2 <= n <= NU + 1:
                    u = n - 2
                    pe.wait_ge(na_e_ready, u + 1)
                    if u >= 2:
                        pe.wait_ge(na_et_ready, u - 1)
                    for j in range(4):
                        mm = pe.transpose(psum[:, 2 + u % 2, j * P:(j + 1) * P], na_e[:, u % 2, j * P:(j + 1) * P], ident)
                    mm.then_inc(na_tr, 1)
                if 3 <= n <= NU + 2:
                    u = n - 3
                    row, hp, b = u // 2, u % 2, u % 2
                    first = window(row)[0]
                    vals = v_sh if first % 2 else v_na
                    pe.wait_ge(na_et_ready, u + 1)
                    if u >= 2:
                        pe.wait_ge(na_o_ready, 2 * (u - 1))
                    for j in range(4):
                        mm = pe.matmul(bank(4 + b, P), na_et[:, b, j * P:(j + 1) * P],
                                       vals[:, first // 2 + j, hp * P:(hp + 1) * P], start=(j == 0), stop=(j == 3))
                    mm.then_inc(na_pv, 1)
                if n >= 5:
                    u = n - 5
                    pe.wait_ge(na_o_ready, 2 * (u + 1))
                    if u >= 2:
                        pe.wait_ge(na_mixed, 2 * (u - 1))
                    pe.transpose(psum[0:64, 6 + u % 2, 0:P], na_o[:, u % 2], ident).then_inc(na_ot, 1)
            pe.wait_ge(na_mixed, 2 * NU)
            pe.wait_ge(lat_ready, 12)

            def head_project(i, b):
                pe.wait_ge(w_head[b], 32 * i + 32)
                for hf in range(NH):
                    for k in range(2):
                        mm = pe.matmul(bank(hf), w_q[b][:, k, :], tok(M_CQ + k)[:, hf * HALF:(hf + 1) * HALF],
                                       start=(k == 0), stop=(k == 1))
                mm.then_inc(pr_q, 1)
                for hf in range(NH):
                    mm = pe.matmul(bank(2 + hf, rows=slice(0, 64)), w_kv[b][:, 0:64],
                                   tok(M_CKV)[:, hf * HALF:(hf + 1) * HALF], start=True, stop=True)
                mm.then_inc(pr_k, 1)

            def head_values(i, b):
                for t in range(NT):
                    mm = pe.matmul(psum[:, 4 + t // 4, t % 4 * P:t % 4 * P + P], tok(M_CKV)[:, t * P:(t + 1) * P],
                                   w_kv[b], start=True, stop=True)
                mm.then_inc(pr_v, 1)

            def guard(i, b, t, pairs=1):
                if t == 0:
                    pe.wait_ge(q_rounded, 2 * i + (b + 1))
                    pe.wait_ge(k_rounded, 2 * i + (b + 1))
                    pe.wait_ge(v_ready, 2 * i + (b + 1))
                elif t >= pairs:
                    pe.wait_ge(g_max_ready, 16 * i + (8 * b + t + 1 - pairs))
                for hf in range(NH):
                    mm = pe.matmul(bank(4 + 2 * (t % pairs) + hf), q_round[0:96, t * P:(t + 1) * P],
                                   k_round[0:96, hf * HALF:(hf + 1) * HALF], start=True, stop=True)
                mm.then_inc(g_done, 1)

            def turn_max(i, b):
                pe.wait_ge(g_max_ready, 16 * i + (8 * b + 8))
                pe.transpose(psum[0:NT, 4, 0:P], g_max[:, b, :], ident).then_inc(mt_done, 1)

            def scores(i, b, kt, ahead):
                if kt == 0:
                    pe.wait_ge(max_in[b], 16 * i + 16)
                    for copied in (q_nope, q_rope, k_nope):
                        pe.wait_ge(copied, 2 * i + (b + 1 + (ahead and copied is not k_nope)))
                if kt == 1:
                    pe.wait_ge(k_rounded, 2 * i + (b + 1 + ahead))
                if kt >= 2:
                    pe.wait_ge(e_ready, 16 * i + (8 * b + kt - 1))
                for hf in range(NH):
                    mm = pe.matmul(bank(2 * (kt % 2) + hf), kT[b][0:97, kt * P:(kt + 1) * P],
                                   qT[b][0:97, hf * HALF:(hf + 1) * HALF], start=True, stop=True)
                mm.then_inc(s_done, 1)

            def values(i, b, kt):
                pe.wait_ge(e_ready, 16 * i + (8 * b + kt + 1))
                if kt == 0:
                    pe.wait_ge(o_ready, 2 * i + (b + 1))
                    pe.wait_ge(sums_copied, 2 * i + (b + 1))
                for hf in range(NH):
                    mm = pe.matmul(bank(6 + hf), vh[b][:, kt, :], e_ring[kt % NE][:, hf * HALF:(hf + 1) * HALF],
                                   start=(kt == 0), stop=(kt == NT - 1))
                mm.then_inc(pv_done, 1)

            def head(i, b, ahead, ahead2):
                nxt = (i + (b + 1) // 2, (b + 1) % 2)
                for kt in range(NT):
                    scores(i, b, kt, ahead)
                    if kt:
                        values(i, b, kt - 1)
                        if ahead:
                            guard(*nxt, kt - 1)
                values(i, b, NT - 1)
                if ahead:
                    guard(*nxt, NT - 1)
                if ahead:
                    turn_max(*nxt)
                if ahead2:
                    head_project(i + 1, b)
                    pe.wait_ge(mt_copied, 2 * nxt[0] + (nxt[1] + 1))
                    head_values(i + 1, b)

            head_project(0, 0)
            head_values(0, 0)
            pe.wait_ge(kpe_round, 1)
            pe.wait_ge(v_ones, 4)
            for t in range(NT):
                guard(0, 0, t, pairs=2)
            turn_max(0, 0)
            pe.wait_ge(q_rounded, 1)
            head_project(0, 1)
            pe.wait_ge(mt_copied, 1)
            head_values(0, 1)
            with pe.Fori(0, HEADS // 2 - 1) as i:
                for b in range(2):
                    head(i, b, True, True)
            for b in range(2):
                head(HEADS // 2 - 1, b, b == 0, False)
            pe.sem_inc(job_done, NJ)
            pe.wait_ge(o_ready, HEADS + 1)
            pe.wait_ge(sums_copied, HEADS + 1)
            pe.wait_ge(lora_in, 32)
            for hp in range(2):
                over_channels(4 + 2 * hp, gate_w[:, hp, :], gate_sh).then_inc(gate_done, 1)
            for hp in range(2):
                pe.wait_ge(rk_ready, hp + 1)
                pe.wait_ge(gate_ready, hp + 1)
                over_channels(4 + 2 * hp, cst(C_HEADS), bonus[:, hp]).then_inc(bonus_done, 1)
            with pe.Fori(0, NT) as i:
                for j, (name, who) in enumerate(JOBS):
                    bk = j % NBANK
                    last = JOBS[j - NBANK if j >= NBANK else LAST_IN_BANK[bk]][0]
                    taken(pe, i, last, before=j < NBANK)
                    if j == 4:
                        pe.wait_ge(bonus_ready, 2)
                    if name == "AZ0":
                        pe.wait_ge(y_cleared, 3)
                    kind = name.split(".")[0].rstrip("01")
                    d = int(name.split(".")[0][len(kind)])
                    m = int(name.split(".")[1]) if "." in name else 0
                    if kind in ("A", "N", "KA", "R", "KR") and name == "A0":
                        pe.wait_ge(staged, i * 24 + 24)
                        pe.wait_ge(cleared, 8)
                    if kind == "A":
                        for hp in range(2):
                            mm = pe.matmul(psum[:, bk, 256 * hp:256 * hp + 256], As[2 * d + hp],
                                           Bm[2 * d + hp].rearrange("p e t -> p (e t)"), start=True, stop=True)
                    elif kind in ("N", "T"):
                        taken(pe, i, f"A{d}" if kind == "N" else f"W{d}.{m}")
                        for h in range(4):
                            mm = pe.transpose(psum[:, bk, P * h:P * h + P], (Araw if kind == "N" else Wm)[d][:, h, :], ident)
                    elif kind in ("KA", "R", "KR"):
                        for h in range(4):
                            q, e = 2 * d + h // 2, h % 2
                            lhs = (Km if kind[0] == "K" else Bm)[q][:, e, :]
                            rhs = As[q] if kind == "KA" else chunk(Rt[:, q:q + 1], d, i)[:, 0]
                            mm = pe.matmul(psum[:, bk, P * h:P * h + P], lhs, rhs, start=True, stop=True)
                    elif kind == "tok":
                        q = 2 * d + int(name[-1])
                        for n, src in enumerate((Bm[q], Km[q])):
                            for e in range(2):
                                mm = pe.transpose(psum[:, bk, 256 * n + P * e:256 * n + P * e + P], src[:, e, :], ident)
                    elif kind == "V":
                        for hp in range(2):
                            mm = pe.transpose(psum[:, bk, P * hp:P * hp + P], Vs[2 * d + hp], ident)
                    elif kind == "AV":
                        taken(pe, i, f"KA{d}")
                        taken(pe, i, f"V{d}")
                        for h in range(4):
                            mm = pe.matmul(psum[:, bk, P * h:P * h + P], KAm[d][:, h, :],
                                           tokv[d][:, h // 2, :], start=True, stop=True)
                    elif kind == "G":
                        pe.wait_ge(lev_ready, i * 2 * (LEVELS - 1) + 2 * (m - 1) + d + 1)
                        taken(pe, i, f"N{d}" if m == 1 else f"W{d}.{m - 1}")
                        for h in range(4):
                            mm = pe.matmul(psum[:, bk, P * h:P * h + P], Alev[d][m % 2][:, h, :], Wm[d][:, h, :],
                                           start=True, stop=True)
                    elif kind == "W":
                        taken(pe, i, f"G{d}.{m}")
                        if m == 1:
                            pe.wait_ge(t0_ready, i * 2 + d + 1)
                        else:
                            taken(pe, i, f"T{d}.{m - 1}")
                        for h in range(4):
                            mm = pe.matmul(psum[:, bk, P * h:P * h + P], Tm[d][:, h, :], Gm[d][:, h, :],
                                           start=True, stop=True)
                    elif kind == "AZ":
                        taken(pe, i, f"S{d}", before=True)
                        for hp in range(2):
                            mm = pe.matmul(psum[:, bk, P * hp:P * hp + P], As[2 * d + hp], Zs[d][:, hp, :],
                                           start=True, stop=True)
                    elif kind == "U":
                        taken(pe, i, f"W{d}.{LEVELS - 1}")
                        taken(pe, i, f"AZ{d}")
                        for h in range(4):
                            mm = pe.matmul(psum[:, bk, P * h:P * h + P], Wm[d][:, h, :], Xs[d][:, h // 2, :],
                                           start=True, stop=True)
                    elif kind == "Y":
                        taken(pe, i, f"U{d}")
                        taken(pe, i, f"KR{d}")
                        for hp in range(2):
                            q = 2 * d + hp
                            cols = slice(P * hp, P * hp + P)
                            pe.matmul(psum[:, bk, cols], Zs[d][:, hp, :], chunk(Rt[:, q:q + 1], d, i)[:, 0],
                                      start=True, stop=False, skip_group_check=True)
                            for e in range(2):
                                rows, own_half = slice(64 * e, 64 * e + 64), slice(64 * e, 64 * e + 64)
                                pe.matmul(psum[rows, bk, cols], Us[d][:, hp, own_half], Rm[d][:, 2 * hp + e, :],
                                          start=False, stop=False, skip_group_check=True)
                                mm = pe.matmul(psum[rows, bk, cols], tokv[d][:, hp, own_half], KRm[d][:, 2 * hp + e, :],
                                               start=False, stop=True, skip_group_check=True)
                    else:
                        for hp in range(2):
                            q = 2 * d + hp
                            cols = slice(P * hp, P * hp + P)
                            pe.matmul(psum[:, bk, cols], tokm[q][:, 0, :], Us[d][:, hp, :], start=True, stop=False)
                            mm = pe.matmul(psum[:, bk, cols], tokm[q][:, 1, :], tokv[d][:, hp, :], start=False, stop=True)
                    mm.then_inc(job_done, 1)
            taken(pe, NT - 1, "S1")
            for hp in range(2):
                over_channels(2 * hp, cst(C_HEADS), y_out[:, hp]).then_inc(gn_mean, 1)

            def mix_out(t, hf, ks):
                for k in ks:
                    pe.wait_ge(w_out_in[k // 2], 32)
                    mm = pe.matmul(bank(mixed_bank(t) + hf), mix[:, k, t * P:(t + 1) * P],
                                   w_out[k][:, hf * HALF:(hf + 1) * HALF], start=(k == 2), stop=(k == 1))
                return mm

            mix_out(0, 0, range(2, 8))
            for hp in range(2):
                pe.wait_ge(gn_sq, hp + 1)
                over_channels(2 * hp, cst(C_HEADS), Bt[:, hp]).then_inc(gn_var, 1)
            mix_out(0, 1, range(2, 8))
            for hf in range(NH):
                mix_out(1, hf, range(2, 8))
            pe.wait_ge(gn_ms, 2)
            for hf in range(NH):
                mix_out(2, hf, range(2, 8))
            pe.wait_ge(o_rw, 2)

            def turn1(hf):
                pe.wait_ge(norm1, 4 * hf + 4)
                for k in range(KT):
                    n = 8 * hf + k
                    if k >= 4:
                        pe.wait_ge(h1_tmp_ready[k % 2], (n - 4) // 2 + 1)
                    for t in range(4):
                        mm = pe.transpose(psum[:, 4 * hf + k % 4, t * P:(t + 1) * P],
                                          resid[:, 4 * hf + t, k * P:(k + 1) * P], ident)
                    mm.then_inc(tr1, 1)

            for t in range(3):
                for hf in range(NH):
                    mm = mix_out(t, hf, range(2))
                mm.then_inc(mixed, 1)
            for t in range(3, NT):
                pe.wait_ge(sum1, t - 1)
                if t == 6:
                    turn1(0)
                for hf in range(NH):
                    mm = mix_out(t, hf, (*range(2, 8), 0, 1))
                mm.then_inc(mixed, 1)

            def gate_up(b, j, c, hfs=range(NH)):
                for n in range(2):
                    pe.wait_ge(w_lo_ready[n], 2 * j + (c + 1))
                    for hf in hfs:
                        cols = slice(hf * HALF, (hf + 1) * HALF)
                        for k in range(KT):
                            for i, (w, x) in enumerate(((w_hi, h1_hi), (w_hi, h1_lo), (w_lo, h1_hi))):
                                mm = pe.matmul(bank(4 * b + 2 * n + hf), w[b][n][:, P * k:P * k + P], x[k][:, cols],
                                               start=(k == 0 and i == 0), stop=(k == KT - 1 and i == 2))
                if 1 in hfs:
                    mm.then_inc(ff_done, 1)

            pe.wait_ge(h1_lo_ready, KT)
            gate_up(0, 0, 0, hfs=(0,))
            turn1(1)
            pe.wait_ge(h1_lo_ready, 2 * KT)
            gate_up(0, 0, 0, hfs=(1,))
            gate_up(1, 0, 1)
            with pe.Fori(0, FT // 2 - 1) as j:
                for b in range(2):
                    pe.wait_ge(ff_ready, 2 * j + (b + 1))
                    gate_up(b, j, b + 2)

            def down(b, j, n, ends=None, free=None):
                pe.wait_ge(wd_lo_ready, 2 * j + (n + 1))
                pe.wait_ge(act_lo_ready, 2 * j + (n + 1))
                for t in range(4):
                    if free:
                        pe.wait_ge(free, t + 1 if free is sum2 else FT - 1 + t // 2)
                    for hf in range(NH):
                        for i, (x, w) in enumerate(((act_hi, wd_hi), (act_hi, wd_lo), (act_lo, wd_hi))):
                            mm = pe.matmul(bank(2 * t + hf), x[b][:, t * P:(t + 1) * P],
                                           w[b][:, hf * HALF:(hf + 1) * HALF],
                                           start=(free is not None and i == 0), stop=(ends is not None and i == 2))
                    if ends:
                        mm.then_inc(down_done, 1)
                if not ends:
                    mm.then_inc(down_k, 1)

            for quad in range(2):
                down(0, 0, quad * FT, free=sum2 if quad else ff_ready)
                down(1, 0, quad * FT + 1)
                with pe.Fori(0, FT // 2 - 2) as j:
                    for b in range(2):
                        down(b, j, quad * FT + 2 + b)
                if quad == 0:
                    down(0, 0, FT - 2)
                    down(1, 0, FT - 1, ends=down_done)
            pe.wait_ge(wd_lo_ready, 2 * FT)
            pe.wait_ge(act_lo_ready, 2 * FT)
            for t in range(4):
                for b in range(2):
                    for hf in range(NH):
                        for i, (x, w) in enumerate(((act_hi, wd_hi), (act_hi, wd_lo), (act_lo, wd_hi))):
                            mm = pe.matmul(bank(2 * t + hf), x[b][:, t * P:(t + 1) * P],
                                           w[b][:, hf * HALF:(hf + 1) * HALF], start=False, stop=(b == 1 and i == 2))
                mm.then_inc(down_done, 1)


def tables():
    import numpy as np
    r = np.arange(P)
    row, col = r[:, None], r[None, :]
    c = np.zeros((P, NC, P), np.float32)
    c[:, C_ID] = np.eye(P)
    c[:, C_HEADS] = row // 64 == col // 64
    c[:, C_ONES] = 1
    c[:, C_BEFORE_F] = row < col
    c[:, C_BEFORE_B] = row > col
    c[:, C_REC_F] = row <= col
    c[:, C_REC_B] = row > col
    for m in range(LEVELS):
        b = 1 << m
        lv = (row // (2 * b) == col // (2 * b)) & (row // b % 2 == 1) & (col // b % 2 == 0)
        c[:, C_LV + m] = lv
        c[:, C_LVT + m] = lv.T
    j, kc = np.arange(P) % 64, np.arange(64)
    start = np.clip(j - 8, 0, 48)[:, None]
    ok = (kc >= start) & (kc < start + 16)
    c[:, C_COLS, 0:64] = ok
    c[:, C_COLS, 64:128] = np.where(ok, 0, -1e30)
    return c.reshape(P, NC * P)


def rope():
    import numpy as np
    inv = np.power(np.float32(10000.0), -np.arange(0, 32, 2, dtype=np.float32) / np.float32(32)).astype(np.float32)
    ang = (np.arange(T, dtype=np.float32)[:, None] * inv[None, :]).astype(np.float32)
    cos, sin = np.cos(ang).T, np.sin(ang).T
    one = np.concatenate([np.concatenate([cos, cos]), np.concatenate([-sin, sin])], 0)
    return np.ascontiguousarray(np.concatenate([one, one], 0), np.float32)


def layout(x, ln_in_g, ln_in_b, w_in, rw_mu, rw_w0, rw_w2, rw_a0, rw_a2, rw_g2, rw_k_k, rw_k_a,
           rw_r_k, rw_gn_g, rw_gn_b, na_rpb, mla_q_norm_g, mla_w_q_b, mla_kv_norm_g, mla_w_kv_b,
           w_out, ln1_g, ln1_b, w_ffn_gate, w_ffn_up, w_ffn_down, ln2_g, ln2_b):
    import numpy as np
    f = np.float32
    z = {}
    z["x"] = np.asarray(x).reshape(NT, P, D)
    w = np.asarray(w_in)[0]
    pe0 = 960 + 768 + 384
    cols = list(range(0, 960)) + list(range(pe0, pe0 + 32)) + list(range(pe0 + 16, pe0 + 32)) + \
        list(range(pe0, pe0 + 16)) + list(range(960, 960 + 512)) + list(range(1728, 1728 + 384))
    assert len(cols) == NM * P
    z["w_in"] = w[:, cols].reshape(KT, P, NM, P).transpose(2, 1, 0, 3)
    z["w_nv"] = w[:, 960 + 512:1728].reshape(KT, P, 256).transpose(1, 0, 2)
    par = np.zeros((P, NPAR), f)

    def put(name, v):
        at, n = PARAMS[name]
        par[:, at:at + n] = np.asarray(v).reshape(n, P).T

    put("ln_in_g", ln_in_g)
    put("ln_in_b", ln_in_b)
    mu = np.zeros((2, NSHIFT * P), f)
    mu[:, :960] = np.asarray(rw_mu)[0]
    put("mu0", mu[0])
    put("mu1", mu[1])
    for name, v in (("w0", rw_w0), ("a0", rw_a0), ("k_k", rw_k_k), ("k_a", rw_k_a), ("r_k", rw_r_k),
                    ("gn_g", rw_gn_g), ("gn_b", rw_gn_b), ("qn_g", mla_q_norm_g), ("kvn_g", mla_kv_norm_g),
                    ("ln1_g", ln1_g), ("ln1_b", ln1_b)):
        put(name, v)
    z["params"] = par
    z["rows"] = np.stack([np.asarray(v).reshape(-1) for v in (ln_in_g, ln_in_b, ln1_g, ln1_b, ln2_g, ln2_b)])
    z["consts"] = tables()
    z["rope"] = rope()
    lora = np.zeros((10, P, P), f)
    for d in range(2):
        for hp in range(2):
            lora[2 * d + hp, 32 * d:32 * d + 32] = np.asarray(rw_w2)[0, d][:, hp * P:(hp + 1) * P]
            lora[4 + 2 * d + hp, 64 + 32 * d:96 + 32 * d] = np.asarray(rw_a2)[0, d][:, hp * P:(hp + 1) * P]
    for hp in range(2):
        lora[8 + hp, 0:64] = np.asarray(rw_g2)[0][:, hp * P:(hp + 1) * P]
    z["lora"] = lora.transpose(1, 0, 2)
    dc = np.clip(np.arange(64)[None, :] - np.arange(64)[:, None] + 15, 0, NDC - 1)
    z["rpb"] = np.asarray(na_rpb)[0][:, :, dc].reshape(2, 2, NDR, 64, 64).transpose(1, 3, 0, 2, 4).reshape(P, 2, NDR, 64)
    wq = np.asarray(mla_w_q_b)[0].reshape(2, P, 8, 96)
    sw = list(range(96)) + list(range(80, 96)) + list(range(64, 80))
    z["w_q"] = wq[:, :, :, sw].transpose(2, 1, 0, 3)
    z["w_kv"] = np.asarray(mla_w_kv_b)[0].reshape(P, 8, P).transpose(1, 0, 2)
    z["w_out"] = np.asarray(w_out)[0].reshape(8, P, 1024)
    z["w_gate"] = np.asarray(w_ffn_gate)[0].reshape(KT, P, FT, P).transpose(2, 1, 0, 3)
    z["w_up"] = np.asarray(w_ffn_up)[0].reshape(KT, P, FT, P).transpose(2, 1, 0, 3)
    z["w_down"] = np.asarray(w_ffn_down)[0].reshape(FT, P, 1024)
    return {k: np.ascontiguousarray(v) for k, v in z.items()}


def kernel(**inputs):
    import concourse.bacc as bacc
    from concourse.bass_utils import run_bass_kernel_spmd

    nc = bacc.Bacc("TRN2", target_bir_lowering=False, num_devices=1)
    arrays = layout(**inputs)
    aps = {n: nc.dram_tensor(f"in_{n}", v.shape, mybir.dt.from_np(v.dtype), kind="ExternalInput").ap()
           for n, v in arrays.items()}
    y = nc.dram_tensor("out_y", (NT, P, D), F32, kind="ExternalOutput").ap()
    hybrid_encoder(nc, aps, y)
    r = run_bass_kernel_spmd(nc, [{f"in_{n}": v for n, v in arrays.items()}], core_ids=[0])
    return r.results[0]["out_y"].reshape(1, T, D)
```
